# Optimizing a Trainium2 kernel written in Bass

```python
import math
import jax
import jax.numpy as jnp
from jax import lax
import numpy as np

D_MODEL = 1024
BATCH = 1
SEQ = 256
DEPTH = 2

GRID_W = 64
CTX_LEN = 256
N_MIXERS = 2
N_ATTN_LAYERS = (DEPTH + 1) // 2
N_POOL_LAYERS = DEPTH // 2
N_MOD = 6
N_HEADS = 8
HEAD_DIM = 64
V_DIM = 2 * HEAD_DIM
ROPE_THETA = 10000.0
Q_BLOCK = 128
POOL_WINDOWS = (2, 4, 8, 16)
N_POOL_GROUPS = 4
POOL_GROUP_DIM = D_MODEL // N_POOL_GROUPS
N_EXPERTS = 32
N_EXPERT_GROUPS = 4
EXPERTS_PER_GROUP = N_EXPERTS // N_EXPERT_GROUPS
TOP_K = 2
D_EXPERT = D_MODEL // 2
MOE_BLOCK = 256
NORM_EPS = 1e-6

kernel_name = 'hybrid_diffattn_pool_moe_dit'

def rms_norm(x, gain):
    xf = x.astype(jnp.float32)
    y = xf * lax.rsqrt(jnp.mean(xf * xf, axis=-1, keepdims=True) + NORM_EPS)
    return (y * gain.astype(jnp.float32)).astype(x.dtype)

def modulate(h, shift, scale):
    return h * (1 + scale) + shift

def rope_2d_tables(n_tokens, dtype):
    rows = n_tokens // GRID_W
    row = jnp.repeat(jnp.arange(rows, dtype=jnp.float32), GRID_W)
    col = jnp.tile(jnp.arange(GRID_W, dtype=jnp.float32), rows)
    half = HEAD_DIM // 2
    inv_freq = ROPE_THETA ** (-jnp.arange(0, half, 2, dtype=jnp.float32) / half)
    ang_r = row[:, None] * inv_freq
    ang_c = col[:, None] * inv_freq
    ang = jnp.concatenate([ang_r, ang_r, ang_c, ang_c], axis=-1)
    return jnp.cos(ang).astype(dtype), jnp.sin(ang).astype(dtype)

def apply_rope_2d(x, cos, sin):
    x1, x2, x3, x4 = jnp.split(x, 4, axis=-1)
    rot = jnp.concatenate([-x2, x1, -x4, x3], axis=-1)
    return x * cos + rot * sin

def diff_attention(h, hc, w_in, w_out, q_gain, k_gain, lam, lam_init, sub_gain, cos, sin, ctx_out):
    B, L, D = h.shape
    C = hc.shape[1]

    def qk_heads(t, n):
        return t.reshape(B, n, N_HEADS, 2, HEAD_DIM).transpose(0, 2, 3, 1, 4)

    def v_heads(t, n):
        return t.reshape(B, n, N_HEADS, V_DIM).transpose(0, 2, 1, 3)

    q, k, v = jnp.split(h @ w_in, 3, axis=-1)
    q = apply_rope_2d(rms_norm(qk_heads(q, L), q_gain), cos, sin)
    k = apply_rope_2d(rms_norm(qk_heads(k, L), k_gain), cos, sin)
    v = v_heads(v, L)
    kc, vc = jnp.split(hc @ w_in[:, D:], 2, axis=-1)
    kc = rms_norm(qk_heads(kc, C), k_gain)
    vc = v_heads(vc, C)
    k_all = jnp.concatenate([k, kc], axis=3)
    v_all = jnp.concatenate([v, vc], axis=2)
    scale = HEAD_DIM ** -0.5

    def attend(q_blk, keys, vals):
        s = jnp.einsum('bhmqd,bhmkd->bhmqk', q_blk, keys).astype(jnp.float32) * scale
        p = jax.nn.softmax(s, axis=-1)
        w = (p[:, :, 0] - lam * p[:, :, 1]).astype(vals.dtype)
        return jnp.einsum('bhqk,bhkv->bhqv', w, vals)

    def finish(o):
        o = rms_norm(o, sub_gain) * (1 - lam_init)
        return o.reshape(o.shape[0], o.shape[1], N_HEADS * V_DIM) @ w_out

    n_blk = L // Q_BLOCK
    q_blocks = q.reshape(B, N_HEADS, 2, n_blk, Q_BLOCK, HEAD_DIM).transpose(3, 0, 1, 2, 4, 5)
    o = lax.map(lambda qb: attend(qb, k_all, v_all), q_blocks)
    y = finish(o.transpose(1, 0, 3, 2, 4).reshape(B, L, N_HEADS, V_DIM))
    yc = None
    if ctx_out:
        qc = rms_norm(qk_heads(hc @ w_in[:, :D], C), q_gain)
        yc = finish(attend(qc, kc, vc).transpose(0, 2, 1, 3))
    return y, yc

def pool_mixer(h, w_in, w_group, ch_scale, w_out):
    B, L, D = h.shape
    u = h @ w_in
    cs = jnp.concatenate([jnp.zeros((B, 1, D), jnp.float32),
                          jnp.cumsum(u.astype(jnp.float32), axis=1)], axis=1)
    t = jnp.arange(L)
    outs = []
    for g, win in enumerate(POOL_WINDOWS):
        sl = slice(g * POOL_GROUP_DIM, (g + 1) * POOL_GROUP_DIM)
        lo = jnp.maximum(t - win // 2, 0)
        hi = jnp.minimum(t + win // 2, L)
        cs_g = cs[:, :, sl]
        mean = (jnp.take(cs_g, hi, axis=1) - jnp.take(cs_g, lo, axis=1)) / (hi - lo).astype(jnp.float32)[None, :, None]
        d = (mean - u[:, :, sl].astype(jnp.float32)).astype(h.dtype)
        outs.append(d @ w_group[g])
    y = jnp.concatenate(outs, axis=-1) * ch_scale
    return y @ w_out

def route(h_flat, router_w, router_b):
    n = h_flat.shape[0]
    logits = (h_flat @ router_w).astype(jnp.float32) + router_b.astype(jnp.float32)
    probs = jax.nn.softmax(logits, axis=-1).reshape(n, N_EXPERT_GROUPS, EXPERTS_PER_GROUP)
    group_score = lax.top_k(probs, TOP_K)[0].sum(-1)
    g_sel = jnp.argmax(group_score, axis=-1)
    in_group = probs[jnp.arange(n), g_sel]
    vals, idx = lax.top_k(in_group, TOP_K)
    experts = g_sel[:, None] * EXPERTS_PER_GROUP + idx
    gates = vals / jnp.sum(vals, axis=-1, keepdims=True)
    return experts, gates

def moe(h_flat, router_w, router_b, w_gate, w_up, w_down):
    n, d = h_flat.shape
    experts, gates = route(h_flat, router_w, router_b)
    a = n * TOP_K
    flat_e = experts.reshape(-1)
    flat_tok = jnp.repeat(jnp.arange(n, dtype=jnp.int32), TOP_K)
    flat_gate = gates.reshape(-1)
    order = jnp.argsort(flat_e)
    sorted_e = flat_e[order]
    counts = jnp.bincount(flat_e, length=N_EXPERTS)
    padded = (counts + MOE_BLOCK - 1) // MOE_BLOCK * MOE_BLOCK
    start = jnp.cumsum(counts) - counts
    pad_end = jnp.cumsum(padded)
    pad_start = pad_end - padded
    dest = pad_start[sorted_e] + jnp.arange(a) - start[sorted_e]
    n_blocks = -(-a // MOE_BLOCK) + N_EXPERTS
    n_slots = n_blocks * MOE_BLOCK
    slot_tok = jnp.full((n_slots,), n, jnp.int32).at[dest].set(flat_tok[order])
    slot_gate = jnp.zeros((n_slots,), jnp.float32).at[dest].set(flat_gate[order])
    block_start = jnp.arange(n_blocks) * MOE_BLOCK
    block_e = jnp.minimum(jnp.sum(pad_end[None, :] <= block_start[:, None], axis=1), N_EXPERTS - 1)
    h_pad = jnp.concatenate([h_flat, jnp.zeros((1, d), h_flat.dtype)], axis=0)
    xs = h_pad[slot_tok].reshape(n_blocks, MOE_BLOCK, d)

    def expert_block(args):
        xb, e = args
        return (jax.nn.silu(xb @ w_gate[e]) * (xb @ w_up[e])) @ w_down[e]

    ys = lax.map(expert_block, (xs, block_e)).reshape(n_slots, d)
    ys = ys * slot_gate[:, None].astype(ys.dtype)
    return jax.ops.segment_sum(ys, slot_tok, num_segments=n + 1)[:n]

def setup_inputs(seed: int = 0) -> dict:
    key = jax.random.key(seed)
    ks = jax.random.split(key, 26)
    f32 = jnp.float32
    D = D_MODEL
    G = POOL_GROUP_DIM

    def nrm(k, shape, scale):
        return jax.random.normal(k, shape, f32) * scale

    return {
        'x': nrm(ks[0], (BATCH, SEQ, D), 1.0),
        'c': nrm(ks[1], (BATCH, D), 1.0),
        'ctx': nrm(ks[2], (BATCH, CTX_LEN, D), 1.0),
        'c_ctx': nrm(ks[3], (D,), 1.0),
        'ada_w': nrm(ks[4], (DEPTH, D, N_MOD * D), 0.5 * D ** -0.5),
        'ada_b': nrm(ks[5], (DEPTH, N_MOD * D), 0.01),
        'norm1_g': 1.0 + nrm(ks[6], (DEPTH, D), 0.05),
        'norm2_g': 1.0 + nrm(ks[7], (DEPTH, D), 0.05),
        'attn_w_in': nrm(ks[8], (N_ATTN_LAYERS, D, 3 * D), D ** -0.5),
        'attn_w_out': nrm(ks[9], (N_ATTN_LAYERS, N_HEADS * V_DIM, D), (N_HEADS * V_DIM) ** -0.5),
        'attn_q_gain': 1.0 + nrm(ks[10], (N_ATTN_LAYERS, HEAD_DIM), 0.05),
        'attn_k_gain': 1.0 + nrm(ks[11], (N_ATTN_LAYERS, HEAD_DIM), 0.05),
        'attn_lq1': nrm(ks[12], (N_ATTN_LAYERS, HEAD_DIM), 0.1),
        'attn_lk1': nrm(ks[13], (N_ATTN_LAYERS, HEAD_DIM), 0.1),
        'attn_lq2': nrm(ks[14], (N_ATTN_LAYERS, HEAD_DIM), 0.1),
        'attn_lk2': nrm(ks[15], (N_ATTN_LAYERS, HEAD_DIM), 0.1),
        'attn_sub_gain': 1.0 + nrm(ks[16], (N_ATTN_LAYERS, V_DIM), 0.05),
        'pool_w_in': nrm(ks[17], (N_POOL_LAYERS, D, D), D ** -0.5),
        'pool_w_group': nrm(ks[18], (N_POOL_LAYERS, N_POOL_GROUPS, G, G), G ** -0.5),
        'pool_scale': 1.0 + nrm(ks[19], (N_POOL_LAYERS, D), 0.1),
        'pool_w_out': nrm(ks[20], (N_POOL_LAYERS, D, D), D ** -0.5),
        'router_w': nrm(ks[21], (D, N_EXPERTS), D ** -0.5),
        'router_b': nrm(ks[22], (N_EXPERTS,), 0.01),
        'moe_w_gate': nrm(ks[23], (DEPTH, N_EXPERTS, D, D_EXPERT), D ** -0.5),
        'moe_w_up': nrm(ks[24], (DEPTH, N_EXPERTS, D, D_EXPERT), D ** -0.5),
        'moe_w_down': nrm(ks[25], (DEPTH, N_EXPERTS, D_EXPERT, D), D_EXPERT ** -0.5),
    }

def reference(x, c, ctx, c_ctx, ada_w, ada_b, norm1_g, norm2_g,
              attn_w_in, attn_w_out, attn_q_gain, attn_k_gain,
              attn_lq1, attn_lk1, attn_lq2, attn_lk2, attn_sub_gain,
              pool_w_in, pool_w_group, pool_scale, pool_w_out,
              router_w, router_b, moe_w_gate, moe_w_up, moe_w_down):
    B, L, D = x.shape
    cos, sin = rope_2d_tables(L, x.dtype)
    c_act = jax.nn.silu(c)
    cc_act = jax.nn.silu(c_ctx)
    for i in range(DEPTH):
        kind = i % N_MIXERS
        j = i // N_MIXERS
        update_ctx = any(l % N_MIXERS == 0 for l in range(i + 1, DEPTH))
        need_ctx_in = (kind == 0) or update_ctx
        mod = (c_act @ ada_w[i] + ada_b[i])[:, None, :]
        sh1, s1, g1, sh2, s2, g2 = jnp.split(mod, N_MOD, axis=-1)
        h = modulate(rms_norm(x, norm1_g[i]), sh1, s1)
        if need_ctx_in:
            mod_c = cc_act @ ada_w[i] + ada_b[i]
            csh1, cs1, cg1, csh2, cs2, cg2 = jnp.split(mod_c, N_MOD, axis=-1)
            hc = modulate(rms_norm(ctx, norm1_g[i]), csh1, cs1)
        if kind == 0:
            lam_init = 0.8 - 0.6 * math.exp(-0.3 * i)
            f32 = jnp.float32
            lam = (jnp.exp(jnp.sum(attn_lq1[j].astype(f32) * attn_lk1[j].astype(f32)))
                   - jnp.exp(jnp.sum(attn_lq2[j].astype(f32) * attn_lk2[j].astype(f32))) + lam_init)
            y, yc = diff_attention(h, hc, attn_w_in[j], attn_w_out[j], attn_q_gain[j], attn_k_gain[j],
                                   lam, lam_init, attn_sub_gain[j], cos, sin, update_ctx)
        else:
            y = pool_mixer(h, pool_w_in[j], pool_w_group[j], pool_scale[j], pool_w_out[j])
            yc = pool_mixer(hc, pool_w_in[j], pool_w_group[j], pool_scale[j], pool_w_out[j]) if update_ctx else None
        x = x + g1 * y
        h2 = modulate(rms_norm(x, norm2_g[i]), sh2, s2)
        if update_ctx:
            ctx = ctx + cg1 * yc
            h2c = modulate(rms_norm(ctx, norm2_g[i]), csh2, cs2)
            tokens = jnp.concatenate([h2.reshape(-1, D), h2c.reshape(-1, D)], axis=0)
            out = moe(tokens, router_w, router_b, moe_w_gate[i], moe_w_up[i], moe_w_down[i])
            x = x + g2 * out[:B * L].reshape(B, L, D)
            ctx = ctx + cg2 * out[B * L:].reshape(ctx.shape)
        else:
            out = moe(h2.reshape(-1, D), router_w, router_b, moe_w_gate[i], moe_w_up[i], moe_w_down[i])
            x = x + g2 * out.reshape(B, L, D)
    return x


_drawn_inputs = setup_inputs


def setup_inputs(seed=0):
    import zlib

    import numpy as np

    out = dict(_drawn_inputs(seed))
    spreads = {}
    factors = {'attn_q_gain': 5.665, 'attn_lq2': 8.0, 'router_b': 3.139}
    for name, (base, spread) in spreads.items():
        noise = np.random.default_rng([zlib.crc32(name.encode()), seed]).standard_normal(out[name].shape)
        drawn = base * np.exp(spread * noise) if base else spread * noise
        out[name] = jnp.asarray(drawn.astype(out[name].dtype))
    for name, factor in factors.items():
        out[name] = (out[name] * factor).astype(out[name].dtype)
    return out
```

```python
import math
from contextlib import ExitStack

import numpy as np

import concourse.bass as bass
from concourse import mybir

F32 = mybir.dt.float32
BF16 = mybir.dt.bfloat16
I32 = mybir.dt.int32
ALU = mybir.AluOpType
ACT = mybir.ActivationFunctionType
AX = mybir.AxisListType.X

P = 128
D = 1024
KC = D // P
SEQ = 256
NT = SEQ // P
HEADS, HD = 8, 64
EPS = 1e-6
LAM_INIT = 0.8 - 0.6 * math.exp(-0.3 * 0)
SCALE = HD ** -0.5
NE, NG, PER_G = 32, 4, 8
FF = 512
SLOTS = 64
OVER = (2 * SEQ) // (SLOTS + 1)
GRP = 3
BODY = 2 * GRP
TURNS = NE // BODY
GW = GRP * SLOTS
WINDOWS = (2, 4, 8, 16)
PAD = max(WINDOWS) // 2
UP = SEQ + 2 * PAD

C_ID, C_TRI, C_ONES, C_SEL = 0, 128, 256, 384
C_IOTA = 512
C_STACK = C_IOTA + GW
C_W4 = C_STACK + 32
C_W32 = C_W4 + 4
C_BASE = C_W32 + 32
C_DELTA = C_BASE + 32
C_TILE = C_DELTA + 32
N_CONST = C_TILE + 8
V_C, V_N1, V_N2, V_PS, V_SUB, V_ADA = 0, 16, 32, 48, 56, 57
N_VEC = V_ADA + 64
R_QG, R_KG, R_LQ, R_RB = 0, 64, 128, 384
N_ROW = 416
COL_PARTS = (0, 1, 3, 4)


def constants():
    c = np.zeros((P, N_CONST), np.float32)
    r = np.arange(P)
    c[:, C_ID:C_ID + P] = np.eye(P)
    c[:, C_TRI:C_TRI + P] = r[:, None] < r[None, :]
    c[:, C_ONES:C_ONES + P] = 1
    c[::32, C_SEL:C_SEL + P] = 1
    c[:, C_IOTA:C_IOTA + GW] = np.arange(GW)
    c[:, C_STACK:C_STACK + 32] = r[:, None] % 32 == np.arange(32)
    c[:, C_W4:C_W4 + 4] = NG - np.arange(4)
    c[:, C_W32:C_W32 + 32] = NE - np.arange(32)
    c[:, C_BASE:C_BASE + 32] = SLOTS * np.arange(32)
    c[:, C_DELTA:C_DELTA + 32] = NE * SLOTS - SLOTS - SLOTS * np.arange(32)
    c[:, C_TILE:C_TILE + 8] = np.arange(8)
    half = HD // 2
    inv = (10000.0 ** (-np.arange(0, half, 2, dtype=np.float32) / half)).astype(np.float32)
    t = np.arange(SEQ)
    ar = (t // 64).astype(np.float32)[:, None] * inv
    ac = (t % 64).astype(np.float32)[:, None] * inv
    cos = np.cos(np.concatenate([ar, ar, ac, ac], 1))
    sin = np.sin(np.concatenate([-ar, ar, -ac, ac], 1))
    rope = np.stack([cos, sin]).astype(np.float32).reshape(2, NT, P, HD).transpose(2, 0, 1, 3)
    n = np.stack([np.minimum(t + w // 2, SEQ) - np.maximum(t - w // 2, 0) for w in WINDOWS])
    inv_n = (np.float32(1) / n.astype(np.float32)).astype(np.float32)
    return c, np.ascontiguousarray(rope).reshape(P, -1), inv_n.reshape(1, -1)


def program(nc, x_d, ctx_d, ada_w, ada_b, w_in, w_out, pool_in, pool_grp, pool_out, router_w,
            w_gate, w_up, w_down, vec_d, row_d, const_d, rope_d, inv_n_d, out_d):
    stack = ExitStack()
    with stack:
        def sb(name, n, dt=F32):
            return stack.enter_context(nc.sbuf_tensor(name, [P, n], dt))

        def sem(name):
            return stack.enter_context(nc.semaphore(name))

        ring = sb("ring", 36864)
        X = sb("X", 2048)
        HT = sb("HT", 4096)
        KT = sb("KT", 4096)
        QT = sb("QT", 2048)
        TMP = sb("TMP", 2048)
        const = sb("const", N_CONST)
        vec = sb("vec", N_VEC)
        rope_g = sb("rope_g", 4 * 2 * HD)
        ccols = sb("ccols", KC * 32)
        cols = sb("cols", 80)
        stat = sb("stat", 80)
        rbias = sb("rbias", 32)
        ov_info = sb("ov_info", 8, I32)
        PS = stack.enter_context(nc.psum_tensor("PS", [P, 8, 512], F32))

        def bank(i, n=1):
            return PS[:, i, :] if n == 1 else PS[:, i:i + n, :].rearrange("p b n -> p (b n)")

        ident = const[:, C_ID:C_ID + P]
        tri = const[:, C_TRI:C_TRI + P]
        ones = const[:, C_ONES:C_ONES + P]
        sel = const[:, C_SEL:C_SEL + P]
        x_sb = X[:, :].rearrange("p (t d) -> p t d", t=NT)

        def unit(i):
            return ring[:, 8192 * i:8192 * (i + 1)].rearrange("p (k n) -> p k n", k=8)

        vals = ring[:, 24576:28672].rearrange("p (t n) -> p t n", t=4)
        work = 28672
        modraw = ring[:, work:work + 1024]
        raw = ring[:, work + 1024:work + 2048]
        sq = ring[:, work + 2048:work + 3072]
        ra = ring[:, work + 3072:work + 4096]
        rb = ring[:, work + 4096:work + 5120]
        qn = ring[:, work + 5120:work + 6144]
        xn0 = ring[:, work + 5120:work + 7168].rearrange("p (t d) -> p t d", t=NT)
        rope_raw = ring[:, work + 7168:work + 7424].rearrange("p (a t d) -> p a t d", a=2, t=NT)
        rows = ring[:, work + 7424:work + 7424 + N_ROW]
        lam_t = ring[:, work + 7840:work + 7968]
        probs = ring[:, work + 1024:work + 3072].rearrange("p (b m n) -> p b m n", b=2, m=2)
        wmix = ring[:, work + 3072:work + 4096].rearrange("p (b n) -> p b n", b=2)
        wT = ring[:, work + 4096:work + 5120].rearrange("p (b c n) -> p b c n", b=2, c=4)
        o_sb = ring[:, work + 5120:work + 5376].rearrange("p (b n) -> p b n", b=2)
        o_n = ring[:, work + 5376:work + 5632].rearrange("p (b n) -> p b n", b=2)
        o_junk = ring[:, work + 5632:work + 5760]

        ctx_sb = TMP[:, :].rearrange("p (t d) -> p t d", t=NT)
        hT = HT[:, :].rearrange("p (k t) -> p k t", k=KC)
        oT = HT[:, 0:2048].rearrange("p (h t) -> p h t", h=HEADS)
        h2T = HT[:, 0:2048].rearrange("p (k t) -> p k t", k=KC)
        gate_row = [TMP[:, 0:1024], TMP[:, 1024:2048], HT[:, 2048:3072], HT[:, 3072:4096]]
        kT = KT[:, :].rearrange("p (h t) -> p h t", h=HEADS)
        qT = QT[:, :].rearrange("p (h t) -> p h t", h=HEADS)
        xn = KT[:, 0:2048].rearrange("p (t d) -> p t d", t=NT)


        slot = [ring[:, 12288 * i:12288 * (i + 1)] for i in range(3)]
        gu_w = [s[:, 0:8192].rearrange("p (k a f) -> p k a f", k=KC, a=2) for s in slot]
        dn_w = [s[:, 8192:12288].rearrange("p (c n) -> p c n", c=4) for s in slot]
        xsT = [KT[:, 2048:2048 + KC * GW].rearrange("p (k n) -> p k n", k=KC),
               QT[:, 0:KC * GW].rearrange("p (k n) -> p k n", k=KC)]
        silu_sb = KT[:, 3584:3840]
        h_sb = KT[:, 3840:4096]
        res_t = KT[:, 3584:4096]
        rw = QT[:, 1536:1792].rearrange("p (k e) -> p k e", k=KC)
        part_lg = QT[:, 1792:2048]
        sg = [HT[:, 768 * i:768 * (i + 1)].rearrange("p (t j a n) -> p t j a n", t=NT, j=GRP, a=2) for i in range(2)]
        s01 = HT[:, 1536:1920].rearrange("p (t n) -> p t n", t=NT)
        part = [rope_g[:, 0:384].rearrange("p (t n) -> p t n", t=NT), s01]
        t_sb = TMP[:, 0:512]
        y_sb = TMP[:, 512:1024]
        route = sb("route", 16)
        pos, gate, pcur = (route[:, 4 * i:4 * i + 4] for i in range(3))
        nt_tmp = sb("nt_tmp", 32)
        mhalf = sb("mhalf", 16)

        def rt(i, n=64):
            return TMP[:, 64 * i:64 * i + n]

        def t2(ap):
            return ap.rearrange("p (t e) -> p t e", t=NT)

        pool_w = slot[2][:, 0:8192].rearrange("p (k n) -> p k n", k=KC)
        grp_w = slot[2][:, 8192:10240].rearrange("p (g i n) -> p g i n", g=4, i=2)
        pout_w = slot[0][:, 0:8192].rearrange("p (k n) -> p k n", k=KC)
        dT = KT[:, 2048:4096].rearrange("p (b t) -> p b t", b=8)
        y1T = KT[:, 0:2048].rearrange("p (b t) -> p b t", b=8)
        up = QT[:, 0:2 * UP].rearrange("p (i t) -> p i t", i=2)
        pool_sum = [TMP[:, 1024:1024 + 2 * UP].rearrange("p (i t) -> p i t", i=2),
                    QT[:, 2 * UP:4 * UP].rearrange("p (i t) -> p i t", i=2)]
        inv_n = TMP[:, 0:1024].rearrange("p (g t) -> p g t", g=4)

        ss0, ms0 = stat[:, 0:4], stat[:, 4:8]
        ssn, msn = stat[:, 12:14], stat[:, 14:16]
        ssk, msk = stat[:, 18:34], stat[:, 34:50]
        neglam = stat[:, 76:77]
        lam_s = stat[:, 77:79]

        def ust(b, i, n=1):
            return stat[:, 50 + 10 * b + i:50 + 10 * b + i + n]

        def oss(b):
            return stat[:, 70 + b:71 + b]

        def oms(b):
            return stat[:, 72 + b:73 + b]

        def col(l, what):
            c = 32 * l + 8 * what
            return cols[:, c:c + 8]

        def bias_col(i):
            l, p = divmod(i, 6)
            c = V_ADA + 8 * (4 * l + COL_PARTS.index(p))
            return vec[:, c:c + 8]

        const_in, rows_in, vec_in, x_in, ctx_in = (sem(n) for n in ("const_in", "rows_in", "vec_in", "x_in", "ctx_in"))
        rw_in, bias0_in, bias1_in = sem("rw_in"), sem("bias0_in"), sem("bias1_in")
        ada_in = [sem(f"ada_in{i}") for i in range(12)]
        w_in_s = {n: sem(f"w{n}_in") for n in "kvqo"}
        chain = sem("chain")
        zeroed, minus_half, silu_c, lam_sum, lam_exp, lam_done = (sem(n) for n in ("zeroed", "minus_half", "silu_c", "lam_sum", "lam_exp", "lam_done"))
        ss_ready, ms_ready, pow_done, xn0_ready = (sem(n) for n in ("ss_ready", "ms_ready", "pow_done", "xn0_ready"))
        mod_mm, mod_raw, mod_fin, mod_used = (sem(n) for n in ("mod_mm", "mod_raw", "mod_fin", "mod_used"))
        xt_x, xt_c, h_x, h_c = (sem(n) for n in ("xt_x", "xt_c", "h_x", "h_c"))
        proj_done, proj_used, sq_ready, qn_ready, kq_tr, kq_in = (sem(n) for n in ("proj_done", "proj_used", "sq_ready", "qn_ready", "kq_tr", "kq_in"))
        scored, max_ready, exp_done, w_ready, w_tr, wT_ready, pv_done, o_ready, on_ready, o_tr, oT_ready = (
            sem(n) for n in ("scored", "max_ready", "exp_done", "w_ready", "w_tr", "wT_ready", "pv_done", "o_ready", "on_ready", "o_tr", "oT_ready"))
        op_done, x_upd, ssn_ready, xn_ready, nt_tr, h2_v, h2_a = (sem(n) for n in ("op_done", "x_upd", "ssn_ready", "xn_ready", "nt_tr", "h2_v", "h2_a"))
        rt_part, rt_sb, rt_logit, lg_ready, lg_exp, rt_sel, rt_cnt, routed = (sem(n) for n in ("rt_part", "rt_sb", "rt_logit", "lg_ready", "lg_exp", "rt_sel", "rt_cnt", "routed"))
        pin_in, pout_in, invn_in, u_done, up_ready, d_ready, y1_done, y1_ready, po_done = (
            sem(n) for n in ("pin_in", "pout_in", "invn_in", "u_done", "up_ready", "d_ready", "y1_done", "y1_ready", "po_done"))
        out_stored, borders = sem("out_stored"), sem("borders")

        class Layer:
            def __init__(self, l):
                self.l = l
                self.gu_in = [sem(f"gu_in{l}_{i}") for i in range(3)]
                self.dn_in = [sem(f"dn_in{l}_{i}") for i in range(3)]
                (self.shifted, self.parts, self.sg_done, self.s_ready, self.xg_done, self.xs_done, self.gu_done,
                 self.silu_done, self.h_ready, self.tr_done, self.t_ready, self.dn_done, self.y_ready, self.acc_done) = (
                    sem(f"{n}{l}") for n in ("shifted", "parts", "sg_done", "s_ready", "xg_done", "xs_done", "gu_done",
                                             "silu_done", "h_ready", "tr_done", "t_ready", "dn_done", "y_ready", "acc_done"))
                (self.ov_in, self.ov_shift, self.ov_parts, self.ov_sg, self.ov_s, self.ov_xg, self.ov_xs, self.ov_gu,
                 self.ov_silu, self.ov_h, self.ov_tr, self.ov_t, self.ov_y) = (
                    sem(f"ov_{n}{l}") for n in ("in", "shift", "parts", "sg", "s", "xg", "xs", "gu", "silu", "h", "tr", "t", "y"))

            def slot(self, e):
                return (e + self.l) % 3

        layers = [Layer(0), Layer(1)]
        ov_slot = [L.slot(NE - 1) for L in layers]
        block = stack.enter_context(nc.Block())

        @block.sync
        def _(sp):
            def rows_of(w, c0, n):
                return w.rearrange("(k p) n -> p k n", p=P)[:, :, c0:c0 + n]

            def load_expert(L, e, s):
                sp.dma_start(gu_w[s][:, :, 0, :], w_gate[L.l, e].rearrange("(k p) f -> p k f", p=P)).then_inc(L.gu_in[s], 16)
                sp.dma_start(gu_w[s][:, :, 1, :], w_up[L.l, e].rearrange("(k p) f -> p k f", p=P)).then_inc(L.gu_in[s], 16)
                sp.dma_start(dn_w[s], w_down[L.l, e].rearrange("(c p) n -> p c n", p=P)).then_inc(L.dn_in[s], 16)

            def load_freed(L, e, s):
                sp.wait_ge(L.gu_done, e - 2)
                sp.wait_ge(L.dn_done, e - 2)
                load_expert(L, e, s)

            sp.dma_start(vec[:, :], vec_d).then_inc(vec_in, 16)
            sp.dma_start(ctx_sb, ctx_d[0].rearrange("(t p) d -> p t d", p=P)).then_inc(ctx_in, 16)
            sp.dma_start(x_sb, x_d[0].rearrange("(t p) d -> p t d", p=P)).then_inc(x_in, 16)

            def load_ada(i):
                sp.dma_start(unit(i % 2), rows_of(ada_w[i // 6], D * (i % 6), D)).then_inc(ada_in[i], 16)

            load_ada(0)
            load_ada(1)
            sp.dma_start(unit(2), rows_of(w_in[0], D, D)).then_inc(w_in_s["k"], 16)
            for i in range(2, 6):
                sp.wait_ge(mod_mm, i - 1)
                load_ada(i)
            sp.wait_ge(mod_mm, 5)
            sp.dma_start(unit(0), rows_of(w_in[0], 2 * D, D)).then_inc(w_in_s["v"], 16)
            sp.wait_ge(mod_mm, 6)
            sp.dma_start(unit(1), rows_of(w_in[0], 0, D)).then_inc(w_in_s["q"], 16)
            sp.wait_ge(proj_done, 4)
            sp.dma_start(unit(2), rows_of(w_out[0], 0, D)).then_inc(w_in_s["o"], 16)
            for i in range(6, 12):
                if i == 6:
                    sp.wait_ge(proj_done, 8)
                elif i == 7:
                    sp.wait_ge(proj_done, 10)
                else:
                    sp.wait_ge(mod_mm, i - 1)
                load_ada(i)
            L = layers[0]
            sp.wait_ge(mod_mm, 12)
            load_expert(L, 0, 0)
            sp.wait_ge(oT_ready, 16)
            sp.wait_ge(mod_used, 12)
            load_expert(L, 2, 2)
            sp.wait_ge(op_done, 4)
            load_expert(L, 1, 1)
            for L in layers:
                with sp.Fori(0, (NE - 5) // 3) as it:
                    for c in range(3):
                        load_freed(L, 3 * it + (3 + c), L.slot(c))
                for e in range(3 + 3 * ((NE - 5) // 3), NE):
                    load_freed(L, e, L.slot(e))
                if L.l == 0:
                    sp.wait_ge(L.gu_done, 30)
                    sp.wait_ge(L.dn_done, 30)
                    sp.dma_start(pool_w, rows_of(pool_in[0], 0, D)).then_inc(pin_in, 16)
                    sp.dma_start(grp_w, pool_grp[0].rearrange("g (i p) n -> p g i n", p=P)).then_inc(pin_in, 16)
                    sp.wait_ge(L.gu_done, 31)
                    sp.wait_ge(L.dn_done, 31)
                    sp.dma_start(pout_w, rows_of(pool_out[0], 0, D)).then_inc(pout_in, 16)
                sp.wait_ge(L.gu_done, NE)
                sp.wait_ge(L.dn_done, NE)
                sp.wait_ge(routed, L.l + 1)
                n_ov = sp.value_load(ov_info[0:1, OVER:OVER + 1], min_val=0, max_val=OVER)
                with sp.Fori(0, OVER) as i:
                    with sp.If(i < n_ov):
                        sp.wait_ge(L.dn_done, NE + i)
                        e = sp.value_load(ov_info[0:1, bass.ds(i, 1)], min_val=0, max_val=NE - 1)
                        s = ov_slot[L.l]
                        sp.dma_start(gu_w[s][:, :, 0, :], w_gate[L.l, bass.ds(e, 1)].rearrange("o (k p) f -> p (o k) f", p=P)).then_inc(L.ov_in, 16)
                        sp.dma_start(gu_w[s][:, :, 1, :], w_up[L.l, bass.ds(e, 1)].rearrange("o (k p) f -> p (o k) f", p=P)).then_inc(L.ov_in, 16)
                        sp.dma_start(dn_w[s], w_down[L.l, bass.ds(e, 1)].rearrange("o (c p) n -> p (o c) n", p=P)).then_inc(L.ov_in, 16)
                if L.l == 0:
                    L1 = layers[1]
                    sp.wait_ge(L.acc_done, 1)
                    load_expert(L1, 0, L1.slot(0))
                    sp.dma_start(TMP[:, 0:1024], inv_n_d[0].partition_broadcast(P)).then_inc(invn_in, 16)
                    sp.wait_ge(y1_done, 8)
                    load_expert(L1, 1, L1.slot(1))
                    sp.wait_ge(po_done, 4)
                    load_expert(L1, 2, L1.slot(2))

        @block.gpsimd
        def _(pool):
            nc.gpsimd.memset(mhalf[:, :], -0.5).then_inc(minus_half, 1)
            pool.wait_ge(minus_half, 1)

            def inverse_root(n, ap):
                pool.wait_ge(ms_ready, n + 1)
                nc.gpsimd.tensor_tensor(ap, ap, mhalf[:, 0:ap.shape[1]], ALU.pow).then_inc(pow_done, 1)

            inverse_root(0, ms0[:, 0:2])
            inverse_root(1, ms0[:, 2:4])
            for n in range(6):
                inverse_root(2 + n, msk)
            for u in range(16):
                inverse_root(8 + u, oms(u % 2))
            for n in range(6):
                inverse_root(24 + n, msn[:, n % 2:n % 2 + 1])

        @block.tensor
        def _(pe):
            mm, tr = nc.tensor.matmul, nc.tensor.transpose

            def ada_mm(i):
                pe.wait_ge(ada_in[i], 16)
                if i == 0:
                    pe.wait_ge(silu_c, 1)
                else:
                    pe.wait_ge(mod_used, i)
                for c in range(2):
                    for half in range(2):
                        for j in range(4):
                            k = 2 * j + c
                            ins = mm(PS[32 * j:32 * j + 32, half, :], ccols[:, 32 * k:32 * k + 32],
                                     unit(i % 2)[:, k, 512 * half:512 * half + 512], start=c == 0, stop=c == 1)
                ins.then_inc(mod_mm, 1)

            def ada_fin(i):
                pe.wait_ge(mod_raw, i + 1)
                if i % 6 in COL_PARTS:
                    for k in range(KC):
                        ins = tr(PS[:, k // 4, 128 * (k % 4):128 * (k % 4) + 128], modraw[:, P * k:P * k + P], ident)
                else:
                    for half in range(2):
                        ins = mm(bank(half), sel, modraw[:, 512 * half:512 * half + 512], start=True, stop=True)
                ins.then_inc(mod_fin, 1)

            pe.wait_ge(const_in, 16)
            for i in range(2):
                ada_mm(i)
                ada_fin(i)
            pe.wait_ge(xn0_ready, 2)
            for k in range(KC):
                if k >= 2:
                    pe.wait_ge(h_x, k - 1)
                    pe.wait_ge(h_c, k - 1)
                for t in range(NT):
                    ins = tr(PS[:, 4 + k % 2, P * t:P * t + P], xn0[:, t, P * k:P * k + P], ident)
                ins.then_inc(xt_x, 1)
                for t in range(NT):
                    ins = tr(PS[:, 6 + k % 2, P * t:P * t + P], ctx_sb[:, t, P * k:P * k + P], ident)
                ins.then_inc(xt_c, 1)
            pe.wait_ge(h_x, KC)
            pe.wait_ge(h_c, KC)

            def proj(n):
                which, t, u = ("k", n, 2) if n < 4 else ("v", n - 4, 0) if n < 8 else ("q", n - 8, 1)
                pe.wait_ge(w_in_s[which], 16)
                if n >= 2:
                    pe.wait_ge(proj_used, n - 1)
                for half in range(2):
                    for k in range(KC):
                        ins = mm(bank(4 + 2 * (n % 2) + half), hT[:, k, P * t:P * t + P],
                                 unit(u)[:, k, 512 * half:512 * half + 512], start=k == 0, stop=k == KC - 1)
                ins.then_inc(proj_done, 1)

            def kq_transpose(m):
                pe.wait_ge(qn_ready, m + 1)
                if m >= 1:
                    pe.wait_ge(kq_in, m)
                for h in range(HEADS):
                    ins = tr(PS[:, 2 + h // 4, P * (h % 4):P * (h % 4) + P], qn[:, P * h:P * h + P], ident)
                ins.then_inc(kq_tr, 1)

            for n in range(10):
                proj(n)
                if 1 <= n <= 4:
                    ada_fin(n + 1)
                    kq_transpose(n - 1)
                if n <= 3:
                    ada_mm(n + 2)
                if n == 9:
                    kq_transpose(4)
            kq_transpose(5)
            pe.wait_ge(kq_in, 6)

            for u in range(18):
                qt, h = divmod(u, HEADS)
                if u < 16:
                    if u >= 2:
                        pe.wait_ge(exp_done, u - 1)
                    for m in range(2):
                        r = slice(64 * m, 64 * m + 64)
                        ins = mm(bank(4 + 2 * (u % 2) + m), qT[r, h, P * qt:P * qt + P], kT[r, h, :], start=True, stop=True)
                    ins.then_inc(scored, 1)
                if 1 <= u <= 16:
                    v = u - 1
                    pe.wait_ge(w_ready, v + 1)
                    if v >= 1:
                        pe.wait_ge(wT_ready, v)
                    for c in range(4):
                        ins = tr(PS[:, 2, P * c:P * c + P], wmix[:, v % 2, P * c:P * c + P], ident)
                    ins.then_inc(w_tr, 1)
                if u < 12:
                    if u % 2 == 0:
                        ada_mm(6 + u // 2)
                    else:
                        ada_fin(6 + u // 2)
                if u >= 2:
                    v = u - 2
                    pe.wait_ge(on_ready, v + 1)
                    tr(PS[:, 3, 128:256], o_n[:, v % 2, :], ident).then_inc(o_tr, 1)
                if 1 <= u <= 16:
                    v = u - 1
                    pe.wait_ge(wT_ready, v + 1)
                    if v >= 1:
                        pe.wait_ge(oT_ready, v)
                    for c in range(4):
                        ins = mm(PS[:, 3, 0:128], wT[:, v % 2, c, :], vals[:, c, P * (v % 8):P * (v % 8) + P],
                                 start=c == 0, stop=c == 3)
                    ins.then_inc(pv_done, 1)

            pe.wait_ge(oT_ready, 16)
            pe.wait_ge(w_in_s["o"], 16)
            for q in range(4):
                for h in range(HEADS):
                    ins = mm(bank(4 + q), oT[:, h, P * (q // 2):P * (q // 2) + P],
                             unit(2)[:, h, 512 * (q % 2):512 * (q % 2) + 512], start=h == 0, stop=h == HEADS - 1)
                ins.then_inc(op_done, 1)

            def norm_transpose(n):
                pe.wait_ge(xn_ready, 2 * n + 2)
                for k in range(KC):
                    if k >= 4:
                        pe.wait_ge((h2_v, h2_a)[k % 2], 4 * n + (k - 4) // 2 + 1)
                    for t in range(NT):
                        ins = tr(PS[:, 4 + k % 4, P * t:P * t + P], xn[:, t, P * k:P * k + P], ident)
                    ins.then_inc(nt_tr, 1)
                pe.wait_ge(h2_v, 4 * n + 4)
                pe.wait_ge(h2_a, 4 * n + 4)

            def route_products(L):
                pe.wait_ge(rw_in, 16)
                for c in range(2):
                    for j in range(4):
                        ins = mm(PS[32 * j:32 * j + 32, 0, 0:256], rw[:, 2 * j + c, :], h2T[:, 2 * j + c, :],
                                 start=c == 0, stop=c == 1)
                ins.then_inc(rt_part, 1)
                pe.wait_ge(rt_sb, L.l + 1)
                for t in range(NT):
                    ins = mm(PS[:, 1, 32 * t:32 * t + 32], part_lg[:, P * t:P * t + P],
                             const[:, C_STACK:C_STACK + 32], start=True, stop=True)
                ins.then_inc(rt_logit, 1)
                pe.wait_ge(rt_sel, L.l + 1)
                chosen = t2(rt(8))
                mm(PS[:, 2, 0:32], tri, chosen[:, 0, :], start=True, stop=True)
                mm(PS[:, 2, 32:64], ones, chosen[:, 0, :], start=True, stop=False)
                mm(PS[:, 2, 32:64], tri, chosen[:, 1, :], start=False, stop=True)
                mm(PS[:, 2, 64:96], ones, chosen[:, 0, :], start=True, stop=False)
                mm(PS[:, 2, 64:96], ones, chosen[:, 1, :], start=False, stop=True).then_inc(rt_cnt, 1)

            def accumulate_zero(start):
                z = ccols[:, :].bitcast(BF16)
                for b in range(4):
                    ins = mm(bank(b), z[:, 0:128], z[:, :], start=start, stop=not start, skip_group_check=True)
                return ins

            def gather(k0, n, dst):
                for c in range(2):
                    for t in range(NT):
                        ins = mm(PS[:, dst, GW * c:GW * c + n], xn[:, t, P * (k0 + c):P * (k0 + c) + P], s01[:, t, 0:n],
                                 start=t == 0, stop=t == NT - 1)
                return ins

            def gate_up(s, xs, j, ks):
                for k in ks:
                    for f in range(2):
                        ins = mm(PS[64 * f:64 * f + 64, 4, :], xs[:, k, SLOTS * j:SLOTS * j + SLOTS],
                                 gu_w[s][:, k, :, 256 * f:256 * f + 256], start=k == 0, stop=k == KC - 1)
                return ins

            def transposes(g, j):
                for t in range(NT):
                    tr(PS[:, 5, P * t:P * t + P], g[:, t, j].rearrange("p a n -> p (a n)"), ident)
                for c in range(2):
                    ins = tr(PS[:, 5, 256 + P * c:256 + P * c + P], h_sb[:, P * c:P * c + P], ident)
                return ins

            def down(s):
                for c in range(4):
                    a, b = divmod(c, 2)
                    lhs = t_sb[:, 256 + P * b + 64 * a:256 + P * b + 64 * a + 64]
                    for f in range(2):
                        ins = mm(PS[64 * f:64 * f + 64, 6, :], lhs, dn_w[s][:, c, 512 * f:512 * f + 512],
                                 start=c == 0, stop=c == 3)
                return ins

            def combine():
                for t in range(NT):
                    for f in range(2):
                        r = slice(64 * f, 64 * f + 64)
                        ins = mm(bank(2 * t + f), t_sb[r, P * t:P * t + P], y_sb[r, :], start=False, stop=False,
                                 skip_group_check=True)
                return ins

            def experts(L):
                pe.wait_ge(L.s_ready, 1)
                for r in range(4):
                    if r >= 2:
                        pe.wait_ge(L.xs_done, r - 1)
                    gather(2 * r, GW, 7 - r % 2).then_inc(L.xg_done, 1)
                pe.wait_ge(routed, L.l + 1)
                accumulate_zero(True)
                pe.wait_ge(L.gu_in[L.slot(0)], 32)
                pe.wait_ge(L.xs_done, 4)
                gate_up(L.slot(0), xsT[0], 0, range(KC)).then_inc(L.gu_done, 1)

                def step(e, c, it, last=False):
                    j, n = c % GRP, c + 1
                    pe.wait_ge(L.h_ready, e + 1)
                    transposes(sg[c // GRP % 2], j).then_inc(L.tr_done, 1)
                    if not last:
                        pe.wait_ge(L.gu_in[L.slot(n)], (2 * it + n // 3) * 32 + 32)
                        if n % GRP == 0:
                            pe.wait_ge(L.xs_done, (2 * it + n // 3) * 4 + 4)
                        gate_up(L.slot(n), xsT[n // GRP % 2], n % GRP, range(4))
                    pe.wait_ge(L.t_ready, e + 1)
                    pe.wait_ge(L.dn_in[L.slot(c)], (2 * it + c // 3) * 16 + 16)
                    down(L.slot(c)).then_inc(L.dn_done, 1)
                    more = not last and c < BODY and j < 2 and not isinstance(it, int)
                    if more:
                        if j == 0:
                            pe.wait_ge(L.s_ready, 2 * it + c // 3 + 2)
                        pe.wait_ge(L.xs_done, (2 * it + c // 3) * 4 + 4 + 2 * j)
                        gather(4 * j, GW, 7).then_inc(L.xg_done, 1)
                    if not last:
                        gate_up(L.slot(n), xsT[n // GRP % 2], n % GRP, range(4, KC)).then_inc(L.gu_done, 1)
                    pe.wait_ge(L.y_ready, e + 1)
                    combine()
                    if more:
                        pe.wait_ge(L.xs_done, (2 * it + c // 3) * 4 + 5 + 2 * j)
                        gather(4 * j + 2, GW, 7).then_inc(L.xg_done, 1)

                with pe.Fori(0, TURNS) as it:
                    for c in range(BODY):
                        step(BODY * it + c, c, it)
                step(BODY * TURNS, 0, TURNS)
                step(BODY * TURNS + 1, 1, TURNS, last=True)

                n_ov = pe.value_load(ov_info[0:1, OVER:OVER + 1], min_val=0, max_val=OVER)
                s = ov_slot[L.l]
                with pe.Fori(0, OVER) as i:
                    with pe.If(i < n_ov):
                        pe.wait_ge(L.ov_s, i + 1)
                        for r in range(4):
                            if r:
                                pe.wait_ge(L.ov_xs, 4 * i + r)
                            gather(2 * r, SLOTS, 7).then_inc(L.ov_xg, 1)
                        pe.wait_ge(L.ov_xs, 4 * i + 4)
                        pe.wait_ge(L.ov_in, 48 * i + 48)
                        gate_up(s, xsT[1], 0, range(KC)).then_inc(L.ov_gu, 1)
                        pe.wait_ge(L.ov_h, i + 1)
                        transposes(sg[1], 0).then_inc(L.ov_tr, 1)
                        pe.wait_ge(L.ov_t, i + 1)
                        down(s).then_inc(L.dn_done, 1)
                        pe.wait_ge(L.ov_y, i + 1)
                        combine()
                accumulate_zero(False).then_inc(L.acc_done, 1)

            norm_transpose(0)
            route_products(layers[0])
            experts(layers[0])

            norm_transpose(1)
            pe.wait_ge(pin_in, 32)
            for b in range(8):
                if b >= 4:
                    pe.wait_ge(up_ready, b - 3)
                for k in range(KC):
                    ins = mm(PS[:, 4 + b % 4, 0:256], pool_w[:, k, P * b:P * b + P], h2T[:, k, :],
                             start=k == 0, stop=k == KC - 1)
                ins.then_inc(u_done, 1)
            for q in range(8):
                g, ob = divmod(q, 2)
                pe.wait_ge(d_ready, g + 1)
                if q < 4:
                    pe.wait_ge(up_ready, q + 5)
                else:
                    pe.wait_ge(y1_ready, q - 3)
                for i in range(2):
                    ins = mm(PS[:, 4 + q % 4, 0:256], grp_w[:, g, i, P * ob:P * ob + P], dT[:, 2 * g + i, :],
                             start=i == 0, stop=i == 1)
                ins.then_inc(y1_done, 1)
            pe.wait_ge(y1_ready, 8)
            pe.wait_ge(pout_in, 16)
            for q in range(4):
                for k in range(KC):
                    ins = mm(bank(q), y1T[:, k, P * (q // 2):P * (q // 2) + P],
                             pout_w[:, k, 512 * (q % 2):512 * (q % 2) + 512], start=k == 0, stop=k == KC - 1)
                ins.then_inc(po_done, 1)

            norm_transpose(2)
            route_products(layers[1])
            experts(layers[1])

        @block.scalar
        def _(act):
            A = nc.scalar.activation
            act.dma_start(const[:, :], const_d).then_inc(const_in, 16)
            act.dma_start(rows, row_d[0].partition_broadcast(P)).then_inc(rows_in, 16)
            act.dma_start(rope_raw, rope_d.rearrange("p (a t d) -> p a t d", a=2, t=NT)).then_inc(rows_in, 16)
            act.wait_ge(vec_in, 16)
            act.wait_ge(zeroed, 1)
            A(ccols[:, :].rearrange("p (k m) -> p m k", m=32)[:, 0:2, :],
              vec[:, V_C:V_C + 16].rearrange("p (m k) -> p m k", m=2), ACT.Silu).then_inc(silu_c, 1)
            act.wait_ge(ctx_in, 16)
            for t in range(NT):
                if t:
                    act.wait_ge(ss_ready, t)
                A(sq, ctx_sb[:, t, :], ACT.Square, accum_out=ss0[:, t:t + 1]).then_inc(ss_ready, 1)
            act.wait_ge(x_in, 16)
            for t in range(NT):
                act.wait_ge(ss_ready, 2 + t)
                A(sq, x_sb[:, t, :], ACT.Square, accum_out=ss0[:, 2 + t:3 + t]).then_inc(ss_ready, 1)

            def mod_copy(i):
                act.wait_ge(mod_mm, i + 1)
                if i >= 1:
                    act.wait_ge(mod_fin, i)
                nc.scalar.copy(modraw, bank(0, 2)).then_inc(mod_raw, 1)

            mod_copy(0)
            mod_copy(1)
            act.wait_ge(lam_sum, 1)
            A(lam_s, lam_s, ACT.Exp).then_inc(lam_exp, 1)
            act.wait_ge(mod_used, 2)
            for k in range(KC):
                act.wait_ge(xt_c, k + 1)
                A(hT[:, k, 256:512], PS[:, 6 + k % 2, 0:256], ACT.Identity, bias=col(2, 1)[:, k:k + 1],
                  scale=col(2, 0)[:, k:k + 1]).then_inc(h_c, 1)
            for g, p in ((0, 2), (1, 5)):
                act.dma_start(gate_row[g], ada_b[0, D * p:D * (p + 1)].partition_broadcast(P)).then_inc(bias0_in, 16)

            def kq_copy(m):
                act.wait_ge(kq_tr, m + 1)
                dst = kT[:, :, P * m:P * m + P] if m < 4 else qT[:, :, P * (m - 4):P * (m - 4) + P]
                nc.scalar.copy(dst, bank(2, 2).rearrange("p (h t) -> p h t", h=HEADS)).then_inc(kq_in, 1)

            for n in range(10):
                act.wait_ge(proj_done, n + 1)
                src = bank(4 + 2 * (n % 2), 2)
                if 4 <= n < 8:
                    nc.scalar.copy(vals[:, n - 4, :], src).then_inc(proj_used, 1)
                else:
                    m = n if n < 4 else n - 4
                    if m >= 1:
                        act.wait_ge(qn_ready, m)
                    nc.scalar.copy(raw, src).then_inc(proj_used, 1)
                    act.wait_ge(proj_used, n + 1)
                    nc.scalar.square(sq, raw).then_inc(sq_ready, 1)
                if 1 <= n <= 4:
                    kq_copy(n - 1)
                if n <= 3:
                    mod_copy(n + 2)
                if n == 9:
                    for g, p in ((2, 2), (3, 5)):
                        act.dma_start(gate_row[g], ada_b[1, D * p:D * (p + 1)].partition_broadcast(P)).then_inc(bias1_in, 16)
                    kq_copy(4)
            kq_copy(5)
            for u in range(17):
                if u < 16:
                    b = u % 2
                    act.wait_ge(max_ready, u + 1)
                    if u >= 2:
                        act.wait_ge(w_ready, u - 1)
                    for m in range(2):
                        ins = A(probs[:, b, m, :], bank(4 + 2 * b + m), ACT.Exp, bias=ust(b, 2 + m),
                                scale=SCALE, accum_out=ust(b, 4 + m))
                    ins.then_inc(exp_done, 1)
                if u >= 1:
                    v = u - 1
                    b = v % 2
                    act.wait_ge(w_tr, v + 1)
                    if v >= 2:
                        act.wait_ge(pv_done, v - 1)
                    nc.scalar.copy(wT[:, b].rearrange("p c n -> p (c n)"), bank(2)).then_inc(wT_ready, 1)
                if u < 12 and u % 2 == 0:
                    mod_copy(6 + u // 2)
                if u >= 1:
                    act.wait_ge(pv_done, v + 1)
                    if v >= 2:
                        act.wait_ge(on_ready, v - 1)
                    nc.scalar.copy(o_sb[:, b, :], PS[:, 3, 0:128]).then_inc(o_ready, 1)
                    act.wait_ge(o_ready, 2 * v + 1)
                    A(o_junk, o_sb[:, b, :], ACT.Square, accum_out=oss(b)).then_inc(o_ready, 1)
            act.wait_ge(scored, 16)
            act.dma_start(rw, router_w.rearrange("(k p) e -> p k e", p=P)).then_inc(rw_in, 16)
            act.wait_ge(mod_used, 12)

            def norm_part(n, l, what):
                for t in range(NT):
                    act.wait_ge(x_upd, 4 * n + 2 * t + 2)
                    if n or t:
                        act.wait_ge(ssn_ready, 2 * n + t)
                    A(bank(0, 2), x_sb[:, t, :], ACT.Square, accum_out=ssn[:, t:t + 1]).then_inc(ssn_ready, 1)
                for k in range(1, KC, 2):
                    act.wait_ge(nt_tr, 8 * n + k + 1)
                    A(h2T[:, k, :], PS[:, 4 + k % 4, 0:256], ACT.Identity, bias=col(l, what + 1)[:, k:k + 1],
                      scale=col(l, what)[:, k:k + 1]).then_inc(h2_a, 1)

            def route_part(L):
                act.wait_ge(rt_part, L.l + 1)
                nc.scalar.copy(part_lg, PS[:, 0, 0:256]).then_inc(rt_sb, 1)
                act.wait_ge(lg_ready, L.l + 1)
                A(rt(0), rt(0), ACT.Exp).then_inc(lg_exp, 1)

            def spread(L, xs, k0, n, src):
                for c in range(2):
                    k = k0 + c
                    ins = A(xs[:, k, 0:n], PS[:, src, GW * c:GW * c + n], ACT.Identity,
                            bias=col(L.l, 3)[:, k:k + 1], scale=col(L.l, 2)[:, k:k + 1])
                return ins

            def experts(L):
                for r in range(4):
                    act.wait_ge(L.xg_done, r + 1)
                    spread(L, xsT[0], 2 * r, GW, 7 - r % 2).then_inc(L.xs_done, 1)
                act.wait_ge(L.gu_done, 1)
                A(silu_sb, PS[:, 4, 0:256], ACT.Silu).then_inc(L.silu_done, 1)

                def step(e, c, it, last=False):
                    j = c % GRP
                    act.wait_ge(L.tr_done, e + 1)
                    nc.scalar.copy(t_sb, bank(5)).then_inc(L.t_ready, 1)
                    more = not isinstance(it, int) and j < 2
                    if more:
                        act.wait_ge(L.xg_done, (2 * it + c // 3) * 4 + 5 + 2 * j)
                        spread(L, xsT[(c // 3 + 1) % 2], 4 * j, GW, 7).then_inc(L.xs_done, 1)
                    if not last:
                        act.wait_ge(L.gu_done, e + 2)
                        act.wait_ge(L.h_ready, e + 1)
                        A(silu_sb, PS[:, 4, 0:256], ACT.Silu).then_inc(L.silu_done, 1)
                    if more:
                        act.wait_ge(L.xg_done, (2 * it + c // 3) * 4 + 6 + 2 * j)
                        spread(L, xsT[(c // 3 + 1) % 2], 4 * j + 2, GW, 7).then_inc(L.xs_done, 1)

                with act.Fori(0, TURNS) as it:
                    for c in range(BODY):
                        step(BODY * it + c, c, it)
                step(BODY * TURNS, 0, TURNS)
                step(BODY * TURNS + 1, 1, TURNS, last=True)
                act.wait_ge(routed, L.l + 1)
                n_ov = act.value_load(ov_info[0:1, OVER:OVER + 1], min_val=0, max_val=OVER)
                with act.Fori(0, OVER) as i:
                    with act.If(i < n_ov):
                        for r in range(4):
                            act.wait_ge(L.ov_xg, 4 * i + r + 1)
                            spread(L, xsT[1], 2 * r, SLOTS, 7).then_inc(L.ov_xs, 1)
                        act.wait_ge(L.ov_gu, i + 1)
                        A(silu_sb, PS[:, 4, 0:256], ACT.Silu).then_inc(L.ov_silu, 1)
                        act.wait_ge(L.ov_tr, i + 1)
                        nc.scalar.copy(t_sb, bank(5)).then_inc(L.ov_t, 1)

            norm_part(0, 0, 2)
            route_part(layers[0])
            experts(layers[0])
            norm_part(1, 1, 0)
            for b in range(8):
                act.wait_ge(u_done, b + 1)
                if b < 2:
                    act.wait_ge(borders, 1)
                else:
                    act.wait_ge(d_ready, b // 2)
                nc.scalar.copy(up[:, b % 2, PAD:PAD + SEQ], PS[:, 4 + b % 4, 0:256]).then_inc(up_ready, 1)
            for q in range(8):
                act.wait_ge(y1_done, q + 1)
                A(y1T[:, q, :], PS[:, 4 + q % 4, 0:256], ACT.Identity, scale=vec[:, V_PS + q:V_PS + q + 1]).then_inc(y1_ready, 1)
            norm_part(2, 1, 2)
            route_part(layers[1])
            experts(layers[1])
            for t in range(NT):
                act.wait_ge(x_upd, 12 + 2 * t + 2)
                act.dma_start(out_d[0, P * t:P * t + P, :], x_sb[:, t, :]).then_inc(out_stored, 16)
            act.wait_ge(out_stored, 32)

        @block.vector
        def _(dve):
            V = nc.vector
            linked = [0]

            def link(ins):
                linked[0] += 1
                ins.then_inc(chain, 1)
                dve.wait_ge(chain, linked[0])

            V.memset(ccols[:, :], 0.0).then_inc(zeroed, 1)

            for a, src, dst in ((0, ctx_sb, ctx_sb), (1, x_sb, xn0)):
                dve.wait_ge(ss_ready, 2 * a + 2)
                V.tensor_scalar(ms0[:, 2 * a:2 * a + 2], ss0[:, 2 * a:2 * a + 2], 1.0 / D, EPS, ALU.mult, ALU.add).then_inc(ms_ready, 1)
                dve.wait_ge(pow_done, a + 1)
                for t in range(NT):
                    ins = V.tensor_scalar(dst[:, t, :], src[:, t, :], ms0[:, 2 * a + t:2 * a + t + 1], None, ALU.mult)
                ins.then_inc(xn0_ready, 1)

            dve.wait_ge(rows_in, 32)
            tab = rope_g[:, :].rearrange("p (a t d) -> p a t d", a=4, t=NT)
            for a, r in ((0, R_QG), (2, R_KG)):
                g = rows[:, r:r + HD]
                V.tensor_tensor(tab[:, a], rope_raw[:, 0], g.unsqueeze(1).broadcast_to([P, NT, HD]), ALU.mult)
                gh = g.rearrange("p (q h n) -> p q h n", q=2, h=2)
                for t in range(NT):
                    to = tab[:, a + 1, t].rearrange("p (q h n) -> p q h n", q=2, h=2)
                    of = rope_raw[:, 1, t].rearrange("p (q h n) -> p q h n", q=2, h=2)
                    for h in range(2):
                        V.tensor_tensor(to[:, :, h], of[:, :, h], gh[:, :, 1 - h], ALU.mult)
            V.tensor_copy(rbias[:, :], rows[:, R_RB:R_RB + NE])
            lq = rows[:, R_LQ:R_LQ + 256].rearrange("p (a b n) -> p a b n", a=2, b=2)
            lt = lam_t.rearrange("p (a n) -> p a n", a=2)
            link(V.tensor_tensor(lt, lq[:, :, 0], lq[:, :, 1], ALU.mult))
            V.reduce_sum(lam_s, lt, AX).then_inc(lam_sum, 1)

            def mod_use(i):
                l, p = divmod(i, 6)
                dve.wait_ge(mod_fin, i + 1)
                if i:
                    dve.wait_ge(mod_used, i)
                if p not in COL_PARTS:
                    dve.wait_ge((bias0_in, bias1_in)[l], 32)
                    g = gate_row[2 * l + (p == 5)]
                    V.tensor_tensor(g, bank(0, 2), g, ALU.add).then_inc(mod_used, 1)
                    return
                parts = bank(0, 2).rearrange("p (k j m) -> p k j m", k=KC, j=4)
                who = 2 if i < 2 else 1
                for m in range(who):
                    ins = V.reduce_sum(nt_tmp[:, 8 * m:8 * m + 8], parts[:, :, :, m], AX)
                link(ins)
                q = COL_PARTS.index(p)
                for m in range(who):
                    to = col(2 if m else l, (1, 0, 3, 2)[q])
                    s = nt_tmp[:, 8 * m:8 * m + 8]
                    if q % 2 == 0:
                        ins = V.tensor_tensor(to, s, bias_col(i), ALU.add)
                    else:
                        ins = V.tensor_tensor(nt_tmp[:, 16 + 8 * m:24 + 8 * m], s, bias_col(i), ALU.add)
                if q % 2:
                    link(ins)
                    v0 = (V_N1 if q == 1 else V_N2) + 8 * l
                    for m in range(who):
                        to = col(2 if m else l, (1, 0, 3, 2)[q])
                        ins = V.scalar_tensor_tensor(to, nt_tmp[:, 16 + 8 * m:24 + 8 * m], 1.0, vec[:, v0:v0 + 8], ALU.add, ALU.mult)
                ins.then_inc(mod_used, 1)

            dve.wait_ge(vec_in, 16)
            mod_use(0)
            mod_use(1)
            dve.wait_ge(mod_used, 2)
            for k in range(KC):
                dve.wait_ge(xt_x, k + 1)
                V.tensor_scalar(hT[:, k, 0:256], PS[:, 4 + k % 2, 0:256], col(0, 0)[:, k:k + 1], col(0, 1)[:, k:k + 1],
                                ALU.mult, ALU.add).then_inc(h_x, 1)
            dve.wait_ge(lam_exp, 1)
            V.scalar_tensor_tensor(neglam, lam_s[:, 1:2], -LAM_INIT, lam_s[:, 0:1], ALU.add, ALU.subtract).then_inc(lam_done, 1)

            def kq_item(m):
                t = m if m < 4 else m - 4
                turned = m >= 4 or m < 2
                dve.wait_ge(sq_ready, m + 1)
                if m:
                    dve.wait_ge(qn_ready, m)
                link(V.reduce_sum(ssk, sq.rearrange("p (h d) -> p h d", d=HD), AX))
                V.tensor_scalar(msk, ssk, 1.0 / HD, EPS, ALU.mult, ALU.add).then_inc(ms_ready, 1)
                if turned:
                    a = 0 if m >= 4 else 2
                    r4 = raw.rearrange("p (h q s n) -> p h q s n", q=2, s=2, n=16)
                    b4 = rb.rearrange("p (h q s n) -> p h q s n", q=2, s=2, n=16)
                    sn = tab[:, a + 1, t].rearrange("p (q s n) -> p q s n", q=2, s=2)
                    V.tensor_tensor(ra.rearrange("p (h d) -> p h d", d=HD), raw.rearrange("p (h d) -> p h d", d=HD),
                                    tab[:, a, t].unsqueeze(1).broadcast_to([P, 16, HD]), ALU.mult)
                    for s in range(2):
                        ins = V.tensor_tensor(b4[:, :, :, s], r4[:, :, :, 1 - s],
                                              sn[:, :, s].unsqueeze(1).broadcast_to([P, 16, 2, 16]), ALU.mult)
                    link(ins)
                    link(V.tensor_tensor(ra, ra, rb, ALU.add))
                else:
                    link(V.tensor_tensor(ra.rearrange("p (h d) -> p h d", d=HD), raw.rearrange("p (h d) -> p h d", d=HD),
                                         rows[:, R_KG:R_KG + HD].unsqueeze(1).broadcast_to([P, 16, HD]), ALU.mult))
                dve.wait_ge(pow_done, 2 + m + 1)
                if m >= 1:
                    dve.wait_ge(kq_tr, m)
                V.tensor_tensor(qn.rearrange("p (h d) -> p h d", d=HD), ra.rearrange("p (h d) -> p h d", d=HD),
                                msk.unsqueeze(2).broadcast_to([P, 16, HD]), ALU.mult).then_inc(qn_ready, 1)

            for n in range(10):
                if 1 <= n <= 4:
                    mod_use(n + 1)
                if n < 4 or n >= 8:
                    kq_item(n if n < 4 else n - 4)
            dve.wait_ge(lam_done, 1)
            for u in range(18):
                b = u % 2
                if u < 16:
                    dve.wait_ge(scored, u + 1)
                    if u >= 2:
                        dve.wait_ge(w_ready, u - 1)
                    link(V.reduce_max(ust(b, 0, 2), PS[:, 4 + 2 * b:6 + 2 * b, :], AX))
                    V.tensor_scalar(ust(b, 2, 2), ust(b, 0, 2), -SCALE, None, ALU.mult).then_inc(max_ready, 1)
                if u >= 2:
                    v = u - 2
                    dve.wait_ge(o_tr, v + 1)
                    V.tensor_scalar(oT[:, v % 8, P * (v // 8):P * (v // 8) + P], PS[:, 3, 128:256],
                                    vec[:, V_SUB:V_SUB + 1], 1 - LAM_INIT, ALU.mult, ALU.mult).then_inc(oT_ready, 1)
                if u < 16:
                    dve.wait_ge(exp_done, u + 1)
                    link(V.reciprocal(ust(b, 6, 2), ust(b, 4, 2)))
                    link(V.tensor_scalar(ust(b, 8), ust(b, 7), neglam, None, ALU.mult))
                    if u >= 2:
                        dve.wait_ge(w_tr, u - 1)
                    link(V.tensor_scalar(wmix[:, b, :], probs[:, b, 0, :], ust(b, 6), None, ALU.mult))
                    V.scalar_tensor_tensor(wmix[:, b, :], probs[:, b, 1, :], ust(b, 8), wmix[:, b, :],
                                           ALU.mult, ALU.add).then_inc(w_ready, 1)
                if u < 12 and u % 2 == 1:
                    mod_use(6 + u // 2)
                if 1 <= u <= 16:
                    v = u - 1
                    c = v % 2
                    dve.wait_ge(o_ready, 2 * v + 2)
                    if v >= 2:
                        dve.wait_ge(on_ready, v - 1)
                    V.tensor_scalar(oms(c), oss(c), 1.0 / P, EPS, ALU.mult, ALU.add).then_inc(ms_ready, 1)
                    dve.wait_ge(pow_done, 8 + v + 1)
                    if v >= 2:
                        dve.wait_ge(o_tr, v - 1)
                    V.tensor_scalar(o_n[:, c, :], o_sb[:, c, :], oms(c), None, ALU.mult).then_inc(on_ready, 1)

            def residual(g, first, wait):
                for q in range(4):
                    wait(q)
                    if g or q:
                        dve.wait_ge(x_upd, 4 * g + q)
                    half = slice(512 * (q % 2), 512 * (q % 2) + 512)
                    link(V.tensor_tensor(res_t, bank(first + q), gate_row[g][:, half], ALU.mult))
                    xs = x_sb[:, q // 2, half]
                    V.tensor_tensor(xs, xs, res_t, ALU.add).then_inc(x_upd, 1)

            def norm_part(n, l, what):
                for t in range(NT):
                    dve.wait_ge(ssn_ready, 2 * n + t + 1)
                    dve.wait_ge(x_upd, 4 * n + 2 * t + 2)
                    V.tensor_scalar(msn[:, t:t + 1], ssn[:, t:t + 1], 1.0 / D, EPS, ALU.mult, ALU.add).then_inc(ms_ready, 1)
                    dve.wait_ge(pow_done, 24 + 2 * n + t + 1)
                    V.tensor_scalar(xn[:, t, :], x_sb[:, t, :], msn[:, t:t + 1], None, ALU.mult).then_inc(xn_ready, 1)
                for k in range(0, KC, 2):
                    dve.wait_ge(nt_tr, 8 * n + k + 1)
                    V.tensor_scalar(h2T[:, k, :], PS[:, 4 + k % 4, 0:256], col(l, what)[:, k:k + 1],
                                    col(l, what + 1)[:, k:k + 1], ALU.mult, ALU.add).then_inc(h2_v, 1)

            def across(ap, n=NE):
                return ap.unsqueeze(2).broadcast_to([P, NT, n])

            def row(c, n, m=NT):
                return const[:, c:c + n].unsqueeze(1).broadcast_to([P, m, n])

            def routing(L):
                pr, pm, t, oh1, oh2, srt = (t2(rt(i)) for i in range(6))
                chosen, pd = t2(rt(8)), t2(rt(9))
                sm = rt(10, 64)
                mx, z, tm, v1, v2, v12 = (sm[:, 2 * i:2 * i + 2] for i in range(6))
                gs, gt = sm[:, 16:24].rearrange("p (t g) -> p t g", t=NT), sm[:, 24:32].rearrange("p (t g) -> p t g", t=NT)
                gsel, gm1 = sm[:, 32:40].rearrange("p (t g) -> p t g", t=NT), sm[:, 40:48].rearrange("p (t g) -> p t g", t=NT)
                ov, cum, before = rt(11, 32), rt(11, 64)[:, 32:64], rt(12, 32)
                late, tile_e, cnt = rt(12, 64)[:, 32:64], rt(7, 8), rt(6)[:, 0:32]
                dve.wait_ge(rt_logit, L.l + 1)
                lg = PS[:, 1, 0:64].rearrange("p (t e) -> p t e", t=NT)
                link(V.tensor_tensor(pr, lg, rbias[:, :].unsqueeze(1).broadcast_to([P, NT, NE]), ALU.add))
                link(V.reduce_max(mx, pr, AX))
                V.tensor_tensor(pr, pr, across(mx), ALU.subtract).then_inc(lg_ready, 1)
                dve.wait_ge(lg_exp, L.l + 1)
                link(V.reduce_sum(z, pr, AX))
                link(V.reciprocal(z, z))
                link(V.tensor_tensor(pr, pr, across(z), ALU.mult))
                for tt in range(NT):
                    for g in range(NG):
                        ins = V.max(srt[:, tt, 8 * g:8 * g + 8], pr[:, tt, 8 * g:8 * g + 8])
                link(ins)
                s4 = srt.rearrange("p t (g s) -> p t g s", g=NG)
                link(V.tensor_tensor(gs, s4[:, :, :, 0], s4[:, :, :, 1], ALU.add))
                link(V.reduce_max(mx, gs, AX))
                link(V.tensor_tensor(gt, gs, across(mx, NG), ALU.is_equal))
                link(V.tensor_tensor(gt, gt, row(C_W4, NG), ALU.mult))
                link(V.reduce_max(tm, gt, AX))
                link(V.tensor_tensor(gsel, gt, across(tm, NG), ALU.is_equal))
                link(V.tensor_scalar(gm1, gsel, -1.0, None, ALU.add))

                def g8(ap, tt):
                    return ap[:, tt].unsqueeze(2).broadcast_to([P, NG, PER_G])

                def e4(ap, tt):
                    return ap[:, tt].rearrange("p (g s) -> p g s", g=NG)

                for tt in range(NT):
                    ins = V.tensor_tensor(e4(pm, tt), e4(pr, tt), g8(gsel, tt), ALU.mult)
                link(ins)
                for tt in range(NT):
                    ins = V.tensor_tensor(e4(pm, tt), e4(pm, tt), g8(gm1, tt), ALU.add)
                link(ins)

                def first_largest(v, oh):
                    link(V.reduce_max(v, pm, AX))
                    link(V.tensor_tensor(t, pm, across(v), ALU.is_equal))
                    link(V.tensor_tensor(t, t, row(C_W32, NE), ALU.mult))
                    link(V.reduce_max(tm, t, AX))
                    link(V.tensor_tensor(oh, t, across(tm), ALU.is_equal))

                first_largest(v1, oh1)
                link(V.scalar_tensor_tensor(pm, oh1, -4.0, pm, ALU.mult, ALU.add))
                first_largest(v2, oh2)
                V.tensor_tensor(chosen, oh1, oh2, ALU.add).then_inc(rt_sel, 1)
                link(V.tensor_tensor(v12, v1, v2, ALU.add))
                link(V.reciprocal(v12, v12))
                V.tensor_tensor(gate[:, 0:2], v1, v12, ALU.mult)
                link(V.tensor_tensor(gate[:, 2:4], v2, v12, ALU.mult))
                dve.wait_ge(rt_cnt, L.l + 1)
                link(V.tensor_copy(cnt, PS[:, 2, 64:96]))
                link(V.tensor_scalar(ov, cnt, SLOTS + 0.5, None, ALU.is_ge))
                for n in range(2, SEQ // SLOTS):
                    link(V.scalar_tensor_tensor(ov, cnt, SLOTS * n + 0.5, ov, ALU.is_ge, ALU.add))
                link(V.tensor_tensor_scan(cum, const[:, C_ONES:C_ONES + 32], ov, 0.0, ALU.mult, ALU.add))
                link(V.tensor_tensor(before, cum, ov, ALU.subtract))
                link(V.scalar_tensor_tensor(late, before, float(SLOTS), const[:, C_DELTA:C_DELTA + NE], ALU.mult, ALU.add))
                cmp = rt(0, 7 * 32).rearrange("p (i e) -> p i e", i=OVER)
                ranks = PS[:, 2, 0:64].rearrange("p (t e) -> p t e", t=NT)
                link(V.tensor_scalar(pd, ranks, SLOTS - 0.5, None, ALU.is_ge))
                link(V.tensor_tensor(pd, pd, late.unsqueeze(1).broadcast_to([P, NT, NE]), ALU.mult))
                link(V.tensor_tensor(pd, pd, ranks, ALU.add))
                link(V.tensor_tensor(pd, pd, row(C_BASE, NE), ALU.add))
                for a, oh in ((0, oh1), (1, oh2)):
                    link(V.tensor_tensor(oh, pd, oh, ALU.mult))
                    link(V.reduce_sum(pos[:, 2 * a:2 * a + 2], oh, AX))
                link(V.tensor_tensor(cmp, cum.unsqueeze(1).broadcast_to([P, OVER, NE]),
                                     const[:, C_TILE:C_TILE + OVER].unsqueeze(2).broadcast_to([P, OVER, NE]), ALU.is_le))
                link(V.reduce_sum(tile_e[:, 0:OVER], cmp, AX))
                link(V.tensor_copy(tile_e[:, OVER:OVER + 1], cum[:, NE - 1:NE]))
                link(V.tensor_copy(ov_info[:, :], tile_e[:, 0:8]))
                V.tensor_copy(pcur, pos).then_inc(routed, 1)
                dve.wait_ge(routed, L.l + 1)

            def choose(n, g, parts, whole, binary, before=None):
                if before is not None:
                    dve.wait_ge(*before)
                for a in range(2):
                    for t in range(NT):
                        i = 2 * a + t
                        ins = V.tensor_scalar(part[a][:, t, 0:n], const[:, C_IOTA:C_IOTA + n], pcur[:, i:i + 1],
                                              gate[:, i:i + 1], ALU.is_equal, ALU.mult)
                ins.then_inc(parts[0], 1)
                dve.wait_ge(*parts)
                for t in range(NT):
                    first, second = (part[a][:, t, 0:n].rearrange("p (j n) -> p j n", n=SLOTS).unsqueeze(2)
                                     .broadcast_to([P, n // SLOTS, 2, SLOTS]) for a in range(2))
                    ins = V.tensor_tensor(g[:, t, 0:n // SLOTS], first, second, ALU.add)
                ins.then_inc(whole[0], 1)
                dve.wait_ge(*whole)
                V.tensor_scalar(s01[:, :, 0:n].rearrange("p t (j n) -> p t j n", n=SLOTS), g[:, :, 0:n // SLOTS, 0], 0.0, None,
                                ALU.is_gt).then_inc(binary, 1)

            def experts(L):
                choose(GW, sg[0], (L.parts, 1), (L.sg_done, 1), L.s_ready)

                def hidden(n):
                    dve.wait_ge(L.silu_done, n)
                    V.tensor_tensor(h_sb, silu_sb, PS[:, 4, 256:512], ALU.mult).then_inc(L.h_ready, 1)

                hidden(1)

                def step(e, c, it, last=False):
                    if not isinstance(it, int) and c % GRP == 0:
                        g = 2 * it + c // 3 + 1
                        V.tensor_scalar(pcur, pcur, -float(GW), None, ALU.add).then_inc(L.shifted, 1)
                        dve.wait_ge(L.shifted, g)
                        choose(GW, sg[(c // 3 + 1) % 2], (L.parts, g + 1), (L.sg_done, g + 1), L.s_ready, (L.s_ready, g))
                    dve.wait_ge(L.dn_done, e + 1)
                    V.tensor_copy(y_sb, bank(6)).then_inc(L.y_ready, 1)
                    if not last:
                        hidden(e + 2)

                with dve.Fori(0, TURNS) as it:
                    for c in range(BODY):
                        step(BODY * it + c, c, it)
                step(BODY * TURNS, 0, TURNS)
                step(BODY * TURNS + 1, 1, TURNS, last=True)
                link(V.tensor_scalar(pcur, pos, -float(NE * SLOTS - SLOTS), None, ALU.add))
                n_ov = dve.value_load(ov_info[0:1, OVER:OVER + 1], min_val=0, max_val=OVER)
                with dve.Fori(0, OVER) as i:
                    with dve.If(i < n_ov):
                        V.tensor_scalar(pcur, pcur, -float(SLOTS), None, ALU.add).then_inc(L.ov_shift, 1)
                        dve.wait_ge(L.ov_shift, i + 1)
                        choose(SLOTS, sg[1], (L.ov_parts, i + 1), (L.ov_sg, i + 1), L.ov_s)
                        dve.wait_ge(L.ov_silu, i + 1)
                        V.tensor_tensor(h_sb, silu_sb, PS[:, 4, 256:512], ALU.mult).then_inc(L.ov_h, 1)
                        dve.wait_ge(L.dn_done, NE + i + 1)
                        V.tensor_copy(y_sb, bank(6)).then_inc(L.ov_y, 1)

            residual(0, 4, lambda q: dve.wait_ge(op_done, q + 1))
            norm_part(0, 0, 2)
            V.memset(ccols[:, :], 0.0)
            routing(layers[0])
            experts(layers[0])
            residual(1, 0, lambda q: dve.wait_ge(layers[0].acc_done, 1))
            norm_part(1, 1, 0)

            V.memset(up, 0.0).then_inc(borders, 1)
            dve.wait_ge(invn_in, 16)
            for g, w in enumerate(WINDOWS):
                dve.wait_ge(up_ready, 2 * g + 2)
                cur, reach, a = up, 1, 0
                while reach < w:
                    nxt = pool_sum[a]
                    back, fore = (1, 0) if reach == 1 else (reach // 2, reach // 2)
                    lo, hi = reach, UP - reach + 1
                    link(V.tensor_tensor(nxt[:, :, lo:hi], cur[:, :, lo - back:hi - back], cur[:, :, lo + fore:hi + fore], ALU.add))
                    cur, reach, a = nxt, 2 * reach, 1 - a
                mean = pool_sum[a][:, :, PAD:PAD + SEQ]
                link(V.tensor_tensor(mean, cur[:, :, PAD:PAD + SEQ], inv_n[:, g].unsqueeze(1).broadcast_to([P, 2, SEQ]), ALU.mult))
                V.tensor_tensor(dT[:, 2 * g:2 * g + 2, :], mean, up[:, :, PAD:PAD + SEQ], ALU.subtract).then_inc(d_ready, 1)

            residual(2, 0, lambda q: dve.wait_ge(po_done, q + 1))
            norm_part(2, 1, 2)
            routing(layers[1])
            experts(layers[1])
            residual(3, 0, lambda q: dve.wait_ge(layers[1].acc_done, 1))


_DIRECT = ["x", "ctx", "ada_w", "ada_b", "attn_w_in", "attn_w_out", "pool_w_in", "pool_w_group", "pool_w_out",
           "router_w", "moe_w_gate", "moe_w_up", "moe_w_down"]


def kernel(**inputs):
    import concourse.bacc as bacc
    from concourse.bass_utils import run_bass_kernel_spmd

    a = {n: np.ascontiguousarray(v) for n, v in inputs.items()}

    def columns(v):
        return v.reshape(-1, KC, P).transpose(2, 0, 1).reshape(P, -1)

    ada_cols = a["ada_b"].reshape(2, 6, D)[:, list(COL_PARTS)]
    vec = np.concatenate([columns(a["c"]), columns(a["c_ctx"]), columns(a["norm1_g"]), columns(a["norm2_g"]),
                          columns(a["pool_scale"]), a["attn_sub_gain"].reshape(P, 1), columns(ada_cols)], 1)
    row = np.concatenate([a[n].reshape(-1) for n in ("attn_q_gain", "attn_k_gain", "attn_lq1", "attn_lk1", "attn_lq2",
                                                     "attn_lk2", "router_b")])[None]
    const, rope, inv_n = constants()
    arrays = {n: a[n] for n in _DIRECT}
    arrays |= {"vec": np.ascontiguousarray(vec), "row": np.ascontiguousarray(row), "const": const, "rope": rope, "inv_n": inv_n}
    nc = bacc.Bacc("TRN2", target_bir_lowering=False, num_devices=1)
    args = [nc.dram_tensor(f"in_{n}", v.shape, mybir.dt.from_np(v.dtype), kind="ExternalInput").ap() for n, v in arrays.items()]
    out = nc.dram_tensor("out", (1, SEQ, D), F32, kind="ExternalOutput").ap()
    program(nc, *args, out)
    r = run_bass_kernel_spmd(nc, [{f"in_{n}": v for n, v in arrays.items()}], core_ids=[0])
    return r.results[0]["out"]
```

```python
import math
from contextlib import ExitStack

import numpy as np

import concourse.bass as bass
from concourse import mybir

F32 = mybir.dt.float32
BF16 = mybir.dt.bfloat16
I32 = mybir.dt.int32
ALU = mybir.AluOpType
ACT = mybir.ActivationFunctionType
AX = mybir.AxisListType.X

P = 128
D = 1024
KC = D // P
SEQ = 256
NT = SEQ // P
HEADS, HD = 8, 64
EPS = 1e-6
LAM_INIT = 0.8 - 0.6 * math.exp(-0.3 * 0)
SCALE = HD ** -0.5
NE, NG, PER_G = 32, 4, 8
FF = 512
SLOTS = 64
OVER = (2 * SEQ) // (SLOTS + 1)
GRP = 3
BODY = 2 * GRP
TURNS = NE // BODY
GW = GRP * SLOTS
WINDOWS = (2, 4, 8, 16)
PAD = max(WINDOWS) // 2
UP = SEQ + 2 * PAD

C_ID, C_TRI, C_ONES, C_SEL = 0, 128, 256, 384
C_IOTA = 512
C_STACK = C_IOTA + GW
C_W4 = C_STACK + 32
C_W32 = C_W4 + 4
C_BASE = C_W32 + 32
C_DELTA = C_BASE + 32
C_TILE = C_DELTA + 32
N_CONST = C_TILE + 8
V_C, V_N1, V_N2, V_PS, V_SUB, V_ADA = 0, 16, 32, 48, 56, 57
N_VEC = V_ADA + 64
R_QG, R_KG, R_LQ, R_RB = 0, 64, 128, 384
N_ROW = 416
COL_PARTS = (0, 1, 3, 4)


def constants():
    c = np.zeros((P, N_CONST), np.float32)
    r = np.arange(P)
    c[:, C_ID:C_ID + P] = np.eye(P)
    c[:, C_TRI:C_TRI + P] = r[:, None] < r[None, :]
    c[:, C_ONES:C_ONES + P] = 1
    c[::32, C_SEL:C_SEL + P] = 1
    c[:, C_IOTA:C_IOTA + GW] = np.arange(GW)
    c[:, C_STACK:C_STACK + 32] = r[:, None] % 32 == np.arange(32)
    c[:, C_W4:C_W4 + 4] = NG - np.arange(4)
    c[:, C_W32:C_W32 + 32] = NE - np.arange(32)
    c[:, C_BASE:C_BASE + 32] = SLOTS * np.arange(32)
    c[:, C_DELTA:C_DELTA + 32] = NE * SLOTS - SLOTS - SLOTS * np.arange(32)
    c[:, C_TILE:C_TILE + 8] = np.arange(8)
    half = HD // 2
    inv = (10000.0 ** (-np.arange(0, half, 2, dtype=np.float32) / half)).astype(np.float32)
    t = np.arange(SEQ)
    ar = (t // 64).astype(np.float32)[:, None] * inv
    ac = (t % 64).astype(np.float32)[:, None] * inv
    cos = np.cos(np.concatenate([ar, ar, ac, ac], 1))
    sin = np.sin(np.concatenate([-ar, ar, -ac, ac], 1))
    rope = np.stack([cos, sin]).astype(np.float32).reshape(2, NT, P, HD).transpose(2, 0, 1, 3)
    n = np.stack([np.minimum(t + w // 2, SEQ) - np.maximum(t - w // 2, 0) for w in WINDOWS])
    inv_n = (np.float32(1) / n.astype(np.float32)).astype(np.float32)
    return c, np.ascontiguousarray(rope).reshape(P, -1), inv_n.reshape(1, -1)


def program(nc, x_d, ctx_d, ada_w, ada_b, w_in, w_out, pool_in, pool_grp, pool_out, router_w,
            w_gate, w_up, w_down, vec_d, row_d, const_d, rope_d, inv_n_d, out_d):
    stack = ExitStack()
    with stack:
        def sb(name, n, dt=F32):
            return stack.enter_context(nc.sbuf_tensor(name, [P, n], dt))

        def sem(name):
            return stack.enter_context(nc.semaphore(name))

        ring = sb("ring", 36864)
        X = sb("X", 2048)
        HT = sb("HT", 4096)
        KT = sb("KT", 4096)
        QT = sb("QT", 2048)
        TMP = sb("TMP", 2048)
        const = sb("const", N_CONST)
        vec = sb("vec", N_VEC)
        rope_g = sb("rope_g", 4 * 2 * HD)
        ccols = sb("ccols", KC * 32)
        cols = sb("cols", 80)
        stat = sb("stat", 80)
        rbias = sb("rbias", 32)
        ov_info = sb("ov_info", 8, I32)
        PS = stack.enter_context(nc.psum_tensor("PS", [P, 8, 512], F32))

        def bank(i, n=1):
            return PS[:, i, :] if n == 1 else PS[:, i:i + n, :].rearrange("p b n -> p (b n)")

        ident = const[:, C_ID:C_ID + P]
        tri = const[:, C_TRI:C_TRI + P]
        ones = const[:, C_ONES:C_ONES + P]
        sel = const[:, C_SEL:C_SEL + P]
        x_sb = X[:, :].rearrange("p (t d) -> p t d", t=NT)

        def unit(i):
            return ring[:, 8192 * i:8192 * (i + 1)].rearrange("p (k n) -> p k n", k=8)

        vals = ring[:, 24576:28672].rearrange("p (t n) -> p t n", t=4)
        work = 28672
        modraw = ring[:, work:work + 1024]
        raw = ring[:, work + 1024:work + 2048]
        sq = ring[:, work + 2048:work + 3072]
        ra = ring[:, work + 3072:work + 4096]
        rb = ring[:, work + 4096:work + 5120]
        qn = ring[:, work + 5120:work + 6144]
        xn0 = ring[:, work + 5120:work + 7168].rearrange("p (t d) -> p t d", t=NT)
        rope_raw = ring[:, work + 7168:work + 7424].rearrange("p (a t d) -> p a t d", a=2, t=NT)
        rows = ring[:, work + 7424:work + 7424 + N_ROW]
        lam_t = ring[:, work + 7840:work + 7968]
        probs = ring[:, work + 1024:work + 3072].rearrange("p (b m n) -> p b m n", b=2, m=2)
        wmix = ring[:, work + 3072:work + 4096].rearrange("p (b n) -> p b n", b=2)
        wT = ring[:, work + 4096:work + 5120].rearrange("p (b c n) -> p b c n", b=2, c=4)
        o_sb = ring[:, work + 5120:work + 6144].rearrange("p (b n) -> p b n", b=8)

        ctx_sb = TMP[:, :].rearrange("p (t d) -> p t d", t=NT)
        hT = HT[:, :].rearrange("p (k t) -> p k t", k=KC)
        oT = HT[:, 0:2048].rearrange("p (h t) -> p h t", h=HEADS)
        h2T = HT[:, 0:2048].rearrange("p (k t) -> p k t", k=KC)
        gate_row = [TMP[:, 0:1024], TMP[:, 1024:2048], HT[:, 2048:3072], HT[:, 3072:4096]]
        kT = KT[:, :].rearrange("p (h t) -> p h t", h=HEADS)
        qT = [z.rearrange("p (h t) -> p h t", h=HEADS) for z in (QT[:, :], ring[:, work + 6144:work + 8192])]
        xn = KT[:, 0:2048].rearrange("p (t d) -> p t d", t=NT)


        slot = [ring[:, 12288 * i:12288 * (i + 1)] for i in range(3)]
        gu_w = [s[:, 0:8192].rearrange("p (k a f) -> p k a f", k=KC, a=2) for s in slot]
        dn_w = [s[:, 8192:12288].rearrange("p (c n) -> p c n", c=4) for s in slot]
        xsT = [KT[:, 2048:2048 + KC * GW].rearrange("p (k n) -> p k n", k=KC),
               QT[:, 0:KC * GW].rearrange("p (k n) -> p k n", k=KC)]
        silu_sb = KT[:, 3584:3840]
        h_sb = KT[:, 3840:4096]
        res_t = KT[:, 3584:4096]
        rw = QT[:, 1536:1792].rearrange("p (k e) -> p k e", k=KC)
        part_lg = QT[:, 1792:2048]
        sg = HT[:, 0:768].rearrange("p (t n) -> p t n", t=NT)
        s01 = HT[:, 768:1152].rearrange("p (t n) -> p t n", t=NT)
        t_sb = HT[:, 1152:1664]
        part = [rope_g[:, 0:384].rearrange("p (t n) -> p t n", t=NT), HT[:, 1664:2048].rearrange("p (t n) -> p t n", t=NT)]
        y_sb = TMP[:, 0:1024]
        route = sb("route", 16)
        pos, gate, pcur = (route[:, 4 * i:4 * i + 4] for i in range(3))
        nt_tmp = sb("nt_tmp", 32)
        mhalf = sb("mhalf", 16)

        def rt(i, n=64):
            return TMP[:, 64 * i:64 * i + n]

        def t2(ap):
            return ap.rearrange("p (t e) -> p t e", t=NT)

        pool_w = slot[2][:, 0:8192].rearrange("p (k n) -> p k n", k=KC)
        grp_w = slot[2][:, 8192:10240].rearrange("p (g i n) -> p g i n", g=4, i=2)
        pout_w = slot[0][:, 0:8192].rearrange("p (k n) -> p k n", k=KC)
        dT = KT[:, 2048:4096].rearrange("p (b t) -> p b t", b=8)
        y1T = KT[:, 0:2048].rearrange("p (b t) -> p b t", b=8)
        up = QT[:, 0:2 * UP].rearrange("p (i t) -> p i t", i=2)
        pool_sum = [TMP[:, 1024:1024 + 2 * UP].rearrange("p (i t) -> p i t", i=2),
                    QT[:, 2 * UP:4 * UP].rearrange("p (i t) -> p i t", i=2)]
        inv_n = TMP[:, 0:1024].rearrange("p (g t) -> p g t", g=4)

        ss0, ms0 = stat[:, 0:4], stat[:, 4:8]
        ssn, msn = stat[:, 12:14], stat[:, 14:16]
        ssk, msk = stat[:, 18:34], stat[:, 34:50]
        neglam = stat[:, 76:77]
        lam_s = stat[:, 77:79]

        def ust(b, i, n=1):
            return stat[:, 50 + 10 * b + i:50 + 10 * b + i + n]

        oss, oms = stat[:, 18:34], stat[:, 34:50]

        def col(l, what):
            c = 32 * l + 8 * what
            return cols[:, c:c + 8]

        def bias_col(i):
            l, p = divmod(i, 6)
            c = V_ADA + 8 * (4 * l + COL_PARTS.index(p))
            return vec[:, c:c + 8]

        const_in, rows_in, vec_in, x_in, ctx_in = (sem(n) for n in ("const_in", "rows_in", "vec_in", "x_in", "ctx_in"))
        rw_in, bias0_in, bias1_in = sem("rw_in"), sem("bias0_in"), sem("bias1_in")
        ada_in = [sem(f"ada_in{i}") for i in range(12)]
        w_in_s = {n: sem(f"w{n}_in") for n in "kvqo"}
        chain = sem("chain")
        zeroed, minus_half, silu_c, lam_sum, lam_exp, lam_done = (sem(n) for n in ("zeroed", "minus_half", "silu_c", "lam_sum", "lam_exp", "lam_done"))
        ss_ready, ms_ready, pow_done, xn0_ready = (sem(n) for n in ("ss_ready", "ms_ready", "pow_done", "xn0_ready"))
        mod_mm, mod_raw, mod_fin, mod_used = (sem(n) for n in ("mod_mm", "mod_raw", "mod_fin", "mod_used"))
        xt_x, xt_c, h_x, h_c = (sem(n) for n in ("xt_x", "xt_c", "h_x", "h_c"))
        proj_done, proj_used, sq_ready, qn_ready, kq_tr, kq_in = (sem(n) for n in ("proj_done", "proj_used", "sq_ready", "qn_ready", "kq_tr", "kq_in"))
        scored, max_ready, exp_done, w_ready, w_tr, wT_ready, pv_done, o_ready, on_ready, o_tr, oT_ready = (
            sem(n) for n in ("scored", "max_ready", "exp_done", "w_ready", "w_tr", "wT_ready", "pv_done", "o_ready", "on_ready", "o_tr", "oT_ready"))
        op_done, x_upd, ssn_ready, xn_ready, nt_tr, h2_v, h2_a = (sem(n) for n in ("op_done", "x_upd", "ssn_ready", "xn_ready", "nt_tr", "h2_v", "h2_a"))
        rt_part, rt_sb, rt_logit, lg_ready, lg_exp, rt_sel, rt_cnt, routed = (sem(n) for n in ("rt_part", "rt_sb", "rt_logit", "lg_ready", "lg_exp", "rt_sel", "rt_cnt", "routed"))
        pin_in, pout_in, invn_in, u_done, up_ready, d_ready, y1_done, y1_ready, po_done = (
            sem(n) for n in ("pin_in", "pout_in", "invn_in", "u_done", "up_ready", "d_ready", "y1_done", "y1_ready", "po_done"))
        out_stored, borders, q_zeroed = sem("out_stored"), sem("borders"), sem("q_zeroed")

        class Layer:
            def __init__(self, l):
                self.l = l
                self.gu_in = [sem(f"gu_in{l}_{i}") for i in range(3)]
                self.dn_in = [sem(f"dn_in{l}_{i}") for i in range(3)]
                (self.shifted, self.parts, self.sg_done, self.s_ready, self.xg_done, self.xs_done, self.gu_done,
                 self.silu_done, self.h_ready, self.tr_done, self.t_ready, self.dn_done, self.y_v, self.y_a, self.acc_done) = (
                    sem(f"{n}{l}") for n in ("shifted", "parts", "sg_done", "s_ready", "xg_done", "xs_done", "gu_done",
                                             "silu_done", "h_ready", "tr_done", "t_ready", "dn_done", "y_v", "y_a", "acc_done"))
                (self.ov_in, self.ov_shift, self.ov_parts, self.ov_sg, self.ov_s, self.ov_xg, self.ov_xs, self.ov_gu,
                 self.ov_silu, self.ov_h, self.ov_tr, self.ov_t, self.ov_yv, self.ov_ya) = (
                    sem(f"ov_{n}{l}") for n in ("in", "shift", "parts", "sg", "s", "xg", "xs", "gu", "silu", "h", "tr", "t", "yv", "ya"))

            def slot(self, e):
                return (e + self.l) % 3

        layers = [Layer(0), Layer(1)]
        ov_slot = [L.slot(NE - 1) for L in layers]
        block = stack.enter_context(nc.Block())

        @block.sync
        def _(sp):
            def rows_of(w, c0, n):
                return w.rearrange("(k p) n -> p k n", p=P)[:, :, c0:c0 + n]

            def load_expert(L, e, s):
                sp.dma_start(gu_w[s][:, :, 0, :], w_gate[L.l, e].rearrange("(k p) f -> p k f", p=P)).then_inc(L.gu_in[s], 16)
                sp.dma_start(gu_w[s][:, :, 1, :], w_up[L.l, e].rearrange("(k p) f -> p k f", p=P)).then_inc(L.gu_in[s], 16)
                sp.dma_start(dn_w[s], w_down[L.l, e].rearrange("(c p) n -> p c n", p=P)).then_inc(L.dn_in[s], 16)

            def load_freed(L, e, s):
                sp.wait_ge(L.gu_done, e - 2)
                sp.wait_ge(L.dn_done, e - 2)
                load_expert(L, e, s)

            sp.dma_start(vec[:, :], vec_d).then_inc(vec_in, 16)
            sp.dma_start(ctx_sb, ctx_d[0].rearrange("(t p) d -> p t d", p=P)).then_inc(ctx_in, 16)
            sp.dma_start(x_sb, x_d[0].rearrange("(t p) d -> p t d", p=P)).then_inc(x_in, 16)

            def load_ada(i):
                sp.dma_start(unit(i % 2), rows_of(ada_w[i // 6], D * (i % 6), D)).then_inc(ada_in[i], 16)

            load_ada(0)
            load_ada(1)
            sp.dma_start(unit(2), rows_of(w_in[0], D, D)).then_inc(w_in_s["k"], 16)
            for i in range(2, 6):
                sp.wait_ge(mod_mm, i - 1)
                load_ada(i)
            sp.wait_ge(mod_mm, 5)
            sp.dma_start(unit(0), rows_of(w_in[0], 2 * D, D)).then_inc(w_in_s["v"], 16)
            sp.wait_ge(mod_mm, 6)
            sp.dma_start(unit(1), rows_of(w_in[0], 0, D)).then_inc(w_in_s["q"], 16)
            sp.wait_ge(proj_done, 4)
            sp.dma_start(unit(2), rows_of(w_out[0], 0, D)).then_inc(w_in_s["o"], 16)
            for i in range(6, 12):
                if i == 6:
                    sp.wait_ge(proj_done, 8)
                elif i == 7:
                    sp.wait_ge(proj_done, 10)
                else:
                    sp.wait_ge(mod_mm, i - 1)
                load_ada(i)
            L = layers[0]
            sp.wait_ge(mod_mm, 12)
            load_expert(L, 0, 0)
            sp.wait_ge(oT_ready, 4)
            sp.wait_ge(mod_used, 12)
            load_expert(L, 2, 2)
            sp.wait_ge(op_done, 4)
            load_expert(L, 1, 1)
            for L in layers:
                with sp.Fori(0, (NE - 5) // 3) as it:
                    for c in range(3):
                        load_freed(L, 3 * it + (3 + c), L.slot(c))
                for e in range(3 + 3 * ((NE - 5) // 3), NE):
                    load_freed(L, e, L.slot(e))
                if L.l == 0:
                    sp.wait_ge(L.gu_done, 30)
                    sp.wait_ge(L.dn_done, 30)
                    sp.dma_start(pool_w, rows_of(pool_in[0], 0, D)).then_inc(pin_in, 16)
                    sp.dma_start(grp_w, pool_grp[0].rearrange("g (i p) n -> p g i n", p=P)).then_inc(pin_in, 16)
                    sp.wait_ge(L.gu_done, 31)
                    sp.wait_ge(L.dn_done, 31)
                    sp.dma_start(pout_w, rows_of(pool_out[0], 0, D)).then_inc(pout_in, 16)
                sp.wait_ge(L.gu_done, NE)
                sp.wait_ge(L.dn_done, NE)
                sp.wait_ge(routed, L.l + 1)
                n_ov = sp.value_load(ov_info[0:1, OVER:OVER + 1], min_val=0, max_val=OVER)
                with sp.Fori(0, OVER) as i:
                    with sp.If(i < n_ov):
                        sp.wait_ge(L.dn_done, NE + i)
                        e = sp.value_load(ov_info[0:1, bass.ds(i, 1)], min_val=0, max_val=NE - 1)
                        s = ov_slot[L.l]
                        sp.dma_start(gu_w[s][:, :, 0, :], w_gate[L.l, bass.ds(e, 1)].rearrange("o (k p) f -> p (o k) f", p=P)).then_inc(L.ov_in, 16)
                        sp.dma_start(gu_w[s][:, :, 1, :], w_up[L.l, bass.ds(e, 1)].rearrange("o (k p) f -> p (o k) f", p=P)).then_inc(L.ov_in, 16)
                        sp.dma_start(dn_w[s], w_down[L.l, bass.ds(e, 1)].rearrange("o (c p) n -> p (o c) n", p=P)).then_inc(L.ov_in, 16)
                if L.l == 0:
                    L1 = layers[1]
                    sp.wait_ge(L.acc_done, 1)
                    load_expert(L1, 0, L1.slot(0))
                    sp.dma_start(TMP[:, 0:1024], inv_n_d[0].partition_broadcast(P)).then_inc(invn_in, 16)
                    sp.wait_ge(y1_done, 8)
                    load_expert(L1, 1, L1.slot(1))
                    sp.wait_ge(po_done, 4)
                    load_expert(L1, 2, L1.slot(2))

        @block.gpsimd
        def _(pool):
            nc.gpsimd.memset(mhalf[:, :], -0.5).then_inc(minus_half, 1)
            pool.wait_ge(minus_half, 1)

            def inverse_root(n, ap):
                pool.wait_ge(ms_ready, n + 1)
                nc.gpsimd.tensor_tensor(ap, ap, mhalf[:, 0:ap.shape[1]], ALU.pow).then_inc(pow_done, 1)

            inverse_root(0, ms0[:, 0:2])
            inverse_root(1, ms0[:, 2:4])
            for n in range(6):
                inverse_root(2 + n, msk)
            for g in range(4):
                inverse_root(8 + g, oms[:, 4 * g:4 * g + 4])
            for n in range(6):
                inverse_root(12 + n, msn[:, n % 2:n % 2 + 1])

        @block.tensor
        def _(pe):
            mm, tr = nc.tensor.matmul, nc.tensor.transpose

            def ada_mm(i):
                pe.wait_ge(ada_in[i], 16)
                if i == 0:
                    pe.wait_ge(silu_c, 1)
                else:
                    pe.wait_ge(mod_used, i)
                for c in range(2):
                    for half in range(2):
                        for j in range(4):
                            k = 2 * j + c
                            ins = mm(PS[32 * j:32 * j + 32, half, :], ccols[:, 32 * k:32 * k + 32],
                                     unit(i % 2)[:, k, 512 * half:512 * half + 512], start=c == 0, stop=c == 1)
                ins.then_inc(mod_mm, 1)

            def ada_fin(i):
                pe.wait_ge(mod_raw, i + 1)
                if i % 6 in COL_PARTS:
                    for k in range(KC):
                        ins = tr(PS[:, k // 4, 128 * (k % 4):128 * (k % 4) + 128], modraw[:, P * k:P * k + P], ident)
                else:
                    for half in range(2):
                        ins = mm(bank(half), sel, modraw[:, 512 * half:512 * half + 512], start=True, stop=True)
                ins.then_inc(mod_fin, 1)

            pe.wait_ge(const_in, 16)
            for i in range(2):
                ada_mm(i)
                ada_fin(i)
            pe.wait_ge(xn0_ready, 2)
            for k in range(KC):
                if k >= 2:
                    pe.wait_ge(h_x, k - 1)
                    pe.wait_ge(h_c, k - 1)
                for t in range(NT):
                    ins = tr(PS[:, 4 + k % 2, P * t:P * t + P], xn0[:, t, P * k:P * k + P], ident)
                ins.then_inc(xt_x, 1)
                for t in range(NT):
                    ins = tr(PS[:, 6 + k % 2, P * t:P * t + P], ctx_sb[:, t, P * k:P * k + P], ident)
                ins.then_inc(xt_c, 1)
            pe.wait_ge(h_x, KC)
            pe.wait_ge(h_c, KC)

            def proj(n):
                which, t, u = ("k", n, 2) if n < 4 else ("v", n - 4, 0) if n < 8 else ("q", n - 8, 1)
                pe.wait_ge(w_in_s[which], 16)
                if n >= 2:
                    pe.wait_ge(proj_used, n - 1)
                for half in range(2):
                    for k in range(KC):
                        ins = mm(bank(4 + 2 * (n % 2) + half), hT[:, k, P * t:P * t + P],
                                 unit(u)[:, k, 512 * half:512 * half + 512], start=k == 0, stop=k == KC - 1)
                ins.then_inc(proj_done, 1)

            def kq_transpose(m):
                pe.wait_ge(qn_ready, m + 1)
                if m >= 1:
                    pe.wait_ge(kq_in, m)
                for h in range(HEADS):
                    ins = tr(PS[:, 2 + h // 4, P * (h % 4):P * (h % 4) + P], qn[:, P * h:P * h + P], ident)
                ins.then_inc(kq_tr, 1)

            for n in range(10):
                proj(n)
                if 1 <= n <= 4:
                    ada_fin(n + 1)
                    kq_transpose(n - 1)
                if n <= 3:
                    ada_mm(n + 2)
                if n == 9:
                    kq_transpose(4)
            kq_transpose(5)
            pe.wait_ge(kq_in, 6)

            def scores(u):
                qt, h = divmod(u, HEADS)
                if u >= 2:
                    pe.wait_ge(exp_done, u - 1)
                for m in range(2):
                    ins = mm(bank(4 + 2 * (u % 2) + m), qT[m][:, h, P * qt:P * qt + P], kT[:, h, :], start=True, stop=True)
                ins.then_inc(scored, 1)

            def turn_outputs(g):
                pe.wait_ge(on_ready, g + 1)
                if g >= 2:
                    pe.wait_ge(mod_used, 12)
                for j in range(4):
                    ins = tr(PS[:, (2, 2, 0, 1)[g], P * j:P * j + P], o_sb[:, 4 * (g % 2) + j, :], ident)
                ins.then_inc(o_tr, 1)

            scores(0)
            scores(1)
            for u in range(16):
                pe.wait_ge(w_ready, u + 1)
                if u >= 1:
                    pe.wait_ge(wT_ready, u)
                if u in (7, 11):
                    pe.wait_ge(oT_ready, u // 4)
                for c in range(4):
                    ins = tr(PS[:, 2, P * c:P * c + P], wmix[:, u % 2, P * c:P * c + P], ident)
                ins.then_inc(w_tr, 1)
                if u < 14:
                    scores(u + 2)
                pe.wait_ge(wT_ready, u + 1)
                if u >= 1:
                    pe.wait_ge(o_ready, 2 * u)
                h = u % HEADS
                for c in range(4):
                    ins = mm(PS[:, 3, 0:128], wT[:, u % 2, c, :], vals[:, c, P * h:P * h + P], start=c == 0, stop=c == 3)
                ins.then_inc(pv_done, 1)
                if u in (6, 10, 14):
                    turn_outputs((u - 6) // 4)
                if u < 12:
                    if u % 2 == 0:
                        ada_mm(6 + u // 2)
                    else:
                        ada_fin(6 + u // 2)

            pe.wait_ge(w_in_s["o"], 16)
            for q in range(4):
                if q == 0:
                    pe.wait_ge(exp_done, 16)
                    pe.wait_ge(oT_ready, 2)
                if q == 2:
                    pe.wait_ge(oT_ready, 4)
                for h in range(HEADS):
                    ins = mm(bank(4 + q), oT[:, h, P * (q // 2):P * (q // 2) + P],
                             unit(2)[:, h, 512 * (q % 2):512 * (q % 2) + 512], start=h == 0, stop=h == HEADS - 1)
                ins.then_inc(op_done, 1)
                if q == 0:
                    turn_outputs(3)

            def norm_transpose(n):
                pe.wait_ge(xn_ready, 2 * n + 2)
                for k in range(KC):
                    if k >= 4:
                        pe.wait_ge((h2_v, h2_a)[k % 2], 4 * n + (k - 4) // 2 + 1)
                    for t in range(NT):
                        ins = tr(PS[:, 4 + k % 4, P * t:P * t + P], xn[:, t, P * k:P * k + P], ident)
                    ins.then_inc(nt_tr, 1)
                pe.wait_ge(h2_v, 4 * n + 4)
                pe.wait_ge(h2_a, 4 * n + 4)

            def route_products(L):
                pe.wait_ge(rw_in, 16)
                for c in range(2):
                    for j in range(4):
                        ins = mm(PS[32 * j:32 * j + 32, 0, 0:256], rw[:, 2 * j + c, :], h2T[:, 2 * j + c, :],
                                 start=c == 0, stop=c == 1)
                ins.then_inc(rt_part, 1)
                pe.wait_ge(rt_sb, L.l + 1)
                for t in range(NT):
                    ins = mm(PS[:, 1, 32 * t:32 * t + 32], part_lg[:, P * t:P * t + P],
                             const[:, C_STACK:C_STACK + 32], start=True, stop=True)
                ins.then_inc(rt_logit, 1)
                pe.wait_ge(rt_sel, L.l + 1)
                chosen = t2(rt(8))
                mm(PS[:, 2, 0:32], tri, chosen[:, 0, :], start=True, stop=True)
                mm(PS[:, 2, 32:64], ones, chosen[:, 0, :], start=True, stop=False)
                mm(PS[:, 2, 32:64], tri, chosen[:, 1, :], start=False, stop=True)
                mm(PS[:, 2, 64:96], ones, chosen[:, 0, :], start=True, stop=False)
                mm(PS[:, 2, 64:96], ones, chosen[:, 1, :], start=False, stop=True).then_inc(rt_cnt, 1)

            def accumulate_zero(start):
                z = ccols[:, :].bitcast(BF16)
                for b in range(4):
                    ins = mm(bank(b), z[:, 0:128], z[:, :], start=start, stop=not start, skip_group_check=True)
                return ins

            def gather(k0, n, dst):
                for c in range(2):
                    for t in range(NT):
                        ins = mm(PS[:, dst, GW * c:GW * c + n], xn[:, t, P * (k0 + c):P * (k0 + c) + P], s01[:, t, 0:n],
                                 start=t == 0, stop=t == NT - 1)
                return ins

            def gate_up(s, xs, j, ks):
                for k in ks:
                    for f in range(2):
                        ins = mm(PS[64 * f:64 * f + 64, 4, :], xs[:, k, SLOTS * j:SLOTS * j + SLOTS],
                                 gu_w[s][:, k, :, 256 * f:256 * f + 256], start=k == 0, stop=k == KC - 1)
                return ins

            def transposes(first):
                if first is not None:
                    for t in range(NT):
                        tr(PS[:, 5, P * t:P * t + P], sg[:, t, first:first + P], ident)
                for c in range(2):
                    ins = tr(PS[:, 5, 256 + P * c:256 + P * c + P], h_sb[:, P * c:P * c + P], ident)
                return ins

            def down(s):
                for c in range(4):
                    a, b = divmod(c, 2)
                    lhs = t_sb[:, 256 + P * b + 64 * a:256 + P * b + 64 * a + 64]
                    for f in range(2):
                        ins = mm(PS[64 * f:64 * f + 64, 6, :], lhs, dn_w[s][:, c, 512 * f:512 * f + 512],
                                 start=c == 0, stop=c == 3)
                return ins

            def combine():
                for t in range(NT):
                    for f in range(2):
                        mm(bank(2 * t + f), t_sb[:, P * t:P * t + P], y_sb[:, 512 * f:512 * f + 512], start=False, stop=False,
                           skip_group_check=True)

            def experts(L):
                pe.wait_ge(L.s_ready, 1)
                for r in range(4):
                    if r >= 2:
                        pe.wait_ge(L.xs_done, r - 1)
                    gather(2 * r, GW, 7 - r % 2).then_inc(L.xg_done, 1)
                pe.wait_ge(routed, L.l + 1)
                accumulate_zero(True)
                pe.wait_ge(L.gu_in[L.slot(0)], 32)
                pe.wait_ge(L.xs_done, 4)
                gate_up(L.slot(0), xsT[0], 0, range(KC)).then_inc(L.gu_done, 1)

                def step(e, c, it, last=False):
                    j, n = c % GRP, c + 1
                    pe.wait_ge(L.h_ready, e + 1)
                    transposes(None if c % 2 else SLOTS * c).then_inc(L.tr_done, 1)
                    if not last:
                        pe.wait_ge(L.gu_in[L.slot(n)], (2 * it + n // 3) * 32 + 32)
                        if n % GRP == 0:
                            pe.wait_ge(L.xs_done, (2 * it + n // 3) * 4 + 4)
                        gate_up(L.slot(n), xsT[n // GRP % 2], n % GRP, range(4))
                    pe.wait_ge(L.t_ready, e + 1)
                    pe.wait_ge(L.dn_in[L.slot(c)], (2 * it + c // 3) * 16 + 16)
                    if c % 2:
                        pe.wait_ge(L.y_v, e)
                        pe.wait_ge(L.y_a, e)
                    down(L.slot(c)).then_inc(L.dn_done, 1)
                    more = not last and c < BODY and j < 2 and not isinstance(it, int)
                    if more:
                        if j == 0:
                            pe.wait_ge(L.s_ready, 2 * it + c // 3 + 2)
                        pe.wait_ge(L.xs_done, (2 * it + c // 3) * 4 + 4 + 2 * j)
                        gather(4 * j, GW, 7).then_inc(L.xg_done, 1)
                    if not last:
                        gate_up(L.slot(n), xsT[n // GRP % 2], n % GRP, range(4, KC)).then_inc(L.gu_done, 1)
                    if c % 2:
                        pe.wait_ge(L.y_v, e + 1)
                        pe.wait_ge(L.y_a, e + 1)
                        combine()
                    if more:
                        pe.wait_ge(L.xs_done, (2 * it + c // 3) * 4 + 5 + 2 * j)
                        gather(4 * j + 2, GW, 7).then_inc(L.xg_done, 1)

                with pe.Fori(0, TURNS) as it:
                    for c in range(BODY):
                        step(BODY * it + c, c, it)
                step(BODY * TURNS, 0, TURNS)
                step(BODY * TURNS + 1, 1, TURNS, last=True)

                n_ov = pe.value_load(ov_info[0:1, OVER:OVER + 1], min_val=0, max_val=OVER)
                s = ov_slot[L.l]
                with pe.Fori(0, OVER) as i:
                    with pe.If(i < n_ov):
                        pe.wait_ge(L.ov_s, i + 1)
                        for r in range(4):
                            if r:
                                pe.wait_ge(L.ov_xs, 4 * i + r)
                            gather(2 * r, SLOTS, 7).then_inc(L.ov_xg, 1)
                        pe.wait_ge(L.ov_xs, 4 * i + 4)
                        pe.wait_ge(L.ov_in, 48 * i + 48)
                        gate_up(s, xsT[1], 0, range(KC)).then_inc(L.ov_gu, 1)
                        pe.wait_ge(L.ov_h, i + 1)
                        transposes(GW).then_inc(L.ov_tr, 1)
                        pe.wait_ge(L.ov_t, i + 1)
                        down(s).then_inc(L.dn_done, 1)
                        pe.wait_ge(L.ov_yv, i + 1)
                        pe.wait_ge(L.ov_ya, i + 1)
                        combine()
                accumulate_zero(False).then_inc(L.acc_done, 1)

            norm_transpose(0)
            route_products(layers[0])
            experts(layers[0])

            norm_transpose(1)
            pe.wait_ge(pin_in, 32)
            for b in range(8):
                if b >= 4:
                    pe.wait_ge(up_ready, b - 3)
                for k in range(KC):
                    ins = mm(PS[:, 4 + b % 4, 0:256], pool_w[:, k, P * b:P * b + P], h2T[:, k, :],
                             start=k == 0, stop=k == KC - 1)
                ins.then_inc(u_done, 1)
            for q in range(8):
                g, ob = divmod(q, 2)
                pe.wait_ge(d_ready, g + 1)
                if q < 4:
                    pe.wait_ge(up_ready, q + 5)
                else:
                    pe.wait_ge(y1_ready, q - 3)
                for i in range(2):
                    ins = mm(PS[:, 4 + q % 4, 0:256], grp_w[:, g, i, P * ob:P * ob + P], dT[:, 2 * g + i, :],
                             start=i == 0, stop=i == 1)
                ins.then_inc(y1_done, 1)
            pe.wait_ge(y1_ready, 8)
            pe.wait_ge(pout_in, 16)
            for q in range(4):
                for k in range(KC):
                    ins = mm(bank(q), y1T[:, k, P * (q // 2):P * (q // 2) + P],
                             pout_w[:, k, 512 * (q % 2):512 * (q % 2) + 512], start=k == 0, stop=k == KC - 1)
                ins.then_inc(po_done, 1)

            norm_transpose(2)
            route_products(layers[1])
            experts(layers[1])

        @block.scalar
        def _(act):
            A = nc.scalar.activation
            act.dma_start(const[:, :], const_d).then_inc(const_in, 16)
            act.dma_start(rows, row_d[0].partition_broadcast(P)).then_inc(rows_in, 16)
            act.dma_start(rope_raw, rope_d.rearrange("p (a t d) -> p a t d", a=2, t=NT)).then_inc(rows_in, 16)
            act.wait_ge(vec_in, 16)
            act.wait_ge(zeroed, 1)
            A(ccols[:, :].rearrange("p (k m) -> p m k", m=32)[:, 0:2, :],
              vec[:, V_C:V_C + 16].rearrange("p (m k) -> p m k", m=2), ACT.Silu).then_inc(silu_c, 1)
            act.wait_ge(ctx_in, 16)
            for t in range(NT):
                if t:
                    act.wait_ge(ss_ready, t)
                A(sq, ctx_sb[:, t, :], ACT.Square, accum_out=ss0[:, t:t + 1]).then_inc(ss_ready, 1)
            act.wait_ge(x_in, 16)
            for t in range(NT):
                act.wait_ge(ss_ready, 2 + t)
                A(sq, x_sb[:, t, :], ACT.Square, accum_out=ss0[:, 2 + t:3 + t]).then_inc(ss_ready, 1)

            def mod_copy(i):
                act.wait_ge(mod_mm, i + 1)
                if i >= 1:
                    act.wait_ge(mod_fin, i)
                nc.scalar.copy(modraw, bank(0, 2)).then_inc(mod_raw, 1)

            mod_copy(0)
            mod_copy(1)
            act.wait_ge(lam_sum, 1)
            A(lam_s, lam_s, ACT.Exp).then_inc(lam_exp, 1)
            act.wait_ge(mod_used, 2)
            for k in range(KC):
                act.wait_ge(xt_c, k + 1)
                A(hT[:, k, 256:512], PS[:, 6 + k % 2, 0:256], ACT.Identity, bias=col(2, 1)[:, k:k + 1],
                  scale=col(2, 0)[:, k:k + 1]).then_inc(h_c, 1)
            for g, p in ((0, 2), (1, 5)):
                act.dma_start(gate_row[g], ada_b[0, D * p:D * (p + 1)].partition_broadcast(P)).then_inc(bias0_in, 16)

            def kq_copy(m):
                act.wait_ge(kq_tr, m + 1)
                src = bank(2, 2).rearrange("p (h t) -> p h t", h=HEADS)
                if m < 4:
                    ins = nc.scalar.copy(kT[:, :, P * m:P * m + P], src)
                else:
                    act.wait_ge(q_zeroed, 2)
                    for a in range(2):
                        r = slice(64 * a, 64 * a + 64)
                        ins = nc.scalar.copy(qT[a][r, :, P * (m - 4):P * (m - 4) + P], src[r])
                ins.then_inc(kq_in, 1)

            for n in range(10):
                act.wait_ge(proj_done, n + 1)
                src = bank(4 + 2 * (n % 2), 2)
                if 4 <= n < 8:
                    nc.scalar.copy(vals[:, n - 4, :], src).then_inc(proj_used, 1)
                else:
                    m = n if n < 4 else n - 4
                    if m >= 1:
                        act.wait_ge(qn_ready, m)
                    nc.scalar.copy(raw, src).then_inc(proj_used, 1)
                    act.wait_ge(proj_used, n + 1)
                    nc.scalar.square(sq, raw).then_inc(sq_ready, 1)
                if 1 <= n <= 4:
                    kq_copy(n - 1)
                if n <= 3:
                    mod_copy(n + 2)
                if n == 9:
                    for g, p in ((2, 2), (3, 5)):
                        act.dma_start(gate_row[g], ada_b[1, D * p:D * (p + 1)].partition_broadcast(P)).then_inc(bias1_in, 16)
                    kq_copy(4)
            kq_copy(5)
            def exponentials(u):
                b = u % 2
                act.wait_ge(max_ready, u + 1)
                if u >= 2:
                    act.wait_ge(w_ready, u - 1)
                for m in range(2):
                    ins = A(probs[:, b, m, :], bank(4 + 2 * b + m), ACT.Exp, bias=ust(b, 2 + m),
                            scale=SCALE, accum_out=ust(b, 4 + m))
                ins.then_inc(exp_done, 1)

            exponentials(0)
            exponentials(1)
            for u in range(16):
                act.wait_ge(w_tr, u + 1)
                if u >= 2:
                    act.wait_ge(pv_done, u - 1)
                nc.scalar.copy(wT[:, u % 2].rearrange("p c n -> p (c n)"), bank(2)).then_inc(wT_ready, 1)
                if u < 12 and u % 2 == 1:
                    mod_copy(6 + u // 2)
                act.wait_ge(pv_done, u + 1)
                if u >= 8 and u % 4 == 0:
                    act.wait_ge(o_tr, u // 4 - 1)
                nc.scalar.copy(o_sb[:, u % 8, :], PS[:, 3, 0:128]).then_inc(o_ready, 1)
                if u >= 1:
                    act.wait_ge(o_ready, 2 * u)
                A(PS[:, 3, 128:256], PS[:, 3, 0:128], ACT.Square, accum_out=oss[:, u:u + 1]).then_inc(o_ready, 1)
                if u < 14:
                    exponentials(u + 2)
            act.wait_ge(scored, 16)
            act.dma_start(rw, router_w.rearrange("(k p) e -> p k e", p=P)).then_inc(rw_in, 16)
            act.wait_ge(mod_used, 12)

            def norm_part(n, l, what):
                for t in range(NT):
                    act.wait_ge(x_upd, 4 * n + 2 * t + 2)
                    if n or t:
                        act.wait_ge(ssn_ready, 2 * n + t)
                    A(bank(0, 2), x_sb[:, t, :], ACT.Square, accum_out=ssn[:, t:t + 1]).then_inc(ssn_ready, 1)
                for k in range(1, KC, 2):
                    act.wait_ge(nt_tr, 8 * n + k + 1)
                    A(h2T[:, k, :], PS[:, 4 + k % 4, 0:256], ACT.Identity, bias=col(l, what + 1)[:, k:k + 1],
                      scale=col(l, what)[:, k:k + 1]).then_inc(h2_a, 1)

            def route_part(L):
                act.wait_ge(rt_part, L.l + 1)
                nc.scalar.copy(part_lg, PS[:, 0, 0:256]).then_inc(rt_sb, 1)
                act.wait_ge(lg_ready, L.l + 1)
                A(rt(0), rt(0), ACT.Exp).then_inc(lg_exp, 1)

            def spread(L, xs, k0, n, src):
                for c in range(2):
                    k = k0 + c
                    ins = A(xs[:, k, 0:n], PS[:, src, GW * c:GW * c + n], ACT.Identity,
                            bias=col(L.l, 3)[:, k:k + 1], scale=col(L.l, 2)[:, k:k + 1])
                return ins

            def upper_outputs(second):
                return nc.scalar.copy(y_sb[64 * second:64 * second + 64, 512:1024], PS[64:128, 6, :])

            def experts(L):
                for r in range(4):
                    act.wait_ge(L.xg_done, r + 1)
                    spread(L, xsT[0], 2 * r, GW, 7 - r % 2).then_inc(L.xs_done, 1)
                act.wait_ge(L.gu_done, 1)
                A(silu_sb, PS[:, 4, 0:256], ACT.Silu).then_inc(L.silu_done, 1)

                def step(e, c, it, last=False):
                    j = c % GRP
                    act.wait_ge(L.tr_done, e + 1)
                    a = 256 * (c % 2)
                    nc.scalar.copy(t_sb[:, a:512], PS[:, 5, a:512]).then_inc(L.t_ready, 1)
                    act.wait_ge(L.dn_done, e + 1)
                    upper_outputs(c % 2).then_inc(L.y_a, 1)
                    more = not isinstance(it, int) and j < 2
                    if more:
                        act.wait_ge(L.xg_done, (2 * it + c // 3) * 4 + 5 + 2 * j)
                        spread(L, xsT[(c // 3 + 1) % 2], 4 * j, GW, 7).then_inc(L.xs_done, 1)
                    if not last:
                        act.wait_ge(L.gu_done, e + 2)
                        act.wait_ge(L.h_ready, e + 1)
                        A(silu_sb, PS[:, 4, 0:256], ACT.Silu).then_inc(L.silu_done, 1)
                    if more:
                        act.wait_ge(L.xg_done, (2 * it + c // 3) * 4 + 6 + 2 * j)
                        spread(L, xsT[(c // 3 + 1) % 2], 4 * j + 2, GW, 7).then_inc(L.xs_done, 1)

                with act.Fori(0, TURNS) as it:
                    for c in range(BODY):
                        step(BODY * it + c, c, it)
                step(BODY * TURNS, 0, TURNS)
                step(BODY * TURNS + 1, 1, TURNS, last=True)
                act.wait_ge(routed, L.l + 1)
                n_ov = act.value_load(ov_info[0:1, OVER:OVER + 1], min_val=0, max_val=OVER)
                with act.Fori(0, OVER) as i:
                    with act.If(i < n_ov):
                        for r in range(4):
                            act.wait_ge(L.ov_xg, 4 * i + r + 1)
                            spread(L, xsT[1], 2 * r, SLOTS, 7).then_inc(L.ov_xs, 1)
                        act.wait_ge(L.ov_gu, i + 1)
                        A(silu_sb, PS[:, 4, 0:256], ACT.Silu).then_inc(L.ov_silu, 1)
                        act.wait_ge(L.ov_tr, i + 1)
                        nc.scalar.copy(t_sb, bank(5)).then_inc(L.ov_t, 1)
                        act.wait_ge(L.dn_done, NE + i + 1)
                        upper_outputs(0).then_inc(L.ov_ya, 1)

            norm_part(0, 0, 2)
            route_part(layers[0])
            experts(layers[0])
            norm_part(1, 1, 0)
            for b in range(8):
                act.wait_ge(u_done, b + 1)
                if b < 2:
                    act.wait_ge(borders, 1)
                else:
                    act.wait_ge(d_ready, b // 2)
                nc.scalar.copy(up[:, b % 2, PAD:PAD + SEQ], PS[:, 4 + b % 4, 0:256]).then_inc(up_ready, 1)
            for q in range(8):
                act.wait_ge(y1_done, q + 1)
                A(y1T[:, q, :], PS[:, 4 + q % 4, 0:256], ACT.Identity, scale=vec[:, V_PS + q:V_PS + q + 1]).then_inc(y1_ready, 1)
            norm_part(2, 1, 2)
            route_part(layers[1])
            experts(layers[1])
            for t in range(NT):
                act.wait_ge(x_upd, 12 + 2 * t + 2)
                act.dma_start(out_d[0, P * t:P * t + P, :], x_sb[:, t, :]).then_inc(out_stored, 16)
            act.wait_ge(out_stored, 32)

        @block.vector
        def _(dve):
            V = nc.vector
            linked = [0]

            def link(ins):
                linked[0] += 1
                ins.then_inc(chain, 1)
                dve.wait_ge(chain, linked[0])

            V.memset(ccols[:, :], 0.0).then_inc(zeroed, 1)

            for a, src, dst in ((0, ctx_sb, ctx_sb), (1, x_sb, xn0)):
                dve.wait_ge(ss_ready, 2 * a + 2)
                V.tensor_scalar(ms0[:, 2 * a:2 * a + 2], ss0[:, 2 * a:2 * a + 2], 1.0 / D, EPS, ALU.mult, ALU.add).then_inc(ms_ready, 1)
                dve.wait_ge(pow_done, a + 1)
                for t in range(NT):
                    ins = V.tensor_scalar(dst[:, t, :], src[:, t, :], ms0[:, 2 * a + t:2 * a + t + 1], None, ALU.mult)
                ins.then_inc(xn0_ready, 1)

            dve.wait_ge(rows_in, 32)
            tab = rope_g[:, :].rearrange("p (a t d) -> p a t d", a=4, t=NT)
            for a, r in ((0, R_QG), (2, R_KG)):
                g = rows[:, r:r + HD]
                V.tensor_tensor(tab[:, a], rope_raw[:, 0], g.unsqueeze(1).broadcast_to([P, NT, HD]), ALU.mult)
                gh = g.rearrange("p (q h n) -> p q h n", q=2, h=2)
                for t in range(NT):
                    to = tab[:, a + 1, t].rearrange("p (q h n) -> p q h n", q=2, h=2)
                    of = rope_raw[:, 1, t].rearrange("p (q h n) -> p q h n", q=2, h=2)
                    for h in range(2):
                        V.tensor_tensor(to[:, :, h], of[:, :, h], gh[:, :, 1 - h], ALU.mult)
            V.tensor_copy(rbias[:, :], rows[:, R_RB:R_RB + NE])
            lq = rows[:, R_LQ:R_LQ + 256].rearrange("p (a b n) -> p a b n", a=2, b=2)
            lt = lam_t.rearrange("p (a n) -> p a n", a=2)
            link(V.tensor_tensor(lt, lq[:, :, 0], lq[:, :, 1], ALU.mult))
            V.reduce_sum(lam_s, lt, AX).then_inc(lam_sum, 1)

            def mod_use(i):
                l, p = divmod(i, 6)
                dve.wait_ge(mod_fin, i + 1)
                if i:
                    dve.wait_ge(mod_used, i)
                if p not in COL_PARTS:
                    dve.wait_ge((bias0_in, bias1_in)[l], 32)
                    g = gate_row[2 * l + (p == 5)]
                    V.tensor_tensor(g, bank(0, 2), g, ALU.add).then_inc(mod_used, 1)
                    return
                parts = bank(0, 2).rearrange("p (k j m) -> p k j m", k=KC, j=4)
                who = 2 if i < 2 else 1
                for m in range(who):
                    ins = V.reduce_sum(nt_tmp[:, 8 * m:8 * m + 8], parts[:, :, :, m], AX)
                link(ins)
                q = COL_PARTS.index(p)
                for m in range(who):
                    to = col(2 if m else l, (1, 0, 3, 2)[q])
                    s = nt_tmp[:, 8 * m:8 * m + 8]
                    if q % 2 == 0:
                        ins = V.tensor_tensor(to, s, bias_col(i), ALU.add)
                    else:
                        ins = V.tensor_tensor(nt_tmp[:, 16 + 8 * m:24 + 8 * m], s, bias_col(i), ALU.add)
                if q % 2:
                    link(ins)
                    v0 = (V_N1 if q == 1 else V_N2) + 8 * l
                    for m in range(who):
                        to = col(2 if m else l, (1, 0, 3, 2)[q])
                        ins = V.scalar_tensor_tensor(to, nt_tmp[:, 16 + 8 * m:24 + 8 * m], 1.0, vec[:, v0:v0 + 8], ALU.add, ALU.mult)
                ins.then_inc(mod_used, 1)

            dve.wait_ge(vec_in, 16)
            mod_use(0)
            mod_use(1)
            dve.wait_ge(mod_used, 2)
            for k in range(KC):
                dve.wait_ge(xt_x, k + 1)
                V.tensor_scalar(hT[:, k, 0:256], PS[:, 4 + k % 2, 0:256], col(0, 0)[:, k:k + 1], col(0, 1)[:, k:k + 1],
                                ALU.mult, ALU.add).then_inc(h_x, 1)
            dve.wait_ge(lam_exp, 1)
            V.scalar_tensor_tensor(neglam, lam_s[:, 1:2], -LAM_INIT, lam_s[:, 0:1], ALU.add, ALU.subtract).then_inc(lam_done, 1)

            def kq_item(m):
                t = m if m < 4 else m - 4
                turned = m >= 4 or m < 2
                dve.wait_ge(sq_ready, m + 1)
                if m:
                    dve.wait_ge(qn_ready, m)
                link(V.reduce_sum(ssk, sq.rearrange("p (h d) -> p h d", d=HD), AX))
                V.tensor_scalar(msk, ssk, 1.0 / HD, EPS, ALU.mult, ALU.add).then_inc(ms_ready, 1)
                if turned:
                    a = 0 if m >= 4 else 2
                    r4 = raw.rearrange("p (h q s n) -> p h q s n", q=2, s=2, n=16)
                    b4 = rb.rearrange("p (h q s n) -> p h q s n", q=2, s=2, n=16)
                    sn = tab[:, a + 1, t].rearrange("p (q s n) -> p q s n", q=2, s=2)
                    V.tensor_tensor(ra.rearrange("p (h d) -> p h d", d=HD), raw.rearrange("p (h d) -> p h d", d=HD),
                                    tab[:, a, t].unsqueeze(1).broadcast_to([P, 16, HD]), ALU.mult)
                    for s in range(2):
                        ins = V.tensor_tensor(b4[:, :, :, s], r4[:, :, :, 1 - s],
                                              sn[:, :, s].unsqueeze(1).broadcast_to([P, 16, 2, 16]), ALU.mult)
                    link(ins)
                    link(V.tensor_tensor(ra, ra, rb, ALU.add))
                else:
                    link(V.tensor_tensor(ra.rearrange("p (h d) -> p h d", d=HD), raw.rearrange("p (h d) -> p h d", d=HD),
                                         rows[:, R_KG:R_KG + HD].unsqueeze(1).broadcast_to([P, 16, HD]), ALU.mult))
                dve.wait_ge(pow_done, 2 + m + 1)
                if m >= 1:
                    dve.wait_ge(kq_tr, m)
                V.tensor_tensor(qn.rearrange("p (h d) -> p h d", d=HD), ra.rearrange("p (h d) -> p h d", d=HD),
                                msk.unsqueeze(2).broadcast_to([P, 16, HD]), ALU.mult).then_inc(qn_ready, 1)

            for n in range(10):
                if 1 <= n <= 4:
                    mod_use(n + 1)
                if n < 4 or n >= 8:
                    kq_item(n if n < 4 else n - 4)
                if n == 4:
                    dve.wait_ge(qn_ready, 4)
                    V.memset(qT[0][64:128, :, :], 0.0).then_inc(q_zeroed, 1)
                    V.memset(qT[1][0:64, :, :], 0.0).then_inc(q_zeroed, 1)
            dve.wait_ge(lam_done, 1)

            def maxima(u):
                b = u % 2
                dve.wait_ge(scored, u + 1)
                if u >= 2:
                    dve.wait_ge(w_ready, u - 1)
                link(V.reduce_max(ust(b, 0, 2), PS[:, 4 + 2 * b:6 + 2 * b, :], AX))
                V.tensor_scalar(ust(b, 2, 2), ust(b, 0, 2), -SCALE, None, ALU.mult).then_inc(max_ready, 1)

            def mix(u):
                b = u % 2
                dve.wait_ge(exp_done, u + 1)
                link(V.reciprocal(ust(b, 6, 2), ust(b, 4, 2)))
                link(V.tensor_scalar(ust(b, 8), ust(b, 7), neglam, None, ALU.mult))
                if u >= 2:
                    dve.wait_ge(w_tr, u - 1)
                link(V.tensor_scalar(wmix[:, b, :], probs[:, b, 0, :], ust(b, 6), None, ALU.mult))
                V.scalar_tensor_tensor(wmix[:, b, :], probs[:, b, 1, :], ust(b, 8), wmix[:, b, :],
                                       ALU.mult, ALU.add).then_inc(w_ready, 1)

            def squares(g):
                dve.wait_ge(o_ready, 8 * (g + 1))
                V.tensor_scalar(oms[:, 4 * g:4 * g + 4], oss[:, 4 * g:4 * g + 4], 1.0 / P, EPS,
                                ALU.mult, ALU.add).then_inc(ms_ready, 1)

            def normalise(g):
                dve.wait_ge(pow_done, 8 + g + 1)
                o = o_sb[:, 4 * (g % 2):4 * (g % 2) + 4, :]
                V.tensor_tensor(o, o, oms[:, 4 * g:4 * g + 4].unsqueeze(2).broadcast_to([P, 4, P]), ALU.mult).then_inc(on_ready, 1)

            def outputs(g):
                dve.wait_ge(o_tr, g + 1)
                V.tensor_scalar(oT[:, 4 * (g % 2):4 * (g % 2) + 4, P * (g // 2):P * (g // 2) + P],
                                bank((2, 2, 0, 1)[g]).rearrange("p (j n) -> p j n", j=4),
                                vec[:, V_SUB:V_SUB + 1], 1 - LAM_INIT, ALU.mult, ALU.mult).then_inc(oT_ready, 1)

            maxima(0)
            maxima(1)
            mix(0)
            for u in range(16):
                if u < 15:
                    mix(u + 1)
                if u in (4, 8, 12):
                    squares(u // 4 - 1)
                if u < 14:
                    maxima(u + 2)
                if u in (4, 8, 12):
                    normalise(u // 4 - 1)
                if u in (6, 10, 14):
                    outputs((u - 6) // 4)
                if u < 12 and u % 2 == 1:
                    mod_use(6 + u // 2)
            squares(3)
            normalise(3)
            outputs(3)

            def residual(g, first, wait):
                for q in range(4):
                    wait(q)
                    if g or q:
                        dve.wait_ge(x_upd, 4 * g + q)
                    half = slice(512 * (q % 2), 512 * (q % 2) + 512)
                    link(V.tensor_tensor(res_t, bank(first + q), gate_row[g][:, half], ALU.mult))
                    xs = x_sb[:, q // 2, half]
                    V.tensor_tensor(xs, xs, res_t, ALU.add).then_inc(x_upd, 1)

            def norm_part(n, l, what):
                for t in range(NT):
                    dve.wait_ge(ssn_ready, 2 * n + t + 1)
                    dve.wait_ge(x_upd, 4 * n + 2 * t + 2)
                    V.tensor_scalar(msn[:, t:t + 1], ssn[:, t:t + 1], 1.0 / D, EPS, ALU.mult, ALU.add).then_inc(ms_ready, 1)
                    dve.wait_ge(pow_done, 12 + 2 * n + t + 1)
                    V.tensor_scalar(xn[:, t, :], x_sb[:, t, :], msn[:, t:t + 1], None, ALU.mult).then_inc(xn_ready, 1)
                for k in range(0, KC, 2):
                    dve.wait_ge(nt_tr, 8 * n + k + 1)
                    V.tensor_scalar(h2T[:, k, :], PS[:, 4 + k % 4, 0:256], col(l, what)[:, k:k + 1],
                                    col(l, what + 1)[:, k:k + 1], ALU.mult, ALU.add).then_inc(h2_v, 1)

            def across(ap, n=NE):
                return ap.unsqueeze(2).broadcast_to([P, NT, n])

            def row(c, n, m=NT):
                return const[:, c:c + n].unsqueeze(1).broadcast_to([P, m, n])

            def routing(L):
                pr, pm, t, oh1, oh2, srt = (t2(rt(i)) for i in range(6))
                chosen, pd = t2(rt(8)), t2(rt(9))
                sm = rt(10, 64)
                mx, z, tm, v1, v2, v12 = (sm[:, 2 * i:2 * i + 2] for i in range(6))
                gs, gt = sm[:, 16:24].rearrange("p (t g) -> p t g", t=NT), sm[:, 24:32].rearrange("p (t g) -> p t g", t=NT)
                gsel, gm1 = sm[:, 32:40].rearrange("p (t g) -> p t g", t=NT), sm[:, 40:48].rearrange("p (t g) -> p t g", t=NT)
                ov, cum, before = rt(11, 32), rt(11, 64)[:, 32:64], rt(12, 32)
                late, tile_e, cnt = rt(12, 64)[:, 32:64], rt(7, 8), rt(6)[:, 0:32]
                dve.wait_ge(rt_logit, L.l + 1)
                lg = PS[:, 1, 0:64].rearrange("p (t e) -> p t e", t=NT)
                link(V.tensor_tensor(pr, lg, rbias[:, :].unsqueeze(1).broadcast_to([P, NT, NE]), ALU.add))
                link(V.reduce_max(mx, pr, AX))
                V.tensor_tensor(pr, pr, across(mx), ALU.subtract).then_inc(lg_ready, 1)
                dve.wait_ge(lg_exp, L.l + 1)
                link(V.reduce_sum(z, pr, AX))
                link(V.reciprocal(z, z))
                link(V.tensor_tensor(pr, pr, across(z), ALU.mult))
                for tt in range(NT):
                    for g in range(NG):
                        ins = V.max(srt[:, tt, 8 * g:8 * g + 8], pr[:, tt, 8 * g:8 * g + 8])
                link(ins)
                s4 = srt.rearrange("p t (g s) -> p t g s", g=NG)
                link(V.tensor_tensor(gs, s4[:, :, :, 0], s4[:, :, :, 1], ALU.add))
                link(V.reduce_max(mx, gs, AX))
                link(V.tensor_tensor(gt, gs, across(mx, NG), ALU.is_equal))
                link(V.tensor_tensor(gt, gt, row(C_W4, NG), ALU.mult))
                link(V.reduce_max(tm, gt, AX))
                link(V.tensor_tensor(gsel, gt, across(tm, NG), ALU.is_equal))
                link(V.tensor_scalar(gm1, gsel, -1.0, None, ALU.add))

                def g8(ap, tt):
                    return ap[:, tt].unsqueeze(2).broadcast_to([P, NG, PER_G])

                def e4(ap, tt):
                    return ap[:, tt].rearrange("p (g s) -> p g s", g=NG)

                for tt in range(NT):
                    ins = V.tensor_tensor(e4(pm, tt), e4(pr, tt), g8(gsel, tt), ALU.mult)
                link(ins)
                for tt in range(NT):
                    ins = V.tensor_tensor(e4(pm, tt), e4(pm, tt), g8(gm1, tt), ALU.add)
                link(ins)

                def first_largest(v, oh):
                    link(V.reduce_max(v, pm, AX))
                    link(V.tensor_tensor(t, pm, across(v), ALU.is_equal))
                    link(V.tensor_tensor(t, t, row(C_W32, NE), ALU.mult))
                    link(V.reduce_max(tm, t, AX))
                    link(V.tensor_tensor(oh, t, across(tm), ALU.is_equal))

                first_largest(v1, oh1)
                link(V.scalar_tensor_tensor(pm, oh1, -4.0, pm, ALU.mult, ALU.add))
                first_largest(v2, oh2)
                V.tensor_tensor(chosen, oh1, oh2, ALU.add).then_inc(rt_sel, 1)
                link(V.tensor_tensor(v12, v1, v2, ALU.add))
                link(V.reciprocal(v12, v12))
                V.tensor_tensor(gate[:, 0:2], v1, v12, ALU.mult)
                link(V.tensor_tensor(gate[:, 2:4], v2, v12, ALU.mult))
                dve.wait_ge(rt_cnt, L.l + 1)
                link(V.tensor_copy(cnt, PS[:, 2, 64:96]))
                link(V.tensor_scalar(ov, cnt, SLOTS + 0.5, None, ALU.is_ge))
                for n in range(2, SEQ // SLOTS):
                    link(V.scalar_tensor_tensor(ov, cnt, SLOTS * n + 0.5, ov, ALU.is_ge, ALU.add))
                link(V.tensor_tensor_scan(cum, const[:, C_ONES:C_ONES + 32], ov, 0.0, ALU.mult, ALU.add))
                link(V.tensor_tensor(before, cum, ov, ALU.subtract))
                link(V.scalar_tensor_tensor(late, before, float(SLOTS), const[:, C_DELTA:C_DELTA + NE], ALU.mult, ALU.add))
                cmp = rt(0, 7 * 32).rearrange("p (i e) -> p i e", i=OVER)
                ranks = PS[:, 2, 0:64].rearrange("p (t e) -> p t e", t=NT)
                link(V.tensor_scalar(pd, ranks, SLOTS - 0.5, None, ALU.is_ge))
                link(V.tensor_tensor(pd, pd, late.unsqueeze(1).broadcast_to([P, NT, NE]), ALU.mult))
                link(V.tensor_tensor(pd, pd, ranks, ALU.add))
                link(V.tensor_tensor(pd, pd, row(C_BASE, NE), ALU.add))
                for a, oh in ((0, oh1), (1, oh2)):
                    link(V.tensor_tensor(oh, pd, oh, ALU.mult))
                    link(V.reduce_sum(pos[:, 2 * a:2 * a + 2], oh, AX))
                link(V.tensor_tensor(cmp, cum.unsqueeze(1).broadcast_to([P, OVER, NE]),
                                     const[:, C_TILE:C_TILE + OVER].unsqueeze(2).broadcast_to([P, OVER, NE]), ALU.is_le))
                link(V.reduce_sum(tile_e[:, 0:OVER], cmp, AX))
                link(V.tensor_copy(tile_e[:, OVER:OVER + 1], cum[:, NE - 1:NE]))
                link(V.tensor_copy(ov_info[:, :], tile_e[:, 0:8]))
                V.tensor_copy(pcur, pos).then_inc(routed, 1)
                dve.wait_ge(routed, L.l + 1)

            def choose(n, g, parts, whole, binary, before=None):
                if before is not None:
                    dve.wait_ge(*before)
                for a in range(2):
                    for t in range(NT):
                        i = 2 * a + t
                        ins = V.tensor_scalar(part[a][:, t, 0:n], const[:, C_IOTA:C_IOTA + n], pcur[:, i:i + 1],
                                              gate[:, i:i + 1], ALU.is_equal, ALU.mult)
                ins.then_inc(parts[0], 1)
                dve.wait_ge(*parts)
                V.tensor_tensor(g, part[0][:, :, 0:n], part[1][:, :, 0:n], ALU.add).then_inc(whole[0], 1)
                dve.wait_ge(*whole)
                V.tensor_scalar(s01[:, :, 0:n], g, 0.0, None, ALU.is_gt).then_inc(binary, 1)

            def lower_outputs(second):
                return V.tensor_copy(y_sb[64 * second:64 * second + 64, 0:512], PS[0:64, 6, :])

            def experts(L):
                choose(GW, sg[:, :, 0:GW], (L.parts, 1), (L.sg_done, 1), L.s_ready)

                def hidden(n):
                    dve.wait_ge(L.silu_done, n)
                    V.tensor_tensor(h_sb, silu_sb, PS[:, 4, 256:512], ALU.mult).then_inc(L.h_ready, 1)

                hidden(1)

                def step(e, c, it, last=False):
                    if not isinstance(it, int) and c % GRP == 0:
                        g = 2 * it + c // 3 + 1
                        V.tensor_scalar(pcur, pcur, -float(GW), None, ALU.add).then_inc(L.shifted, 1)
                        dve.wait_ge(L.shifted, g)
                        b = (c // 3 + 1) % 2 * GW
                        choose(GW, sg[:, :, b:b + GW], (L.parts, g + 1), (L.sg_done, g + 1), L.s_ready, (L.s_ready, g))
                    dve.wait_ge(L.dn_done, e + 1)
                    lower_outputs(c % 2).then_inc(L.y_v, 1)
                    if not last:
                        hidden(e + 2)

                with dve.Fori(0, TURNS) as it:
                    for c in range(BODY):
                        step(BODY * it + c, c, it)
                step(BODY * TURNS, 0, TURNS)
                step(BODY * TURNS + 1, 1, TURNS, last=True)
                link(V.tensor_scalar(pcur, pos, -float(NE * SLOTS - SLOTS), None, ALU.add))
                link(V.memset(sg[:, :, GW + SLOTS:GW + P], 0.0))
                n_ov = dve.value_load(ov_info[0:1, OVER:OVER + 1], min_val=0, max_val=OVER)
                with dve.Fori(0, OVER) as i:
                    with dve.If(i < n_ov):
                        V.tensor_scalar(pcur, pcur, -float(SLOTS), None, ALU.add).then_inc(L.ov_shift, 1)
                        dve.wait_ge(L.ov_shift, i + 1)
                        choose(SLOTS, sg[:, :, GW:GW + SLOTS], (L.ov_parts, i + 1), (L.ov_sg, i + 1), L.ov_s)
                        dve.wait_ge(L.ov_silu, i + 1)
                        V.tensor_tensor(h_sb, silu_sb, PS[:, 4, 256:512], ALU.mult).then_inc(L.ov_h, 1)
                        dve.wait_ge(L.dn_done, NE + i + 1)
                        lower_outputs(0).then_inc(L.ov_yv, 1)

            residual(0, 4, lambda q: dve.wait_ge(op_done, q + 1))
            norm_part(0, 0, 2)
            V.memset(ccols[:, :], 0.0)
            routing(layers[0])
            experts(layers[0])
            residual(1, 0, lambda q: dve.wait_ge(layers[0].acc_done, 1))
            norm_part(1, 1, 0)

            V.memset(up, 0.0).then_inc(borders, 1)
            dve.wait_ge(invn_in, 16)
            for g, w in enumerate(WINDOWS):
                dve.wait_ge(up_ready, 2 * g + 2)
                cur, reach, a = up, 1, 0
                while reach < w:
                    nxt = pool_sum[a]
                    back, fore = (1, 0) if reach == 1 else (reach // 2, reach // 2)
                    lo, hi = reach, UP - reach + 1
                    link(V.tensor_tensor(nxt[:, :, lo:hi], cur[:, :, lo - back:hi - back], cur[:, :, lo + fore:hi + fore], ALU.add))
                    cur, reach, a = nxt, 2 * reach, 1 - a
                mean = pool_sum[a][:, :, PAD:PAD + SEQ]
                link(V.tensor_tensor(mean, cur[:, :, PAD:PAD + SEQ], inv_n[:, g].unsqueeze(1).broadcast_to([P, 2, SEQ]), ALU.mult))
                V.tensor_tensor(dT[:, 2 * g:2 * g + 2, :], mean, up[:, :, PAD:PAD + SEQ], ALU.subtract).then_inc(d_ready, 1)

            residual(2, 0, lambda q: dve.wait_ge(po_done, q + 1))
            norm_part(2, 1, 2)
            routing(layers[1])
            experts(layers[1])
            residual(3, 0, lambda q: dve.wait_ge(layers[1].acc_done, 1))


_DIRECT = ["x", "ctx", "ada_w", "ada_b", "attn_w_in", "attn_w_out", "pool_w_in", "pool_w_group", "pool_w_out",
           "router_w", "moe_w_gate", "moe_w_up", "moe_w_down"]


def kernel(**inputs):
    import concourse.bacc as bacc
    from concourse.bass_utils import run_bass_kernel_spmd

    a = {n: np.ascontiguousarray(v) for n, v in inputs.items()}

    def columns(v):
        return v.reshape(-1, KC, P).transpose(2, 0, 1).reshape(P, -1)

    ada_cols = a["ada_b"].reshape(2, 6, D)[:, list(COL_PARTS)]
    vec = np.concatenate([columns(a["c"]), columns(a["c_ctx"]), columns(a["norm1_g"]), columns(a["norm2_g"]),
                          columns(a["pool_scale"]), a["attn_sub_gain"].reshape(P, 1), columns(ada_cols)], 1)
    row = np.concatenate([a[n].reshape(-1) for n in ("attn_q_gain", "attn_k_gain", "attn_lq1", "attn_lk1", "attn_lq2",
                                                     "attn_lk2", "router_b")])[None]
    const, rope, inv_n = constants()
    arrays = {n: a[n] for n in _DIRECT}
    arrays |= {"vec": np.ascontiguousarray(vec), "row": np.ascontiguousarray(row), "const": const, "rope": rope, "inv_n": inv_n}
    nc = bacc.Bacc("TRN2", target_bir_lowering=False, num_devices=1)
    args = [nc.dram_tensor(f"in_{n}", v.shape, mybir.dt.from_np(v.dtype), kind="ExternalInput").ap() for n, v in arrays.items()]
    out = nc.dram_tensor("out", (1, SEQ, D), F32, kind="ExternalOutput").ap()
    program(nc, *args, out)
    r = run_bass_kernel_spmd(nc, [{f"in_{n}": v for n, v in arrays.items()}], core_ids=[0])
    return r.results[0]["out"]
```

```python
import math
from contextlib import ExitStack

import numpy as np

import concourse.bass as bass
from concourse import mybir

F32 = mybir.dt.float32
BF16 = mybir.dt.bfloat16
I32 = mybir.dt.int32
ALU = mybir.AluOpType
ACT = mybir.ActivationFunctionType
AX = mybir.AxisListType.X

P = 128
D = 1024
KC = D // P
SEQ = 256
NT = SEQ // P
HEADS, HD = 8, 64
EPS = 1e-6
LAM_INIT = 0.8 - 0.6 * math.exp(-0.3 * 0)
SCALE = HD ** -0.5
NE, NG, PER_G = 32, 4, 8
FF = 512
SLOTS = 64
OVER = (2 * SEQ) // (SLOTS + 1)
GRP = 3
BODY = 2 * GRP
TURNS = NE // BODY
GW = GRP * SLOTS
WINDOWS = (2, 4, 8, 16)
PAD = max(WINDOWS) // 2
UP = SEQ + 2 * PAD

C_ID, C_TRI, C_ONES, C_SEL = 0, 128, 256, 384
C_IOTA = 512
C_STACK = C_IOTA + GW
C_W4 = C_STACK + 32
C_W32 = C_W4 + 4
C_BASE = C_W32 + 32
C_DELTA = C_BASE + 32
C_TILE = C_DELTA + 32
N_CONST = C_TILE + 8
V_C, V_N1, V_N2, V_PS, V_SUB, V_ADA = 0, 16, 32, 48, 56, 57
N_VEC = V_ADA + 64
R_QG, R_KG, R_LQ, R_RB = 0, 64, 128, 384
N_ROW = 416
OUT_SCALE = 1 - LAM_INIT
PE_BLOCKS = (0, 1, 8, 9, 10, 11)
ADA_AT = {0: 8, 2: 9, 6: 10, 8: 11}
UNIT_LOADS = ((0, 2, 9, 11), (1, 3, 8, 10), ("k", 4, 5, 6, 7))
COL_PARTS = (0, 1, 3, 4)


def constants():
    c = np.zeros((P, N_CONST), np.float32)
    r = np.arange(P)
    c[:, C_ID:C_ID + P] = np.eye(P)
    c[:, C_TRI:C_TRI + P] = r[:, None] < r[None, :]
    c[:, C_ONES:C_ONES + P] = 1
    c[::32, C_SEL:C_SEL + P] = 1
    c[:, C_IOTA:C_IOTA + GW] = np.arange(GW)
    c[:, C_STACK:C_STACK + 32] = r[:, None] % 32 == np.arange(32)
    c[:, C_W4:C_W4 + 4] = NG - np.arange(4)
    c[:, C_W32:C_W32 + 32] = NE - np.arange(32)
    c[:, C_BASE:C_BASE + 32] = SLOTS * np.arange(32)
    c[:, C_DELTA:C_DELTA + 32] = NE * SLOTS - SLOTS - SLOTS * np.arange(32)
    c[:, C_TILE:C_TILE + 8] = np.arange(8)
    half = HD // 2
    inv = (10000.0 ** (-np.arange(0, half, 2, dtype=np.float32) / half)).astype(np.float32)
    t = np.arange(SEQ)
    ar = (t // 64).astype(np.float32)[:, None] * inv
    ac = (t % 64).astype(np.float32)[:, None] * inv
    cos = np.cos(np.concatenate([ar, ar, ac, ac], 1))
    sin = np.sin(np.concatenate([-ar, ar, -ac, ac], 1))
    rope = np.stack([cos, sin]).astype(np.float32).reshape(2, NT, P, HD).transpose(2, 0, 1, 3)
    n = np.stack([np.minimum(t + w // 2, SEQ) - np.maximum(t - w // 2, 0) for w in WINDOWS])
    inv_n = (np.float32(1) / n.astype(np.float32)).astype(np.float32)
    return c, np.ascontiguousarray(rope).reshape(P, -1), inv_n.reshape(1, -1)


def program(nc, x_d, ctx_d, ada_w, ada_b, w_in, w_out, pool_in, pool_grp, pool_out, router_w,
            w_gate, w_up, w_down, vec_d, row_d, const_d, rope_d, inv_n_d, out_d):
    stack = ExitStack()
    with stack:
        def sb(name, n, dt=F32):
            return stack.enter_context(nc.sbuf_tensor(name, [P, n], dt))

        def sem(name):
            return stack.enter_context(nc.semaphore(name))

        ring = sb("ring", 36864)
        X = sb("X", 2048)
        HT = sb("HT", 4096)
        KT = sb("KT", 4096)
        QT = sb("QT", 2048)
        TMP = sb("TMP", 2048)
        const = sb("const", N_CONST)
        vec = sb("vec", N_VEC)
        rope_g = sb("rope_g", 4 * 2 * HD)
        ccols = sb("ccols", KC * 32)
        cols = sb("cols", 80)
        stat = sb("stat", 80)
        rbias = sb("rbias", 32)
        ov_info = sb("ov_info", 8, I32)
        PS = stack.enter_context(nc.psum_tensor("PS", [P, 8, 512], F32))

        def bank(i, n=1):
            return PS[:, i, :] if n == 1 else PS[:, i:i + n, :].rearrange("p b n -> p (b n)")

        ident = const[:, C_ID:C_ID + P]
        tri = const[:, C_TRI:C_TRI + P]
        ones = const[:, C_ONES:C_ONES + P]
        sel = const[:, C_SEL:C_SEL + P]
        x_sb = X[:, :].rearrange("p (t d) -> p t d", t=NT)

        def unit(i):
            return ring[:, 8192 * i:8192 * (i + 1)].rearrange("p (k n) -> p k n", k=8)

        vals = ring[:, 24576:28672].rearrange("p (t n) -> p t n", t=4)
        work = 28672
        modraw = ring[:, work:work + 1024]
        acc_of = {5: ring[:, work + 3072:work + 4096], 7: ring[:, work + 5120:work + 6144]}
        raw = ring[:, work + 1024:work + 2048]
        sq = ring[:, work + 2048:work + 3072]
        ra = ring[:, work + 3072:work + 4096]
        rb = ring[:, work + 4096:work + 5120]
        qn = ring[:, work + 5120:work + 6144]
        xn0 = ring[:, work + 5120:work + 7168].rearrange("p (t d) -> p t d", t=NT)
        rope_raw = ring[:, work + 7168:work + 7424].rearrange("p (a t d) -> p a t d", a=2, t=NT)
        rows = ring[:, work + 7424:work + 7424 + N_ROW]
        lam_t = ring[:, work + 7840:work + 7968]
        probs = ring[:, work + 1024:work + 3072].rearrange("p (b m n) -> p b m n", b=2, m=2)
        wmix = ring[:, work + 3072:work + 4096].rearrange("p (b n) -> p b n", b=2)
        wT = ring[:, work + 4096:work + 5120].rearrange("p (b c n) -> p b c n", b=2, c=4)
        o_sb = ring[:, work + 5120:work + 6144].rearrange("p (b n) -> p b n", b=8)

        ctx_sb = TMP[:, :].rearrange("p (t d) -> p t d", t=NT)
        hT = HT[:, :].rearrange("p (k t) -> p k t", k=KC)
        oT = HT[:, 0:2048].rearrange("p (h t) -> p h t", h=HEADS)
        h2T = HT[:, 0:2048].rearrange("p (k t) -> p k t", k=KC)
        gate_row = [TMP[:, 0:1024], TMP[:, 1024:2048], HT[:, 2048:3072], HT[:, 3072:4096]]
        kT = KT[:, :].rearrange("p (h t) -> p h t", h=HEADS)
        qT = [z.rearrange("p (h t) -> p h t", h=HEADS) for z in (QT[:, :], ring[:, work + 6144:work + 8192])]
        xn = KT[:, 0:2048].rearrange("p (t d) -> p t d", t=NT)


        slot = [ring[:, 12288 * i:12288 * (i + 1)] for i in range(3)]
        gu_w = [s[:, 0:8192].rearrange("p (k a f) -> p k a f", k=KC, a=2) for s in slot]
        dn_w = [s[:, 8192:12288].rearrange("p (c n) -> p c n", c=4) for s in slot]
        xsT = [KT[:, 2048:2048 + KC * GW].rearrange("p (k n) -> p k n", k=KC),
               QT[:, 0:KC * GW].rearrange("p (k n) -> p k n", k=KC)]
        silu_sb = KT[:, 3584:3840]
        h_sb = KT[:, 3840:4096]
        res_t = KT[:, 3584:4096]
        rw = QT[:, 1536:1792].rearrange("p (k e) -> p k e", k=KC)
        part_lg = QT[:, 1792:2048]
        sg = HT[:, 0:768].rearrange("p (t n) -> p t n", t=NT)
        s01 = HT[:, 768:1152].rearrange("p (t n) -> p t n", t=NT)
        t_sb = HT[:, 1152:1664]
        part = [rope_g[:, 0:384].rearrange("p (t n) -> p t n", t=NT), HT[:, 1664:2048].rearrange("p (t n) -> p t n", t=NT)]
        y_sb = TMP[:, 0:1024]
        route = sb("route", 16)
        pos, gate, pcur = (route[:, 4 * i:4 * i + 4] for i in range(3))
        nt_tmp = sb("nt_tmp", 32)
        mhalf = sb("mhalf", 16)

        def rt(i, n=64):
            return TMP[:, 64 * i:64 * i + n]

        def t2(ap):
            return ap.rearrange("p (t e) -> p t e", t=NT)

        pool_w = slot[2][:, 0:8192].rearrange("p (k n) -> p k n", k=KC)
        grp_w = slot[2][:, 8192:10240].rearrange("p (g i n) -> p g i n", g=4, i=2)
        pout_w = slot[0][:, 0:8192].rearrange("p (k n) -> p k n", k=KC)
        dT = KT[:, 2048:4096].rearrange("p (b t) -> p b t", b=8)
        y1T = KT[:, 0:2048].rearrange("p (b t) -> p b t", b=8)
        up = QT[:, 0:2 * UP].rearrange("p (i t) -> p i t", i=2)
        pool_sum = [TMP[:, 1024:1024 + 2 * UP].rearrange("p (i t) -> p i t", i=2),
                    QT[:, 2 * UP:4 * UP].rearrange("p (i t) -> p i t", i=2)]
        inv_n = TMP[:, 0:1024].rearrange("p (g t) -> p g t", g=4)

        ss0, ms0 = stat[:, 0:4], stat[:, 4:8]
        ssn, msn = stat[:, 12:14], stat[:, 14:16]
        ssk, msk = stat[:, 18:34], stat[:, 34:50]
        neglam = stat[:, 76:77]
        lam_s = stat[:, 77:79]

        def ust(b, i, n=1):
            return stat[:, 50 + 10 * b + i:50 + 10 * b + i + n]

        def inv_z(u, m, n=1):
            return stat[:, 2 * (u % 4) + m:2 * (u % 4) + m + n]

        oss, oms = stat[:, 18:34], stat[:, 34:50]

        def col(l, what):
            c = 32 * l + 8 * what
            return cols[:, c:c + 8]

        def bias_col(i):
            l, p = divmod(i, 6)
            c = V_ADA + 8 * (4 * l + COL_PARTS.index(p))
            return vec[:, c:c + 8]

        const_in, rows_in, vec_in, x_in, ctx_in = (sem(n) for n in ("const_in", "rows_in", "vec_in", "x_in", "ctx_in"))
        rw_in, bias0_in, bias1_in = sem("rw_in"), sem("bias0_in"), sem("bias1_in")
        unit_in = [[sem(f"unit_in_{u}_{half}") for half in range(2)] for u in range(3)]
        w_in_s = {n: sem(f"w{n}_in") for n in "vqo"}
        chain = sem("chain")
        zeroed, minus_half, silu_c, lam_sum, lam_exp = (sem(n) for n in ("zeroed", "minus_half", "silu_c", "lam_sum", "lam_exp"))
        ss_ready, ms_ready, pow_done, xn0_ready = (sem(n) for n in ("ss_ready", "ms_ready", "pow_done", "xn0_ready"))
        mod_mm, mod_raw, mod_fin, mod_used, ada_acc = (sem(n) for n in ("mod_mm", "mod_raw", "mod_fin", "mod_used", "ada_acc"))
        xt_x, xt_c, h_x, h_c = (sem(n) for n in ("xt_x", "xt_c", "h_x", "h_c"))
        proj_done, proj_used, sq_ready, qn_ready, kq_tr, kq_in = (sem(n) for n in ("proj_done", "proj_used", "sq_ready", "qn_ready", "kq_tr", "kq_in"))
        scored, max_ready, exp_done, w_ready, w_tr, wT_ready, pv_done, o_ready, on_ready, o_tr, oT_ready = (
            sem(n) for n in ("scored", "max_ready", "exp_done", "w_ready", "w_tr", "wT_ready", "pv_done", "o_ready", "on_ready", "o_tr", "oT_ready"))
        op_done, x_upd, ssn_ready, xn_ready, nt_tr, h2_v, h2_a = (sem(n) for n in ("op_done", "x_upd", "ssn_ready", "xn_ready", "nt_tr", "h2_v", "h2_a"))
        rt_part, rt_sb, rt_logit, lg_ready, lg_exp, rt_sel, rt_cnt, routed = (sem(n) for n in ("rt_part", "rt_sb", "rt_logit", "lg_ready", "lg_exp", "rt_sel", "rt_cnt", "routed"))
        pin_in, pout_in, invn_in, u_done, up_ready, d_ready, y1_done, y1_ready, po_done = (
            sem(n) for n in ("pin_in", "pout_in", "invn_in", "u_done", "up_ready", "d_ready", "y1_done", "y1_ready", "po_done"))
        last_in = sem("last_in")
        out_stored, borders, q_zeroed = sem("out_stored"), sem("borders"), sem("q_zeroed")

        class Layer:
            def __init__(self, l):
                self.l = l
                self.gu_in = [sem(f"gu_in{l}_{i}") for i in range(3)]
                self.dn_in = [sem(f"dn_in{l}_{i}") for i in range(3)]
                (self.shifted, self.parts, self.sg_done, self.s_ready, self.xg_done, self.xs_done, self.gu_done,
                 self.silu_done, self.h_ready, self.tr_done, self.t_ready, self.dn_done, self.y_v, self.y_a, self.acc_done) = (
                    sem(f"{n}{l}") for n in ("shifted", "parts", "sg_done", "s_ready", "xg_done", "xs_done", "gu_done",
                                             "silu_done", "h_ready", "tr_done", "t_ready", "dn_done", "y_v", "y_a", "acc_done"))
                (self.ov_in, self.ov_shift, self.ov_parts, self.ov_sg, self.ov_s, self.ov_xg, self.ov_xs, self.ov_gu,
                 self.ov_silu, self.ov_h, self.ov_tr, self.ov_t, self.ov_yv, self.ov_ya) = (
                    sem(f"ov_{n}{l}") for n in ("in", "shift", "parts", "sg", "s", "xg", "xs", "gu", "silu", "h", "tr", "t", "yv", "ya"))

            def slot(self, e):
                return (e + self.l) % 3

        layers = [Layer(0), Layer(1)]
        ov_slot = [L.slot(NE - 1) for L in layers]
        block = stack.enter_context(nc.Block())

        @block.sync
        def _(sp):
            def rows_of(w, c0, n):
                return w.rearrange("(k p) n -> p k n", p=P)[:, :, c0:c0 + n]

            def load_expert(L, e, s, freed=False):
                if freed:
                    sp.wait_ge(L.gu_done, e - 2)
                if isinstance(e, int) and e == NE - 1:
                    for part in range(2):
                        for a, w in enumerate((w_gate, w_up)):
                            sp.dma_start(gu_w[s][:, 4 * part:4 * part + 4, a, :],
                                         w[L.l, e, 512 * part:512 * part + 512].rearrange("(k p) f -> p k f", p=P)
                                         ).then_inc((L.gu_in[s], last_in)[part], 16)
                else:
                    sp.dma_start(gu_w[s][:, :, 0, :], w_gate[L.l, e].rearrange("(k p) f -> p k f", p=P)).then_inc(L.gu_in[s], 16)
                    sp.dma_start(gu_w[s][:, :, 1, :], w_up[L.l, e].rearrange("(k p) f -> p k f", p=P)).then_inc(L.gu_in[s], 16)
                if freed:
                    sp.wait_ge(L.dn_done, e - 2)
                sp.dma_start(dn_w[s], w_down[L.l, e].rearrange("(c p) n -> p c n", p=P)).then_inc(L.dn_in[s], 16)

            sp.dma_start(vec[:, :], vec_d).then_inc(vec_in, 16)
            sp.dma_start(ctx_sb, ctx_d[0].rearrange("(t p) d -> p t d", p=P)).then_inc(ctx_in, 16)
            sp.dma_start(x_sb, x_d[0].rearrange("(t p) d -> p t d", p=P)).then_inc(x_in, 16)

            def load_ada(i, u):
                for half in range(2):
                    sp.dma_start(unit(u)[:, :, 512 * half:512 * half + 512],
                                 rows_of(ada_w[i // 6], D * (i % 6) + 512 * half, 512)).then_inc(unit_in[u][half], 16)

            def load_rows(i, part, u):
                w = ada_w[i // 6, 512 * part:512 * part + 512, D * (i % 6):D * (i % 6) + D]
                sp.dma_start(unit(u)[:, 4 * part:4 * part + 4, :], w.rearrange("(k p) n -> p k n", p=P)).then_inc(unit_in[u][part], 16)

            load_ada(0, 0)
            load_ada(1, 1)
            for half in range(2):
                sp.dma_start(unit(2)[:, :, 512 * half:512 * half + 512],
                             rows_of(w_in[0], D + 512 * half, 512)).then_inc(unit_in[2][half], 16)
            for i in range(2, 4):
                sp.wait_ge(mod_mm, 2 * i - 2)
                for part in range(2):
                    load_rows(i, part, i % 2)
            sp.wait_ge(ada_acc, 2)
            sp.dma_start(unit(0), rows_of(w_in[0], 2 * D, D)).then_inc(w_in_s["v"], 16)
            sp.wait_ge(ada_acc, 4)
            sp.dma_start(unit(1), rows_of(w_in[0], 0, D)).then_inc(w_in_s["q"], 16)
            for i in range(4, 8):
                for part in range(2):
                    if i == 4:
                        sp.wait_ge(proj_done, 4)
                    else:
                        sp.wait_ge(ada_acc, 2 * (i - 3) + part + 1)
                    load_rows(i, part, 2)
                if i == 5:
                    sp.wait_ge(proj_done, 6)
                    load_ada(8, 1)
            sp.wait_ge(ada_acc, 12)
            sp.dma_start(unit(2), rows_of(w_out[0], 0, D)).then_inc(w_in_s["o"], 16)
            sp.wait_ge(proj_done, 10)
            load_ada(9, 0)
            sp.wait_ge(mod_mm, 6)
            load_ada(10, 1)
            sp.wait_ge(mod_mm, 8)
            load_ada(11, 0)
            L = layers[0]
            sp.wait_ge(mod_mm, 12)
            load_expert(L, 0, 0)
            sp.wait_ge(oT_ready, 4)
            sp.wait_ge(mod_used, 12)
            load_expert(L, 2, 2)
            sp.wait_ge(op_done, 4)
            load_expert(L, 1, 1)
            for L in layers:
                with sp.Fori(0, (NE - 5) // 3) as it:
                    for c in range(3):
                        load_expert(L, 3 * it + (3 + c), L.slot(c), freed=True)
                for e in range(3 + 3 * ((NE - 5) // 3), NE):
                    load_expert(L, e, L.slot(e), freed=True)
                if L.l == 0:
                    sp.wait_ge(L.gu_done, 30)
                    sp.wait_ge(L.dn_done, 30)
                    sp.dma_start(pool_w, rows_of(pool_in[0], 0, D)).then_inc(pin_in, 16)
                    sp.dma_start(grp_w, pool_grp[0].rearrange("g (i p) n -> p g i n", p=P)).then_inc(pin_in, 16)
                    sp.wait_ge(L.gu_done, 31)
                    sp.wait_ge(L.dn_done, 31)
                    sp.dma_start(pout_w, rows_of(pool_out[0], 0, D)).then_inc(pout_in, 16)
                sp.wait_ge(L.gu_done, NE)
                sp.wait_ge(L.dn_done, NE)
                sp.wait_ge(routed, L.l + 1)
                n_ov = sp.value_load(ov_info[0:1, OVER:OVER + 1], min_val=0, max_val=OVER)
                with sp.If(n_ov > 0):
                    with sp.Fori(0, OVER) as i:
                        with sp.If(i < n_ov):
                            sp.wait_ge(L.dn_done, NE + i)
                            e = sp.value_load(ov_info[0:1, bass.ds(i, 1)], min_val=0, max_val=NE - 1)
                            s = ov_slot[L.l]
                            sp.dma_start(gu_w[s][:, :, 0, :], w_gate[L.l, bass.ds(e, 1)].rearrange("o (k p) f -> p (o k) f", p=P)).then_inc(L.ov_in, 16)
                            sp.dma_start(gu_w[s][:, :, 1, :], w_up[L.l, bass.ds(e, 1)].rearrange("o (k p) f -> p (o k) f", p=P)).then_inc(L.ov_in, 16)
                            sp.dma_start(dn_w[s], w_down[L.l, bass.ds(e, 1)].rearrange("o (c p) n -> p (o c) n", p=P)).then_inc(L.ov_in, 16)
                if L.l == 0:
                    L1 = layers[1]
                    sp.wait_ge(L.acc_done, 4)
                    load_expert(L1, 0, L1.slot(0))
                    sp.dma_start(TMP[:, 0:1024], inv_n_d[0].partition_broadcast(P)).then_inc(invn_in, 16)
                    sp.wait_ge(y1_done, 8)
                    load_expert(L1, 1, L1.slot(1))
                    sp.wait_ge(po_done, 4)
                    load_expert(L1, 2, L1.slot(2))

        @block.gpsimd
        def _(pool):
            nc.gpsimd.memset(mhalf[:, :], -0.5).then_inc(minus_half, 1)
            pool.wait_ge(minus_half, 1)

            def inverse_root(n, ap):
                pool.wait_ge(ms_ready, n + 1)
                nc.gpsimd.tensor_tensor(ap, ap, mhalf[:, 0:ap.shape[1]], ALU.pow).then_inc(pow_done, 1)

            inverse_root(0, ms0[:, 0:2])
            inverse_root(1, ms0[:, 2:4])
            for n in range(6):
                inverse_root(2 + n, msk)
            for g in range(4):
                inverse_root(8 + g, oms[:, 4 * g:4 * g + 4])
            for n in range(6):
                inverse_root(12 + n, msn[:, n % 2:n % 2 + 1])

        @block.tensor
        def _(pe):
            mm, tr = nc.tensor.matmul, nc.tensor.transpose

            def ada_mm(i, u):
                if i == 0:
                    pe.wait_ge(silu_c, 1)
                else:
                    pe.wait_ge(mod_used, i)
                for half in range(2):
                    pe.wait_ge(unit_in[u][half], 16 * UNIT_LOADS[u].index(i) + 16)
                    for c in range(2):
                        for j in range(4):
                            k = 2 * j + c
                            ins = mm(PS[32 * j:32 * j + 32, half, :], ccols[:, 32 * k:32 * k + 32],
                                     unit(u)[:, k, 512 * half:512 * half + 512], start=c == 0, stop=c == 1)
                    ins.then_inc(mod_mm, 1)

            def ada_fin(i):
                if i in PE_BLOCKS:
                    n = PE_BLOCKS.index(i)
                    for half in range(2):
                        pe.wait_ge(mod_raw, 2 * n + half + 1)
                        if i % 6 in COL_PARTS:
                            for k in range(4 * half, 4 * half + 4):
                                ins = tr(PS[:, half, 128 * (k % 4):128 * (k % 4) + 128], modraw[:, P * k:P * k + P], ident)
                        else:
                            ins = mm(bank(half), sel, modraw[:, 512 * half:512 * half + 512], start=True, stop=True)
                else:
                    pe.wait_ge(ada_acc, 2 * (i - 1))
                    pe.wait_ge(mod_used, i)
                    acc = acc_of.get(i, modraw)
                    if i % 6 in COL_PARTS:
                        for k in range(KC):
                            ins = mm(PS[:, 0, k:k + 1], acc[:, P * k:P * k + P], ones[:, 0:1], start=True, stop=True)
                    else:
                        for half in range(2):
                            ins = mm(bank(half), ones, acc[:, 512 * half:512 * half + 512], start=True, stop=True)
                ins.then_inc(mod_fin, 1)

            pe.wait_ge(const_in, 16)
            for k in range(KC):
                if k == 0:
                    pe.wait_ge(xn0_ready, 2)
                if k >= 2:
                    pe.wait_ge(h_x, k - 1)
                    pe.wait_ge(h_c, k - 1)
                for t in range(NT):
                    ins = tr(PS[:, 4 + k % 2, P * t:P * t + P], xn0[:, t, P * k:P * k + P], ident)
                ins.then_inc(xt_x, 1)
                for t in range(NT):
                    ins = tr(PS[:, 6 + k % 2, P * t:P * t + P], ctx_sb[:, t, P * k:P * k + P], ident)
                ins.then_inc(xt_c, 1)
            for i in range(2):
                ada_mm(i, i)
                ada_fin(i)

            fin_at = {(1, 0): 2, (2, 1): 3, (5, 0): 4, (7, 0): 5, (8, 0): 6, (9, 0): 7}

            def proj(n):
                which, t, u = ("k", n, 2) if n < 4 else ("q", n - 4, 1) if n < 6 else ("v", n - 6, 0)
                if which != "k":
                    pe.wait_ge(w_in_s[which], 16)
                if n >= 2:
                    pe.wait_ge(proj_used, n - 1)
                for half in range(2):
                    if which == "k":
                        pe.wait_ge(unit_in[2][half], 16)
                    for k in range(KC):
                        if n == 0 and half == 0:
                            pe.wait_ge(h_x, KC + k + 1)
                        elif n == 2 and half == 0:
                            pe.wait_ge(h_c, KC + k + 1)
                        ins = mm(bank(4 + 2 * (n % 2) + half), hT[:, k, P * t:P * t + P],
                                 unit(u)[:, k, 512 * half:512 * half + 512], start=k == 0, stop=k == KC - 1)
                    if half == 1:
                        ins.then_inc(proj_done, 1)
                    if (n, half) in fin_at:
                        ada_fin(fin_at[n, half])

            def kq_transpose(m):
                pe.wait_ge(qn_ready, m + 1)
                if m >= 1:
                    pe.wait_ge(kq_in, m)
                for h in range(HEADS):
                    ins = tr(PS[:, 2 + h // 4, P * (h % 4):P * (h % 4) + P], qn[:, P * h:P * h + P], ident)
                ins.then_inc(kq_tr, 1)

            def scores(u):
                qt, h = divmod(u, HEADS)
                if u >= 2:
                    pe.wait_ge(exp_done, u - 1)
                else:
                    pe.wait_ge(proj_used, 9 + u)
                for m in range(2):
                    ins = mm(bank(4 + 2 * (u % 2) + m), qT[m][:, h, P * qt:P * qt + P], kT[:, h, :], start=True, stop=True)
                ins.then_inc(scored, 1)

            def turn_outputs(g):
                pe.wait_ge(on_ready, g + 1)
                if g >= 2:
                    pe.wait_ge(mod_used, 12)
                else:
                    pe.wait_ge(wT_ready, 4 * g + 7)
                for j in range(4):
                    ins = tr(PS[:, (2, 2, 0, 1)[g], P * j:P * j + P], o_sb[:, 4 * (g % 2) + j, :], ident)
                ins.then_inc(o_tr, 1)

            for n in range(10):
                if n == 9:
                    pe.wait_ge(kq_in, 6)
                    scores(0)
                proj(n)
                if 1 <= n <= 6:
                    kq_transpose(n - 1)
            scores(1)
            def values_product(u):
                pe.wait_ge(wT_ready, u + 1)
                if u >= 1:
                    pe.wait_ge(o_ready, 2 * u)
                h = u % HEADS
                for c in range(4):
                    ins = mm(PS[:, 3, 0:128], wT[:, u % 2, c, :], vals[:, c, P * h:P * h + P], start=c == 0, stop=c == 3)
                ins.then_inc(pv_done, 1)

            def project_outputs(q):
                for h in range(HEADS):
                    ins = mm(bank(4 + q), oT[:, h, P * (q // 2):P * (q // 2) + P],
                             unit(2)[:, h, 512 * (q % 2):512 * (q % 2) + 512], start=h == 0, stop=h == HEADS - 1)
                ins.then_inc(op_done, 1)

            for u in range(16):
                if u == 15:
                    pe.wait_ge(w_in_s["o"], 16)
                    pe.wait_ge(exp_done, 15)
                    pe.wait_ge(oT_ready, 2)
                    project_outputs(0)
                if u < 14:
                    scores(u + 2)
                pe.wait_ge(w_ready, u + 1)
                if u >= 1:
                    pe.wait_ge(wT_ready, u)
                if u in (7, 11):
                    pe.wait_ge(oT_ready, u // 4)
                for c in range(4):
                    ins = tr(PS[:, 2, P * c:P * c + P], wmix[:, u % 2, P * c:P * c + P], ident)
                ins.then_inc(w_tr, 1)
                if u >= 1:
                    values_product(u - 1)
                if u in (6, 10, 14):
                    turn_outputs((u - 6) // 4)
                if u in ADA_AT:
                    ada_mm(ADA_AT[u], (1, 0, 1, 0)[ADA_AT[u] - 8])
                if u - 1 in ADA_AT:
                    ada_fin(ADA_AT[u - 1])

            values_product(15)
            for q in range(1, 4):
                if q == 2:
                    pe.wait_ge(exp_done, 16)
                    pe.wait_ge(oT_ready, 4)
                project_outputs(q)
                if q == 1:
                    turn_outputs(3)

            def norm_transpose(n):
                pe.wait_ge(xn_ready, 2 * n + 2)
                for k in range(KC):
                    if k >= 4:
                        pe.wait_ge((h2_v, h2_a)[k % 2], 4 * n + (k - 4) // 2 + 1)
                    for t in range(NT):
                        ins = tr(PS[:, 4 + k % 4, P * t:P * t + P], xn[:, t, P * k:P * k + P], ident)
                    ins.then_inc(nt_tr, 1)
                pe.wait_ge(h2_v, 4 * n + 4)
                pe.wait_ge(h2_a, 4 * n + 4)

            def route_products(L):
                pe.wait_ge(rw_in, 16)
                for c in range(2):
                    for j in range(4):
                        ins = mm(PS[32 * j:32 * j + 32, 0, 0:256], rw[:, 2 * j + c, :], h2T[:, 2 * j + c, :],
                                 start=c == 0, stop=c == 1)
                ins.then_inc(rt_part, 1)
                pe.wait_ge(rt_sb, L.l + 1)
                for t in range(NT):
                    ins = mm(PS[:, 1, 32 * t:32 * t + 32], part_lg[:, P * t:P * t + P],
                             const[:, C_STACK:C_STACK + 32], start=True, stop=True)
                ins.then_inc(rt_logit, 1)
                pe.wait_ge(rt_sel, L.l + 1)
                chosen = t2(rt(8))
                mm(PS[:, 2, 0:32], tri, chosen[:, 0, :], start=True, stop=True)
                mm(PS[:, 2, 32:64], ones, chosen[:, 0, :], start=True, stop=False)
                mm(PS[:, 2, 32:64], tri, chosen[:, 1, :], start=False, stop=True)
                mm(PS[:, 2, 64:96], ones, chosen[:, 0, :], start=True, stop=False)
                mm(PS[:, 2, 64:96], ones, chosen[:, 1, :], start=False, stop=True).then_inc(rt_cnt, 1)

            def accumulate_zero(start, done=None):
                z = ccols[:, :].bitcast(BF16)
                for b in range(4):
                    ins = mm(bank(b), z[:, 0:128], z[:, :], start=start, stop=not start, skip_group_check=True)
                    if done:
                        ins.then_inc(done, 1)

            def gather(k0, n, dst):
                for c in range(2):
                    for t in range(NT):
                        ins = mm(PS[:, dst, GW * c:GW * c + n], xn[:, t, P * (k0 + c):P * (k0 + c) + P], s01[:, t, 0:n],
                                 start=t == 0, stop=t == NT - 1)
                return ins

            def gate_up(s, xs, j, ks):
                for k in ks:
                    for f in range(2):
                        ins = mm(PS[64 * f:64 * f + 64, 4, :], xs[:, k, SLOTS * j:SLOTS * j + SLOTS],
                                 gu_w[s][:, k, :, 256 * f:256 * f + 256], start=k == 0, stop=k == KC - 1)
                return ins

            def transposes(first):
                if first is not None:
                    for t in range(NT):
                        tr(PS[:, 5, P * t:P * t + P], sg[:, t, first:first + P], ident)
                for c in range(2):
                    ins = tr(PS[:, 5, 256 + P * c:256 + P * c + P], h_sb[:, P * c:P * c + P], ident)
                return ins

            def down(s):
                for c in range(4):
                    a, b = divmod(c, 2)
                    lhs = t_sb[:, 256 + P * b + 64 * a:256 + P * b + 64 * a + 64]
                    for f in range(2):
                        ins = mm(PS[64 * f:64 * f + 64, 6, :], lhs, dn_w[s][:, c, 512 * f:512 * f + 512],
                                 start=c == 0, stop=c == 3)
                return ins

            def combine():
                for t in range(NT):
                    for f in range(2):
                        mm(bank(2 * t + f), t_sb[:, P * t:P * t + P], y_sb[:, 512 * f:512 * f + 512], start=False, stop=False,
                           skip_group_check=True)

            def experts(L):
                pe.wait_ge(L.s_ready, 1)
                for r in range(4):
                    if r >= 2:
                        pe.wait_ge(L.xs_done, r - 1)
                    gather(2 * r, GW, 7 - r % 2).then_inc(L.xg_done, 1)
                pe.wait_ge(routed, L.l + 1)
                accumulate_zero(True)
                pe.wait_ge(L.gu_in[L.slot(0)], 32)
                pe.wait_ge(L.xs_done, 4)
                gate_up(L.slot(0), xsT[0], 0, range(KC)).then_inc(L.gu_done, 1)

                def step(e, c, it, last=False):
                    j, n = c % GRP, c + 1
                    pe.wait_ge(L.h_ready, e + 1)
                    transposes(None if c % 2 else SLOTS * c).then_inc(L.tr_done, 1)
                    if not last:
                        pe.wait_ge(L.gu_in[L.slot(n)], (2 * it + n // 3) * 32 + 32)
                        if n % GRP == 0:
                            pe.wait_ge(L.xs_done, (2 * it + n // 3) * 4 + 4)
                        gate_up(L.slot(n), xsT[n // GRP % 2], n % GRP, range(4))
                    pe.wait_ge(L.t_ready, e + 1)
                    pe.wait_ge(L.dn_in[L.slot(c)], (2 * it + c // 3) * 16 + 16)
                    if c % 2:
                        pe.wait_ge(L.y_v, e)
                        pe.wait_ge(L.y_a, e)
                    down(L.slot(c)).then_inc(L.dn_done, 1)
                    more = not last and c < BODY and j < 2 and not isinstance(it, int)
                    if more:
                        if j == 0:
                            pe.wait_ge(L.s_ready, 2 * it + c // 3 + 2)
                        pe.wait_ge(L.xs_done, (2 * it + c // 3) * 4 + 4 + 2 * j)
                        gather(4 * j, GW, 7).then_inc(L.xg_done, 1)
                    if not last:
                        if isinstance(e, int) and e == NE - 2:
                            pe.wait_ge(last_in, 32 * L.l + 32)
                        gate_up(L.slot(n), xsT[n // GRP % 2], n % GRP, range(4, KC)).then_inc(L.gu_done, 1)
                    if c % 2:
                        pe.wait_ge(L.y_v, e + 1)
                        pe.wait_ge(L.y_a, e + 1)
                        combine()
                    if more:
                        pe.wait_ge(L.xs_done, (2 * it + c // 3) * 4 + 5 + 2 * j)
                        gather(4 * j + 2, GW, 7).then_inc(L.xg_done, 1)

                with pe.Fori(0, TURNS) as it:
                    for c in range(BODY):
                        step(BODY * it + c, c, it)
                step(BODY * TURNS, 0, TURNS)
                step(BODY * TURNS + 1, 1, TURNS, last=True)

                n_ov = pe.value_load(ov_info[0:1, OVER:OVER + 1], min_val=0, max_val=OVER)
                s = ov_slot[L.l]
                with pe.If(n_ov > 0):
                    with pe.Fori(0, OVER) as i:
                        with pe.If(i < n_ov):
                            pe.wait_ge(L.ov_s, i + 1)
                            for r in range(4):
                                if r:
                                    pe.wait_ge(L.ov_xs, 4 * i + r)
                                gather(2 * r, SLOTS, 7).then_inc(L.ov_xg, 1)
                            pe.wait_ge(L.ov_xs, 4 * i + 4)
                            pe.wait_ge(L.ov_in, 48 * i + 48)
                            gate_up(s, xsT[1], 0, range(KC)).then_inc(L.ov_gu, 1)
                            pe.wait_ge(L.ov_h, i + 1)
                            transposes(GW).then_inc(L.ov_tr, 1)
                            pe.wait_ge(L.ov_t, i + 1)
                            down(s).then_inc(L.dn_done, 1)
                            pe.wait_ge(L.ov_yv, i + 1)
                            pe.wait_ge(L.ov_ya, i + 1)
                            combine()
                accumulate_zero(False, L.acc_done)

            norm_transpose(0)
            route_products(layers[0])
            experts(layers[0])

            norm_transpose(1)
            pe.wait_ge(pin_in, 32)
            for b in range(8):
                if b >= 4:
                    pe.wait_ge(up_ready, b - 3)
                for k in range(KC):
                    ins = mm(PS[:, 4 + b % 4, 0:256], pool_w[:, k, P * b:P * b + P], h2T[:, k, :],
                             start=k == 0, stop=k == KC - 1)
                ins.then_inc(u_done, 1)
            for q in range(8):
                g, ob = divmod(q, 2)
                pe.wait_ge(d_ready, g + 1)
                if q < 4:
                    pe.wait_ge(up_ready, q + 5)
                else:
                    pe.wait_ge(y1_ready, q - 3)
                for i in range(2):
                    ins = mm(PS[:, 4 + q % 4, 0:256], grp_w[:, g, i, P * ob:P * ob + P], dT[:, 2 * g + i, :],
                             start=i == 0, stop=i == 1)
                ins.then_inc(y1_done, 1)
            pe.wait_ge(y1_ready, 8)
            pe.wait_ge(pout_in, 16)
            for q in range(4):
                for k in range(KC):
                    ins = mm(bank(q), y1T[:, k, P * (q // 2):P * (q // 2) + P],
                             pout_w[:, k, 512 * (q % 2):512 * (q % 2) + 512], start=k == 0, stop=k == KC - 1)
                ins.then_inc(po_done, 1)

            norm_transpose(2)
            route_products(layers[1])
            experts(layers[1])

        @block.scalar
        def _(act):
            A = nc.scalar.activation
            act.dma_start(const[:, :], const_d).then_inc(const_in, 16)
            act.dma_start(rows, row_d[0].partition_broadcast(P)).then_inc(rows_in, 16)
            act.dma_start(rope_raw, rope_d.rearrange("p (a t d) -> p a t d", a=2, t=NT)).then_inc(rows_in, 16)
            act.wait_ge(vec_in, 16)
            act.wait_ge(zeroed, 1)
            A(ccols[:, :].rearrange("p (k m) -> p m k", m=32)[:, 0:2, :],
              vec[:, V_C:V_C + 16].rearrange("p (m k) -> p m k", m=2), ACT.Silu).then_inc(silu_c, 1)
            act.wait_ge(ctx_in, 16)
            for t in range(NT):
                if t:
                    act.wait_ge(ss_ready, t)
                A(sq, ctx_sb[:, t, :], ACT.Square, accum_out=ss0[:, t:t + 1]).then_inc(ss_ready, 1)
            act.wait_ge(x_in, 16)
            for t in range(NT):
                act.wait_ge(ss_ready, 2 + t)
                A(sq, x_sb[:, t, :], ACT.Square, accum_out=ss0[:, 2 + t:3 + t]).then_inc(ss_ready, 1)

            def mod_copy(i):
                n = PE_BLOCKS.index(i)
                if i >= 1:
                    act.wait_ge(mod_fin, i)
                for half in range(2):
                    act.wait_ge(mod_mm, 2 * n + half + 1)
                    nc.scalar.copy(modraw[:, 512 * half:512 * half + 512], bank(half)).then_inc(mod_raw, 1)

            for k in range(KC):
                act.wait_ge(xt_c, k + 1)
                nc.scalar.copy(hT[:, k, 256:512], PS[:, 6 + k % 2, 0:256]).then_inc(h_c, 1)
            mod_copy(0)
            mod_copy(1)
            act.wait_ge(mod_used, 2)
            act.wait_ge(h_c, KC)
            for k in range(KC):
                A(hT[:, k, 256:512], hT[:, k, 256:512], ACT.Identity, bias=col(2, 1)[:, k:k + 1],
                  scale=col(2, 0)[:, k:k + 1]).then_inc(h_c, 1)
            act.wait_ge(lam_sum, 1)
            A(lam_s, lam_s, ACT.Exp).then_inc(lam_exp, 1)
            for g, p in ((0, 2), (1, 5)):
                act.dma_start(gate_row[g], ada_b[0, D * p:D * (p + 1)].partition_broadcast(P)).then_inc(bias0_in, 16)

            def kq_copy(m):
                act.wait_ge(kq_tr, m + 1)
                src = bank(2, 2).rearrange("p (h t) -> p h t", h=HEADS)
                if m < 4:
                    ins = nc.scalar.copy(kT[:, :, P * m:P * m + P], src)
                else:
                    act.wait_ge(q_zeroed, 2)
                    for a in range(2):
                        r = slice(64 * a, 64 * a + 64)
                        ins = nc.scalar.copy(qT[a][r, :, P * (m - 4):P * (m - 4) + P], src[r])
                ins.then_inc(kq_in, 1)

            def exponentials(u):
                b = u % 2
                act.wait_ge(max_ready, u + 1)
                if u >= 2:
                    act.wait_ge(w_ready, u - 1)
                for m in range(2):
                    ins = A(probs[:, b, m, :], bank(4 + 2 * b + m), ACT.Exp, bias=ust(b, 2 + m),
                            scale=SCALE, accum_out=ust(b, 4 + m))
                ins.then_inc(exp_done, 1)

            def outputs(g):
                act.wait_ge(o_tr, g + 1)
                A(oT[:, 4 * (g % 2):4 * (g % 2) + 4, P * (g // 2):P * (g // 2) + P],
                  bank((2, 2, 0, 1)[g]).rearrange("p (j n) -> p j n", j=4), ACT.Identity,
                  scale=vec[:, V_SUB:V_SUB + 1]).then_inc(oT_ready, 1)

            for n in range(10):
                if n == 9:
                    exponentials(0)
                act.wait_ge(proj_done, n + 1)
                src = bank(4 + 2 * (n % 2), 2)
                if n >= 6:
                    nc.scalar.copy(vals[:, n - 6, :], src).then_inc(proj_used, 1)
                else:
                    if n >= 1:
                        act.wait_ge(qn_ready, n)
                    nc.scalar.copy(raw, src).then_inc(proj_used, 1)
                    act.wait_ge(proj_used, n + 1)
                    nc.scalar.square(sq, raw).then_inc(sq_ready, 1)
                if 1 <= n <= 6:
                    kq_copy(n - 1)
            for g, p in ((2, 2), (3, 5)):
                act.dma_start(gate_row[g], ada_b[1, D * p:D * (p + 1)].partition_broadcast(P)).then_inc(bias1_in, 16)
            exponentials(1)
            def output_copy(u):
                act.wait_ge(pv_done, u + 1)
                if u >= 8 and u % 4 == 0:
                    act.wait_ge(o_tr, u // 4 - 1)
                A(o_sb[:, u % 8, :], PS[:, 3, 0:128], ACT.Identity, scale=inv_z(u, 0)).then_inc(o_ready, 1)
                if u >= 1:
                    act.wait_ge(o_ready, 2 * u)
                A(PS[:, 3, 128:256], PS[:, 3, 0:128], ACT.Square, scale=inv_z(u, 0),
                  accum_out=oss[:, u:u + 1]).then_inc(o_ready, 1)

            for u in range(16):
                act.wait_ge(w_tr, u + 1)
                if u >= 2:
                    act.wait_ge(pv_done, u - 1)
                nc.scalar.copy(wT[:, u % 2].rearrange("p c n -> p (c n)"), bank(2)).then_inc(wT_ready, 1)
                if u - 1 in ADA_AT:
                    mod_copy(ADA_AT[u - 1])
                if u < 14:
                    exponentials(u + 2)
                if u >= 1:
                    output_copy(u - 1)
                if u in (6, 10, 14):
                    outputs((u - 6) // 4)
            output_copy(15)
            outputs(3)
            act.wait_ge(scored, 16)
            act.dma_start(rw, router_w.rearrange("(k p) e -> p k e", p=P)).then_inc(rw_in, 16)
            act.wait_ge(oT_ready, 4)
            act.wait_ge(mod_used, 12)

            def norm_part(n, l, what):
                for t in range(NT):
                    act.wait_ge(x_upd, 4 * n + 2 * t + 2)
                    if n or t:
                        act.wait_ge(ssn_ready, 2 * n + t)
                    A(bank(0, 2), x_sb[:, t, :], ACT.Square, accum_out=ssn[:, t:t + 1]).then_inc(ssn_ready, 1)
                for k in range(1, KC, 2):
                    act.wait_ge(nt_tr, 8 * n + k + 1)
                    A(h2T[:, k, :], PS[:, 4 + k % 4, 0:256], ACT.Identity, bias=col(l, what + 1)[:, k:k + 1],
                      scale=col(l, what)[:, k:k + 1]).then_inc(h2_a, 1)

            def route_part(L):
                act.wait_ge(rt_part, L.l + 1)
                nc.scalar.copy(part_lg, PS[:, 0, 0:256]).then_inc(rt_sb, 1)
                act.wait_ge(lg_ready, L.l + 1)
                A(rt(0), rt(0), ACT.Exp).then_inc(lg_exp, 1)

            def spread(L, xs, k0, n, src):
                for c in range(2):
                    k = k0 + c
                    ins = A(xs[:, k, 0:n], PS[:, src, GW * c:GW * c + n], ACT.Identity,
                            bias=col(L.l, 3)[:, k:k + 1], scale=col(L.l, 2)[:, k:k + 1])
                return ins

            def upper_outputs(second):
                return nc.scalar.copy(y_sb[64 * second:64 * second + 64, 512:1024], PS[64:128, 6, :])

            def experts(L):
                for r in range(4):
                    act.wait_ge(L.xg_done, r + 1)
                    spread(L, xsT[0], 2 * r, GW, 7 - r % 2).then_inc(L.xs_done, 1)
                act.wait_ge(L.gu_done, 1)
                A(silu_sb, PS[:, 4, 0:256], ACT.Silu).then_inc(L.silu_done, 1)

                def step(e, c, it, last=False):
                    j = c % GRP
                    act.wait_ge(L.tr_done, e + 1)
                    a = 256 * (c % 2)
                    nc.scalar.copy(t_sb[:, a:512], PS[:, 5, a:512]).then_inc(L.t_ready, 1)
                    act.wait_ge(L.dn_done, e + 1)
                    upper_outputs(c % 2).then_inc(L.y_a, 1)
                    more = not isinstance(it, int) and j < 2
                    if more:
                        act.wait_ge(L.xg_done, (2 * it + c // 3) * 4 + 5 + 2 * j)
                        spread(L, xsT[(c // 3 + 1) % 2], 4 * j, GW, 7).then_inc(L.xs_done, 1)
                    if not last:
                        act.wait_ge(L.gu_done, e + 2)
                        act.wait_ge(L.h_ready, e + 1)
                        A(silu_sb, PS[:, 4, 0:256], ACT.Silu).then_inc(L.silu_done, 1)
                    if more:
                        act.wait_ge(L.xg_done, (2 * it + c // 3) * 4 + 6 + 2 * j)
                        spread(L, xsT[(c // 3 + 1) % 2], 4 * j + 2, GW, 7).then_inc(L.xs_done, 1)

                with act.Fori(0, TURNS) as it:
                    for c in range(BODY):
                        step(BODY * it + c, c, it)
                step(BODY * TURNS, 0, TURNS)
                step(BODY * TURNS + 1, 1, TURNS, last=True)
                act.wait_ge(routed, L.l + 1)
                n_ov = act.value_load(ov_info[0:1, OVER:OVER + 1], min_val=0, max_val=OVER)
                with act.If(n_ov > 0):
                    with act.Fori(0, OVER) as i:
                        with act.If(i < n_ov):
                            for r in range(4):
                                act.wait_ge(L.ov_xg, 4 * i + r + 1)
                                spread(L, xsT[1], 2 * r, SLOTS, 7).then_inc(L.ov_xs, 1)
                            act.wait_ge(L.ov_gu, i + 1)
                            A(silu_sb, PS[:, 4, 0:256], ACT.Silu).then_inc(L.ov_silu, 1)
                            act.wait_ge(L.ov_tr, i + 1)
                            nc.scalar.copy(t_sb, bank(5)).then_inc(L.ov_t, 1)
                            act.wait_ge(L.dn_done, NE + i + 1)
                            upper_outputs(0).then_inc(L.ov_ya, 1)

            norm_part(0, 0, 2)
            route_part(layers[0])
            experts(layers[0])
            norm_part(1, 1, 0)
            for b in range(8):
                act.wait_ge(u_done, b + 1)
                if b < 2:
                    act.wait_ge(borders, 1)
                else:
                    act.wait_ge(d_ready, b // 2)
                nc.scalar.copy(up[:, b % 2, PAD:PAD + SEQ], PS[:, 4 + b % 4, 0:256]).then_inc(up_ready, 1)
            for q in range(8):
                act.wait_ge(y1_done, q + 1)
                A(y1T[:, q, :], PS[:, 4 + q % 4, 0:256], ACT.Identity, scale=vec[:, V_PS + q:V_PS + q + 1]).then_inc(y1_ready, 1)
            norm_part(2, 1, 2)
            route_part(layers[1])
            experts(layers[1])
            for q in range(4):
                t, half = q // 2, slice(512 * (q % 2), 512 * (q % 2) + 512)
                act.wait_ge(x_upd, 12 + q + 1)
                act.dma_start(out_d[0, P * t:P * t + P, half], x_sb[:, t, half]).then_inc(out_stored, 16)
            act.wait_ge(out_stored, 64)

        @block.vector
        def _(dve):
            V = nc.vector
            linked = [0]

            def link(ins):
                linked[0] += 1
                ins.then_inc(chain, 1)
                dve.wait_ge(chain, linked[0])

            V.memset(ccols[:, :], 0.0).then_inc(zeroed, 1)

            for a, src, dst in ((0, ctx_sb, ctx_sb), (1, x_sb, xn0)):
                dve.wait_ge(ss_ready, 2 * a + 2)
                V.tensor_scalar(ms0[:, 2 * a:2 * a + 2], ss0[:, 2 * a:2 * a + 2], 1.0 / D, EPS, ALU.mult, ALU.add).then_inc(ms_ready, 1)
                dve.wait_ge(pow_done, a + 1)
                for t in range(NT):
                    ins = V.tensor_scalar(dst[:, t, :], src[:, t, :], ms0[:, 2 * a + t:2 * a + t + 1], None, ALU.mult)
                ins.then_inc(xn0_ready, 1)

            dve.wait_ge(rows_in, 32)
            tab = rope_g[:, :].rearrange("p (a t d) -> p a t d", a=4, t=NT)
            for a, r in ((0, R_QG), (2, R_KG)):
                g = rows[:, r:r + HD]
                V.tensor_tensor(tab[:, a], rope_raw[:, 0], g.unsqueeze(1).broadcast_to([P, NT, HD]), ALU.mult)
                gh = g.rearrange("p (q h n) -> p q h n", q=2, h=2)
                for t in range(NT):
                    to = tab[:, a + 1, t].rearrange("p (q h n) -> p q h n", q=2, h=2)
                    of = rope_raw[:, 1, t].rearrange("p (q h n) -> p q h n", q=2, h=2)
                    for h in range(2):
                        V.tensor_tensor(to[:, :, h], of[:, :, h], gh[:, :, 1 - h], ALU.mult)
            V.tensor_copy(rbias[:, :], rows[:, R_RB:R_RB + NE])
            lq = rows[:, R_LQ:R_LQ + 256].rearrange("p (a b n) -> p a b n", a=2, b=2)
            lt = lam_t.rearrange("p (a n) -> p a n", a=2)
            link(V.tensor_tensor(lt, lq[:, :, 0], lq[:, :, 1], ALU.mult))
            V.reduce_sum(lam_s, lt, AX).then_inc(lam_sum, 1)

            def mod_use(i):
                l, p = divmod(i, 6)
                dve.wait_ge(mod_fin, i + 1)
                if i:
                    dve.wait_ge(mod_used, i)
                if p not in COL_PARTS:
                    dve.wait_ge((bias0_in, bias1_in)[l], 32)
                    g = gate_row[2 * l + (p == 5)]
                    V.tensor_tensor(g, bank(0, 2), g, ALU.add).then_inc(mod_used, 1)
                    return
                parts = bank(0, 2).rearrange("p (k j m) -> p k j m", k=KC, j=4)
                who = 2 if i < 2 else 1
                if i in PE_BLOCKS:
                    for m in range(who):
                        ins = V.reduce_sum(nt_tmp[:, 8 * m:8 * m + 8], parts[:, :, :, m], AX)
                    link(ins)
                q = COL_PARTS.index(p)
                for m in range(who):
                    to = col(2 if m else l, (1, 0, 3, 2)[q])
                    s = nt_tmp[:, 8 * m:8 * m + 8] if i in PE_BLOCKS else PS[:, 0, 0:8]
                    if q % 2 == 0:
                        ins = V.tensor_tensor(to, s, bias_col(i), ALU.add)
                    else:
                        ins = V.tensor_tensor(nt_tmp[:, 16 + 8 * m:24 + 8 * m], s, bias_col(i), ALU.add)
                if q % 2:
                    link(ins)
                    v0 = (V_N1 if q == 1 else V_N2) + 8 * l
                    for m in range(who):
                        to = col(2 if m else l, (1, 0, 3, 2)[q])
                        ins = V.scalar_tensor_tensor(to, nt_tmp[:, 16 + 8 * m:24 + 8 * m], 1.0, vec[:, v0:v0 + 8], ALU.add, ALU.mult)
                ins.then_inc(mod_used, 1)

            def accumulate(i, u):
                acc = acc_of.get(i, modraw)
                if i == 7:
                    dve.wait_ge(kq_tr, 6)
                elif i >= 3:
                    dve.wait_ge(mod_fin, i if acc_of.get(i - 1, modraw) is acc else i - 1)
                for k in range(KC):
                    if k % 4 == 0:
                        dve.wait_ge(unit_in[u][k // 4], 16 * UNIT_LOADS[u].index(i) + 16)
                    if k == 0:
                        ins = V.tensor_scalar(acc, unit(u)[:, k, :], ccols[:, 0:1], None, ALU.mult)
                    else:
                        ins = V.scalar_tensor_tensor(acc, unit(u)[:, k, :], ccols[:, 32 * k:32 * k + 1], acc, ALU.mult, ALU.add)
                    if k % 4 == 3:
                        ins.then_inc(ada_acc, 1)
                        if k == 3:
                            dve.wait_ge(ada_acc, 2 * i - 3)
                    else:
                        link(ins)

            for k in range(KC):
                dve.wait_ge(xt_x, k + 1)
                V.tensor_copy(hT[:, k, 0:256], PS[:, 4 + k % 2, 0:256]).then_inc(h_x, 1)
            dve.wait_ge(vec_in, 16)
            mod_use(0)
            mod_use(1)
            dve.wait_ge(mod_used, 2)
            dve.wait_ge(h_x, KC)
            for k in range(KC):
                V.tensor_scalar(hT[:, k, 0:256], hT[:, k, 0:256], col(0, 0)[:, k:k + 1], col(0, 1)[:, k:k + 1],
                                ALU.mult, ALU.add).then_inc(h_x, 1)
            dve.wait_ge(lam_exp, 1)
            link(V.scalar_tensor_tensor(neglam, lam_s[:, 1:2], -LAM_INIT, lam_s[:, 0:1], ALU.add, ALU.subtract))

            def kq_item(m):
                t = m if m < 4 else m - 4
                turned = m >= 4 or m < 2
                dve.wait_ge(sq_ready, m + 1)
                if m:
                    dve.wait_ge(qn_ready, m)
                link(V.reduce_sum(ssk, sq.rearrange("p (h d) -> p h d", d=HD), AX))
                V.tensor_scalar(msk, ssk, 1.0 / HD, EPS, ALU.mult, ALU.add).then_inc(ms_ready, 1)
                if turned:
                    a = 0 if m >= 4 else 2
                    r4 = raw.rearrange("p (h q s n) -> p h q s n", q=2, s=2, n=16)
                    b4 = rb.rearrange("p (h q s n) -> p h q s n", q=2, s=2, n=16)
                    sn = tab[:, a + 1, t].rearrange("p (q s n) -> p q s n", q=2, s=2)
                    V.tensor_tensor(ra.rearrange("p (h d) -> p h d", d=HD), raw.rearrange("p (h d) -> p h d", d=HD),
                                    tab[:, a, t].unsqueeze(1).broadcast_to([P, 16, HD]), ALU.mult)
                    for s in range(2):
                        ins = V.tensor_tensor(b4[:, :, :, s], r4[:, :, :, 1 - s],
                                              sn[:, :, s].unsqueeze(1).broadcast_to([P, 16, 2, 16]), ALU.mult)
                    link(ins)
                    link(V.tensor_tensor(ra, ra, rb, ALU.add))
                else:
                    link(V.tensor_tensor(ra.rearrange("p (h d) -> p h d", d=HD), raw.rearrange("p (h d) -> p h d", d=HD),
                                         rows[:, R_KG:R_KG + HD].unsqueeze(1).broadcast_to([P, 16, HD]), ALU.mult))
                dve.wait_ge(pow_done, 2 + m + 1)
                if m >= 1:
                    dve.wait_ge(kq_tr, m)
                V.tensor_tensor(qn.rearrange("p (h d) -> p h d", d=HD), ra.rearrange("p (h d) -> p h d", d=HD),
                                msk.unsqueeze(2).broadcast_to([P, 16, HD]), ALU.mult).then_inc(qn_ready, 1)

            accumulate(2, 0)
            kq_item(0)
            accumulate(3, 1)
            kq_item(1)
            mod_use(2)
            kq_item(2)
            mod_use(3)
            kq_item(3)
            dve.wait_ge(qn_ready, 4)
            V.memset(qT[0][64:128, :, :], 0.0).then_inc(q_zeroed, 1)
            V.memset(qT[1][0:64, :, :], 0.0).then_inc(q_zeroed, 1)
            accumulate(4, 2)
            kq_item(4)
            kq_item(5)
            mod_use(4)
            for i in range(5, 8):
                accumulate(i, 2)
                if i >= 6:
                    mod_use(i - 1)

            def maxima(u):
                b = u % 2
                dve.wait_ge(scored, u + 1)
                if u >= 2:
                    dve.wait_ge(w_ready, u - 1)
                link(V.reduce_max(ust(b, 0, 2), PS[:, 4 + 2 * b:6 + 2 * b, :], AX))
                V.tensor_scalar(ust(b, 2, 2), ust(b, 0, 2), -SCALE, None, ALU.mult).then_inc(max_ready, 1)

            def mix(u):
                b = u % 2
                dve.wait_ge(exp_done, u + 1)
                if u >= 4:
                    dve.wait_ge(o_ready, 2 * (u - 3))
                link(V.reciprocal(inv_z(u, 0, 2), ust(b, 4, 2)))
                link(V.tensor_scalar(ust(b, 8), inv_z(u, 1), ust(b, 4), neglam, ALU.mult, ALU.mult))
                if u >= 2:
                    dve.wait_ge(w_tr, u - 1)
                V.scalar_tensor_tensor(wmix[:, b, :], probs[:, b, 1, :], ust(b, 8), probs[:, b, 0, :],
                                       ALU.mult, ALU.add).then_inc(w_ready, 1)

            def squares(g):
                dve.wait_ge(o_ready, 8 * (g + 1))
                V.tensor_scalar(oms[:, 4 * g:4 * g + 4], oss[:, 4 * g:4 * g + 4], OUT_SCALE ** -2 / P, EPS * OUT_SCALE ** -2,
                                ALU.mult, ALU.add).then_inc(ms_ready, 1)

            def normalise(g):
                dve.wait_ge(pow_done, 8 + g + 1)
                o = o_sb[:, 4 * (g % 2):4 * (g % 2) + 4, :]
                V.tensor_tensor(o, o, oms[:, 4 * g:4 * g + 4].unsqueeze(2).broadcast_to([P, 4, P]), ALU.mult).then_inc(on_ready, 1)

            maxima(0)
            mix(0)
            mod_use(7)
            maxima(1)
            for u in range(16):
                if u in (5, 9, 13):
                    squares(u // 4 - 1)
                if u < 14:
                    maxima(u + 2)
                if u < 15:
                    mix(u + 1)
                if u in (5, 9, 13):
                    normalise(u // 4 - 1)
                if u - 1 in ADA_AT:
                    mod_use(ADA_AT[u - 1])
            squares(3)
            normalise(3)

            def residual(g, first, wait):
                for q in range(4):
                    wait(q)
                    if g or q:
                        dve.wait_ge(x_upd, 4 * g + q)
                    half = slice(512 * (q % 2), 512 * (q % 2) + 512)
                    link(V.tensor_tensor(res_t, bank(first + q), gate_row[g][:, half], ALU.mult))
                    xs = x_sb[:, q // 2, half]
                    V.tensor_tensor(xs, xs, res_t, ALU.add).then_inc(x_upd, 1)

            def norm_part(n, l, what):
                for t in range(NT):
                    dve.wait_ge(ssn_ready, 2 * n + t + 1)
                    dve.wait_ge(x_upd, 4 * n + 2 * t + 2)
                    V.tensor_scalar(msn[:, t:t + 1], ssn[:, t:t + 1], 1.0 / D, EPS, ALU.mult, ALU.add).then_inc(ms_ready, 1)
                    dve.wait_ge(pow_done, 12 + 2 * n + t + 1)
                    V.tensor_scalar(xn[:, t, :], x_sb[:, t, :], msn[:, t:t + 1], None, ALU.mult).then_inc(xn_ready, 1)
                for k in range(0, KC, 2):
                    dve.wait_ge(nt_tr, 8 * n + k + 1)
                    V.tensor_scalar(h2T[:, k, :], PS[:, 4 + k % 4, 0:256], col(l, what)[:, k:k + 1],
                                    col(l, what + 1)[:, k:k + 1], ALU.mult, ALU.add).then_inc(h2_v, 1)

            def across(ap, n=NE):
                return ap.unsqueeze(2).broadcast_to([P, NT, n])

            def row(c, n, m=NT):
                return const[:, c:c + n].unsqueeze(1).broadcast_to([P, m, n])

            def routing(L):
                pr, pm, t, oh1, oh2, srt = (t2(rt(i)) for i in range(6))
                chosen, pd = t2(rt(8)), t2(rt(9))
                sm = rt(10, 64)
                mx, z, tm, v1, v2, v12 = (sm[:, 2 * i:2 * i + 2] for i in range(6))
                gs, gt = sm[:, 16:24].rearrange("p (t g) -> p t g", t=NT), sm[:, 24:32].rearrange("p (t g) -> p t g", t=NT)
                gsel, gm1 = sm[:, 32:40].rearrange("p (t g) -> p t g", t=NT), sm[:, 40:48].rearrange("p (t g) -> p t g", t=NT)
                ov, cum, before = rt(11, 32), rt(11, 64)[:, 32:64], rt(12, 32)
                late, tile_e, cnt = rt(12, 64)[:, 32:64], rt(7, 8), rt(6)[:, 0:32]
                dve.wait_ge(rt_logit, L.l + 1)
                lg = PS[:, 1, 0:64].rearrange("p (t e) -> p t e", t=NT)
                link(V.tensor_tensor(pr, lg, rbias[:, :].unsqueeze(1).broadcast_to([P, NT, NE]), ALU.add))
                link(V.reduce_max(mx, pr, AX))
                V.tensor_tensor(pr, pr, across(mx), ALU.subtract).then_inc(lg_ready, 1)
                dve.wait_ge(lg_exp, L.l + 1)
                link(V.reduce_sum(z, pr, AX))
                link(V.reciprocal(z, z))
                link(V.tensor_tensor(pr, pr, across(z), ALU.mult))
                for tt in range(NT):
                    for g in range(NG):
                        ins = V.max(srt[:, tt, 8 * g:8 * g + 8], pr[:, tt, 8 * g:8 * g + 8])
                link(ins)
                s4 = srt.rearrange("p t (g s) -> p t g s", g=NG)
                link(V.tensor_tensor(gs, s4[:, :, :, 0], s4[:, :, :, 1], ALU.add))
                link(V.reduce_max(mx, gs, AX))
                link(V.tensor_tensor(gt, gs, across(mx, NG), ALU.is_equal))
                link(V.tensor_tensor(gt, gt, row(C_W4, NG), ALU.mult))
                link(V.reduce_max(tm, gt, AX))
                link(V.tensor_tensor(gsel, gt, across(tm, NG), ALU.is_equal))
                link(V.tensor_scalar(gm1, gsel, -1.0, None, ALU.add))

                def g8(ap, tt):
                    return ap[:, tt].unsqueeze(2).broadcast_to([P, NG, PER_G])

                def e4(ap, tt):
                    return ap[:, tt].rearrange("p (g s) -> p g s", g=NG)

                for tt in range(NT):
                    ins = V.tensor_tensor(e4(pm, tt), e4(pr, tt), g8(gsel, tt), ALU.mult)
                link(ins)
                for tt in range(NT):
                    ins = V.tensor_tensor(e4(pm, tt), e4(pm, tt), g8(gm1, tt), ALU.add)
                link(ins)

                def first_largest(v, oh):
                    link(V.reduce_max(v, pm, AX))
                    link(V.tensor_tensor(t, pm, across(v), ALU.is_equal))
                    link(V.tensor_tensor(t, t, row(C_W32, NE), ALU.mult))
                    link(V.reduce_max(tm, t, AX))
                    link(V.tensor_tensor(oh, t, across(tm), ALU.is_equal))

                first_largest(v1, oh1)
                link(V.scalar_tensor_tensor(pm, oh1, -4.0, pm, ALU.mult, ALU.add))
                first_largest(v2, oh2)
                V.tensor_tensor(chosen, oh1, oh2, ALU.add).then_inc(rt_sel, 1)
                link(V.tensor_tensor(v12, v1, v2, ALU.add))
                link(V.reciprocal(v12, v12))
                V.tensor_tensor(gate[:, 0:2], v1, v12, ALU.mult)
                link(V.tensor_tensor(gate[:, 2:4], v2, v12, ALU.mult))
                dve.wait_ge(rt_cnt, L.l + 1)
                ranks = PS[:, 2, 0:64].rearrange("p (t e) -> p t e", t=NT)
                V.tensor_tensor(t, ranks, row(C_BASE, NE), ALU.add)
                V.tensor_scalar(pd, ranks, SLOTS - 0.5, None, ALU.is_ge)
                link(V.tensor_copy(cnt, PS[:, 2, 64:96]))
                link(V.tensor_scalar(ov, cnt, SLOTS + 0.5, None, ALU.is_ge))
                for n in range(2, SEQ // SLOTS):
                    link(V.scalar_tensor_tensor(ov, cnt, SLOTS * n + 0.5, ov, ALU.is_ge, ALU.add))
                link(V.tensor_tensor_scan(cum, const[:, C_ONES:C_ONES + 32], ov, 0.0, ALU.mult, ALU.add))
                link(V.tensor_tensor(before, cum, ov, ALU.subtract))
                link(V.scalar_tensor_tensor(late, before, float(SLOTS), const[:, C_DELTA:C_DELTA + NE], ALU.mult, ALU.add))
                link(V.tensor_tensor(pd, pd, late.unsqueeze(1).broadcast_to([P, NT, NE]), ALU.mult))
                link(V.tensor_tensor(pd, pd, t, ALU.add))
                for oh in (oh1, oh2):
                    ins = V.tensor_tensor(oh, pd, oh, ALU.mult)
                link(ins)
                link(V.reduce_sum(pos, rt(3, 128).rearrange("p (a e) -> p a e", e=NE), AX))
                link(V.tensor_copy(pcur, pos))

            def overflow_tiles(L):
                cum, tile_e = rt(11, 64)[:, 32:64], rt(7, 8)
                cmp = rt(0, 7 * 32).rearrange("p (i e) -> p i e", i=OVER)
                link(V.tensor_tensor(cmp, cum.unsqueeze(1).broadcast_to([P, OVER, NE]),
                                     const[:, C_TILE:C_TILE + OVER].unsqueeze(2).broadcast_to([P, OVER, NE]), ALU.is_le))
                link(V.reduce_sum(tile_e[:, 0:OVER], cmp, AX))
                link(V.tensor_copy(tile_e[:, OVER:OVER + 1], cum[:, NE - 1:NE]))
                V.tensor_copy(ov_info[:, :], tile_e[:, 0:8]).then_inc(routed, 1)
                dve.wait_ge(routed, L.l + 1)

            def choose(n, g, parts, whole, binary, before=None):
                if before is not None:
                    dve.wait_ge(*before)
                for a in range(2):
                    for t in range(NT):
                        i = 2 * a + t
                        ins = V.tensor_scalar(part[a][:, t, 0:n], const[:, C_IOTA:C_IOTA + n], pcur[:, i:i + 1],
                                              gate[:, i:i + 1], ALU.is_equal, ALU.mult)
                ins.then_inc(parts[0], 1)
                dve.wait_ge(*parts)
                V.tensor_tensor(g, part[0][:, :, 0:n], part[1][:, :, 0:n], ALU.add).then_inc(whole[0], 1)
                dve.wait_ge(*whole)
                V.tensor_scalar(s01[:, :, 0:n], g, 0.0, None, ALU.is_gt).then_inc(binary, 1)

            def lower_outputs(second):
                return V.tensor_copy(y_sb[64 * second:64 * second + 64, 0:512], PS[0:64, 6, :])

            def experts(L):
                choose(GW, sg[:, :, 0:GW], (L.parts, 1), (L.sg_done, 1), L.s_ready)
                overflow_tiles(L)

                def hidden(n):
                    dve.wait_ge(L.silu_done, n)
                    V.tensor_tensor(h_sb, silu_sb, PS[:, 4, 256:512], ALU.mult).then_inc(L.h_ready, 1)

                hidden(1)

                def step(e, c, it, last=False):
                    if not isinstance(it, int) and c % GRP == 0:
                        g = 2 * it + c // 3 + 1
                        V.tensor_scalar(pcur, pcur, -float(GW), None, ALU.add).then_inc(L.shifted, 1)
                        dve.wait_ge(L.shifted, g)
                        b = (c // 3 + 1) % 2 * GW
                        choose(GW, sg[:, :, b:b + GW], (L.parts, g + 1), (L.sg_done, g + 1), L.s_ready, (L.s_ready, g))
                    dve.wait_ge(L.dn_done, e + 1)
                    lower_outputs(c % 2).then_inc(L.y_v, 1)
                    if not last:
                        hidden(e + 2)

                with dve.Fori(0, TURNS) as it:
                    for c in range(BODY):
                        step(BODY * it + c, c, it)
                step(BODY * TURNS, 0, TURNS)
                step(BODY * TURNS + 1, 1, TURNS, last=True)
                link(V.tensor_scalar(pcur, pos, -float(NE * SLOTS - SLOTS), None, ALU.add))
                link(V.memset(sg[:, :, GW + SLOTS:GW + P], 0.0))
                n_ov = dve.value_load(ov_info[0:1, OVER:OVER + 1], min_val=0, max_val=OVER)
                with dve.If(n_ov > 0):
                    with dve.Fori(0, OVER) as i:
                        with dve.If(i < n_ov):
                            V.tensor_scalar(pcur, pcur, -float(SLOTS), None, ALU.add).then_inc(L.ov_shift, 1)
                            dve.wait_ge(L.ov_shift, i + 1)
                            choose(SLOTS, sg[:, :, GW:GW + SLOTS], (L.ov_parts, i + 1), (L.ov_sg, i + 1), L.ov_s)
                            dve.wait_ge(L.ov_silu, i + 1)
                            V.tensor_tensor(h_sb, silu_sb, PS[:, 4, 256:512], ALU.mult).then_inc(L.ov_h, 1)
                            dve.wait_ge(L.dn_done, NE + i + 1)
                            lower_outputs(0).then_inc(L.ov_yv, 1)

            residual(0, 4, lambda q: dve.wait_ge(op_done, q + 1))
            norm_part(0, 0, 2)
            V.memset(ccols[:, :], 0.0)
            routing(layers[0])
            experts(layers[0])
            residual(1, 0, lambda q: dve.wait_ge(layers[0].acc_done, q + 1))
            norm_part(1, 1, 0)

            V.memset(up, 0.0).then_inc(borders, 1)
            dve.wait_ge(invn_in, 16)
            for g, w in enumerate(WINDOWS):
                dve.wait_ge(up_ready, 2 * g + 2)
                cur, reach, a = up, 1, 0
                while reach < w:
                    nxt = pool_sum[a]
                    back, fore = (1, 0) if reach == 1 else (reach // 2, reach // 2)
                    lo, hi = reach, UP - reach + 1
                    link(V.tensor_tensor(nxt[:, :, lo:hi], cur[:, :, lo - back:hi - back], cur[:, :, lo + fore:hi + fore], ALU.add))
                    cur, reach, a = nxt, 2 * reach, 1 - a
                mean = pool_sum[a][:, :, PAD:PAD + SEQ]
                link(V.tensor_tensor(mean, cur[:, :, PAD:PAD + SEQ], inv_n[:, g].unsqueeze(1).broadcast_to([P, 2, SEQ]), ALU.mult))
                V.tensor_tensor(dT[:, 2 * g:2 * g + 2, :], mean, up[:, :, PAD:PAD + SEQ], ALU.subtract).then_inc(d_ready, 1)

            residual(2, 0, lambda q: dve.wait_ge(po_done, q + 1))
            norm_part(2, 1, 2)
            routing(layers[1])
            experts(layers[1])
            residual(3, 0, lambda q: dve.wait_ge(layers[1].acc_done, q + 1))


_DIRECT = ["x", "ctx", "ada_w", "ada_b", "attn_w_in", "attn_w_out", "pool_w_in", "pool_w_group", "pool_w_out",
           "router_w", "moe_w_gate", "moe_w_up", "moe_w_down"]


def kernel(**inputs):
    import concourse.bacc as bacc
    from concourse.bass_utils import run_bass_kernel_spmd

    a = {n: np.ascontiguousarray(v) for n, v in inputs.items()}

    def columns(v):
        return v.reshape(-1, KC, P).transpose(2, 0, 1).reshape(P, -1)

    ada_cols = a["ada_b"].reshape(2, 6, D)[:, list(COL_PARTS)]
    vec = np.concatenate([columns(a["c"]), columns(a["c_ctx"]), columns(a["norm1_g"]), columns(a["norm2_g"]),
                          columns(a["pool_scale"]), a["attn_sub_gain"].reshape(P, 1), columns(ada_cols)], 1)
    row = np.concatenate([a[n].reshape(-1) for n in ("attn_q_gain", "attn_k_gain", "attn_lq1", "attn_lk1", "attn_lq2",
                                                     "attn_lk2", "router_b")])[None]
    const, rope, inv_n = constants()
    arrays = {n: a[n] for n in _DIRECT}
    arrays |= {"vec": np.ascontiguousarray(vec), "row": np.ascontiguousarray(row), "const": const, "rope": rope, "inv_n": inv_n}
    nc = bacc.Bacc("TRN2", target_bir_lowering=False, num_devices=1)
    args = [nc.dram_tensor(f"in_{n}", v.shape, mybir.dt.from_np(v.dtype), kind="ExternalInput").ap() for n, v in arrays.items()]
    out = nc.dram_tensor("out", (1, SEQ, D), F32, kind="ExternalOutput").ap()
    program(nc, *args, out)
    r = run_bass_kernel_spmd(nc, [{f"in_{n}": v for n, v in arrays.items()}], core_ids=[0])
    return r.results[0]["out"]
```
